# Optimizing a Trainium2 kernel written in Bass

```python
import math
import jax, jax.numpy as jnp
from jax import lax
import numpy as np

D_MODEL = 1024
BATCH = 1
SEQ = 512
DEPTH = 2

CHUNK = 64
N_A_LAYERS = DEPTH // 2
N_B_LAYERS = DEPTH - N_A_LAYERS

RWKV_HEAD = 64
RWKV_HEADS = D_MODEL // RWKV_HEAD
DECAY_LORA = 64
A_LORA = 64
GATE_LORA = 160
LNX_EPS = 64e-5

DA_HEAD_DIM = 64
DA_HEADS = D_MODEL // (2 * DA_HEAD_DIM)
DA_V_DIM = 2 * DA_HEAD_DIM
ROPE_DIM = DA_HEAD_DIM // 4
ROPE_THETA = 500000.0
Q_BLOCK = 128
SUBLN_EPS = 1e-5

D_FF = ((8 * D_MODEL + 3 * 256 - 1) // (3 * 256)) * 256

NORM_EPS = 1e-6


def rms_norm(x, g, eps=NORM_EPS):
    xf = x.astype(jnp.float32)
    y = xf * lax.rsqrt(jnp.mean(xf * xf, axis=-1, keepdims=True) + eps)
    return (y * g.astype(jnp.float32)).astype(x.dtype)

def swiglu_ffn(h, w_gu, w_down):
    gate, up = jnp.split(h @ w_gu, 2, axis=-1)
    return (jax.nn.silu(gate) * up) @ w_down

def partial_rope(x, pos):
    half = ROPE_DIM // 2
    inv = jnp.power(ROPE_THETA, -jnp.arange(0, ROPE_DIM, 2, dtype=jnp.float32) / ROPE_DIM)
    ang = pos[:, None] * inv[None, :]
    cos = jnp.cos(ang)[None, :, None, :]
    sin = jnp.sin(ang)[None, :, None, :]
    xf = x.astype(jnp.float32)
    x1 = xf[..., :half]
    x2 = xf[..., half:ROPE_DIM]
    out = jnp.concatenate([x1 * cos - x2 * sin, x2 * cos + x1 * sin, xf[..., ROPE_DIM:]], axis=-1)
    return out.astype(x.dtype)

def rwkv7_time_mix(h, mu, w_r, w_k, w_v, w_o, w0, w1, w2, a0, a1, a2, g1, g2,
                   k_k, k_a, r_k, lnx_w, lnx_b):
    B, S, D = h.shape
    H, N = RWKV_HEADS, RWKV_HEAD
    h_prev = jnp.pad(h, ((0, 0), (1, 0), (0, 0)))[:, :-1]
    hh = h_prev - h
    xr = h + hh * mu[0]
    xw = h + hh * mu[1]
    xk = h + hh * mu[2]
    xv = h + hh * mu[3]
    xa = h + hh * mu[4]
    xg = h + hh * mu[5]

    r = xr @ w_r
    w = -jax.nn.softplus(-(w0 + jnp.tanh(xw @ w1) @ w2)) - 0.5
    k = xk @ w_k
    v = xv @ w_v
    a = jax.nn.sigmoid(a0 + (xa @ a1) @ a2)
    g = jax.nn.sigmoid(xg @ g1) @ g2

    kk = (k * k_k).astype(jnp.float32).reshape(B, S, H, N)
    kk = kk / jnp.maximum(jnp.sqrt(jnp.sum(kk * kk, axis=-1, keepdims=True)), 1e-12)
    k = k * (1.0 + (a - 1.0) * k_a)

    def heads(t):
        return t.astype(jnp.float32).reshape(B, S, H, N)

    r_h, k_h, v_h, a_h = heads(r), heads(k), heads(v), heads(a)
    decay = jnp.exp(-jnp.exp(heads(w)))
    a_vec = -kk
    b_vec = kk * a_h

    def time_major(t):
        return t.transpose(1, 0, 2, 3)

    def step(state, inp):
        r_t, w_t, k_t, v_t, a_t, b_t = inp
        sa = jnp.einsum('bhvk,bhk->bhv', state, a_t)
        state = (state * w_t[:, :, None, :]
                 + sa[..., None] * b_t[:, :, None, :]
                 + v_t[..., None] * k_t[:, :, None, :])
        y_t = jnp.einsum('bhvk,bhk->bhv', state, r_t)
        return state, y_t

    state0 = jnp.zeros((B, H, N, N), jnp.float32)
    _, y = lax.scan(step, state0, (time_major(r_h), time_major(decay), time_major(k_h),
                                   time_major(v_h), time_major(a_vec), time_major(b_vec)))
    y = y.transpose(1, 0, 2, 3)

    mean = jnp.mean(y, axis=-1, keepdims=True)
    var = jnp.mean(jnp.square(y - mean), axis=-1, keepdims=True)
    y = ((y - mean) * lax.rsqrt(var + LNX_EPS)).reshape(B, S, D)
    y = y * lnx_w.astype(jnp.float32) + lnx_b.astype(jnp.float32)
    bonus = jnp.sum(r_h * k_h * r_k.astype(jnp.float32), axis=-1, keepdims=True) * v_h
    y = y + bonus.reshape(B, S, D)
    return (y * g.astype(jnp.float32)).astype(h.dtype) @ w_o

def shared_kv(x, kv_g, kv_w, k_norm_g, pos):
    B, S, _ = x.shape
    hkv = rms_norm(x, kv_g)
    k, v = jnp.split(hkv @ kv_w, 2, axis=-1)
    k = k.reshape(B, S, 2 * DA_HEADS, DA_HEAD_DIM)
    k = partial_rope(rms_norm(k, k_norm_g), pos)
    v = v.reshape(B, S, DA_HEADS, DA_V_DIM)
    return k, v

def diff_attention(h, k, v, pos, w_q, q_norm_g, lam_q1, lam_k1, lam_q2, lam_k2,
                   subln_g, w_o, lam_init):
    B, S, D = h.shape
    H = DA_HEADS
    q = (h @ w_q).reshape(B, S, 2 * H, DA_HEAD_DIM)
    q = partial_rope(rms_norm(q, q_norm_g), pos)
    f32 = jnp.float32
    lam = (jnp.exp(jnp.sum(lam_q1.astype(f32) * lam_k1.astype(f32)))
           - jnp.exp(jnp.sum(lam_q2.astype(f32) * lam_k2.astype(f32))) + lam_init)
    scale = DA_HEAD_DIM ** -0.5
    k_chunk = jnp.arange(S) // CHUNK
    n_blocks = S // Q_BLOCK

    def block(i):
        start = i * Q_BLOCK
        q_blk = lax.dynamic_slice_in_dim(q, start, Q_BLOCK, axis=1)
        s = jnp.einsum('bqhd,bkhd->bhqk', q_blk, k).astype(f32) * scale
        q_chunk = (start + jnp.arange(Q_BLOCK)) // CHUNK
        allowed = k_chunk[None, :] <= q_chunk[:, None]
        s = jnp.where(allowed[None, None], s, -jnp.inf)
        p = jax.nn.softmax(s, axis=-1).reshape(B, H, 2, Q_BLOCK, S)
        p = p[:, :, 0] - lam * p[:, :, 1]
        return jnp.einsum('bhqk,bkhe->bqhe', p.astype(v.dtype), v)

    o = lax.map(block, jnp.arange(n_blocks))
    o = o.transpose(1, 0, 2, 3, 4).reshape(B, S, H, DA_V_DIM)
    o = rms_norm(o, subln_g, eps=SUBLN_EPS) * (1.0 - lam_init)
    return o.reshape(B, S, D) @ w_o

def first_inputs(seed: int = 0) -> dict:
    key = jax.random.key(seed)
    ks = iter(jax.random.split(key, 48))
    D, F, NA, NB = D_MODEL, D_FF, N_A_LAYERS, N_B_LAYERS
    nrm = lambda shape, s: jax.random.normal(next(ks), shape, jnp.float32) * s
    gain = lambda shape: 1.0 + 0.02 * jax.random.normal(next(ks), shape, jnp.float32)
    inp = {}
    inp["x"] = nrm((BATCH, SEQ, D), 1.0)
    inp["g_mix"] = gain((DEPTH, D))
    inp["g_ffn"] = gain((DEPTH, D))
    inp["rw_mu"] = jax.random.uniform(next(ks), (NA, 6, D), jnp.float32)
    inp["rw_w_r"] = nrm((NA, D, D), D ** -0.5)
    inp["rw_w_k"] = nrm((NA, D, D), D ** -0.5)
    inp["rw_w_v"] = nrm((NA, D, D), D ** -0.5)
    inp["rw_w_o"] = nrm((NA, D, D), D ** -0.5)
    inp["rw_w0"] = jax.random.uniform(next(ks), (NA, D), jnp.float32, -6.0, -1.0)
    inp["rw_w1"] = nrm((NA, D, DECAY_LORA), D ** -0.5)
    inp["rw_w2"] = nrm((NA, DECAY_LORA, D), 0.5 * DECAY_LORA ** -0.5)
    inp["rw_a0"] = nrm((NA, D), 0.1)
    inp["rw_a1"] = nrm((NA, D, A_LORA), D ** -0.5)
    inp["rw_a2"] = nrm((NA, A_LORA, D), A_LORA ** -0.5)
    inp["rw_g1"] = nrm((NA, D, GATE_LORA), D ** -0.5)
    inp["rw_g2"] = nrm((NA, GATE_LORA, D), GATE_LORA ** -0.5)
    inp["rw_k_k"] = 0.85 + nrm((NA, D), 0.05)
    inp["rw_k_a"] = 1.0 + nrm((NA, D), 0.05)
    inp["rw_r_k"] = nrm((NA, RWKV_HEADS, RWKV_HEAD), 0.1)
    inp["rw_lnx_w"] = gain((NA, D))
    inp["rw_lnx_b"] = nrm((NA, D), 0.02)
    inp["kv_g"] = gain((D,))
    inp["kv_w"] = nrm((D, 2 * D), D ** -0.5)
    inp["k_norm_g"] = gain((DA_HEAD_DIM,))
    inp["da_w_q"] = nrm((NB, D, D), D ** -0.5)
    inp["da_q_norm_g"] = gain((NB, DA_HEAD_DIM))
    inp["da_lam_q1"] = nrm((NB, DA_HEAD_DIM), 0.1)
    inp["da_lam_k1"] = nrm((NB, DA_HEAD_DIM), 0.1)
    inp["da_lam_q2"] = nrm((NB, DA_HEAD_DIM), 0.1)
    inp["da_lam_k2"] = nrm((NB, DA_HEAD_DIM), 0.1)
    inp["da_subln_g"] = gain((NB, DA_V_DIM))
    inp["da_w_o"] = nrm((NB, D, D), D ** -0.5)
    inp["ffn_w_gu"] = nrm((DEPTH, D, 2 * F), D ** -0.5)
    inp["ffn_w_down"] = nrm((DEPTH, F, D), F ** -0.5)
    return inp

def first_block(x, g_mix, g_ffn, rw_mu, rw_w_r, rw_w_k, rw_w_v, rw_w_o, rw_w0, rw_w1, rw_w2,
              rw_a0, rw_a1, rw_a2, rw_g1, rw_g2, rw_k_k, rw_k_a, rw_r_k, rw_lnx_w, rw_lnx_b,
              kv_g, kv_w, k_norm_g, da_w_q, da_q_norm_g, da_lam_q1, da_lam_k1, da_lam_q2,
              da_lam_k2, da_subln_g, da_w_o, ffn_w_gu, ffn_w_down):
    S = x.shape[1]
    pos = jnp.arange(S, dtype=jnp.float32)
    k_sh, v_sh = None, None
    for layer in range(DEPTH):
        if layer < N_A_LAYERS:
            i = layer
            h = rms_norm(x, g_mix[layer])
            x = x + rwkv7_time_mix(h, rw_mu[i], rw_w_r[i], rw_w_k[i], rw_w_v[i], rw_w_o[i],
                                   rw_w0[i], rw_w1[i], rw_w2[i], rw_a0[i], rw_a1[i], rw_a2[i],
                                   rw_g1[i], rw_g2[i], rw_k_k[i], rw_k_a[i], rw_r_k[i],
                                   rw_lnx_w[i], rw_lnx_b[i])
        else:
            j = layer - N_A_LAYERS
            if j == 0:
                k_sh, v_sh = shared_kv(x, kv_g, kv_w, k_norm_g, pos)
            lam_init = 0.8 - 0.6 * math.exp(-0.3 * layer)
            h = rms_norm(x, g_mix[layer])
            x = x + diff_attention(h, k_sh, v_sh, pos, da_w_q[j], da_q_norm_g[j],
                                   da_lam_q1[j], da_lam_k1[j], da_lam_q2[j], da_lam_k2[j],
                                   da_subln_g[j], da_w_o[j], lam_init)
        h = rms_norm(x, g_ffn[layer])
        x = x + swiglu_ffn(h, ffn_w_gu[layer], ffn_w_down[layer])
    return x


MIX_WIDTH = D_MODEL
BRANCH = MIX_WIDTH // 2
GLA_HEADS = 4
GLA_DK = BRANCH // 2 // GLA_HEADS
GLA_DV = BRANCH // GLA_HEADS
GLA_RANK = 16
GLA_TAU = 16.0
GLA_CHUNK = 64
SGU_GROUPS = 4
SGU_CHUNK = 128
SGU_CH = BRANCH // SGU_GROUPS
RET_HEADS = 4
RET_DK = BRANCH // 2 // RET_HEADS
RET_DV = BRANCH // RET_HEADS
RET_CHUNK = 128
ROPE_BASE = 10000.0
POOL_WINDOWS = (2, 4, 8, 16)
POOL_CH = BRANCH // len(POOL_WINDOWS)
DN_ALPHA = (2 * DEPTH) ** 0.25
DN_BETA = (8 * DEPTH) ** -0.25
LN_EPS = 1e-5

EVEN_SIZES = (GLA_HEADS * GLA_DK, GLA_HEADS * GLA_DK, BRANCH, BRANCH, GLA_RANK,
              BRANCH, BRANCH, BRANCH)
ODD_SIZES = (RET_HEADS * RET_DK, RET_HEADS * RET_DK, BRANCH, BRANCH,
             BRANCH, BRANCH)


def _split(h, sizes):
    idx = [int(i) for i in np.cumsum(sizes)[:-1]]
    return jnp.split(h, idx, axis=-1)

def _layer_norm(x, g, b):
    xf = x.astype(jnp.float32)
    mu = jnp.mean(xf, axis=-1, keepdims=True)
    var = jnp.mean(jnp.square(xf - mu), axis=-1, keepdims=True)
    return ((xf - mu) * lax.rsqrt(var + LN_EPS) * g + b).astype(x.dtype)

def _head_rmsnorm(o, g):
    of = o.astype(jnp.float32)
    return of * lax.rsqrt(jnp.mean(jnp.square(of), axis=-1, keepdims=True) + LN_EPS) * g

def _head_groupnorm(o, g):
    of = o.astype(jnp.float32)
    mu = jnp.mean(of, axis=-1, keepdims=True)
    var = jnp.mean(jnp.square(of - mu), axis=-1, keepdims=True)
    return (of - mu) * lax.rsqrt(var + LN_EPS) * g

def _chunk_scan(decay, chunk_state):
    def step(s_prev, inp):
        dec, cs = inp
        return dec * s_prev + cs, s_prev
    init = jnp.zeros(chunk_state.shape[1:], jnp.float32)
    _, s_in = lax.scan(step, init, (decay, chunk_state))
    return s_in

def _gla(q, k, v, log_a):
    B, S, H, dk = q.shape
    dv = v.shape[-1]
    C = GLA_CHUNK
    n = S // C
    f32 = jnp.float32
    q = q.astype(f32).reshape(B, n, C, H, dk) * (dk ** -0.5)
    k = k.astype(f32).reshape(B, n, C, H, dk)
    v = v.astype(f32).reshape(B, n, C, H, dv)
    b = jnp.cumsum(log_a.astype(f32).reshape(B, n, C, H, dk), axis=2)
    q_dec = q * jnp.exp(b)
    k_dec = k * jnp.exp(-b)
    causal = jnp.tril(jnp.ones((C, C), dtype=bool))
    scores = jnp.einsum('bnihd,bnjhd->bnhij', q_dec, k_dec)
    scores = jnp.where(causal, scores, 0.0)
    o_intra = jnp.einsum('bnhij,bnjhe->bnihe', scores, v)
    b_last = b[:, :, -1]
    k_state = k * jnp.exp(b_last[:, :, None] - b)
    chunk_state = jnp.einsum('bnjhd,bnjhe->bnhde', k_state, v)
    decay = jnp.exp(b_last)[..., None]
    s_in = _chunk_scan(jnp.moveaxis(decay, 1, 0), jnp.moveaxis(chunk_state, 1, 0))
    s_in = jnp.moveaxis(s_in, 0, 1)
    o_inter = jnp.einsum('bnihd,bnhde->bnihe', q_dec, s_in)
    return (o_intra + o_inter).reshape(B, S, H, dv)

def _spatial_gating(u, sv, ln_g, ln_b, w_s, b_s):
    B, S, _ = u.shape
    n = S // SGU_CHUNK
    svr = sv.reshape(B, n, SGU_CHUNK, SGU_GROUPS, SGU_CH)
    svr = _layer_norm(svr, ln_g, ln_b)
    w = jnp.where(jnp.tril(jnp.ones((SGU_CHUNK, SGU_CHUNK), dtype=bool)), w_s, 0.0)
    s = jnp.einsum('gts,bnsgc->bntgc', w, svr) + jnp.transpose(b_s)[None, None, :, :, None]
    return u * s.reshape(B, S, BRANCH).astype(u.dtype)

def _rotary(x, positions):
    half = x.shape[-1] // 2
    inv = ROPE_BASE ** (-jnp.arange(half, dtype=jnp.float32) / half)
    ang = positions.astype(jnp.float32)[..., None] * inv
    cos = jnp.cos(ang)[:, :, None, :]
    sin = jnp.sin(ang)[:, :, None, :]
    xf = x.astype(jnp.float32)
    x1, x2 = xf[..., :half], xf[..., half:]
    return jnp.concatenate([x1 * cos - x2 * sin, x1 * sin + x2 * cos], axis=-1)

def _retention(q, k, v):
    B, S, H, dk = q.shape
    dv = v.shape[-1]
    C = RET_CHUNK
    n = S // C
    f32 = jnp.float32
    log_gamma = jnp.log(1.0 - 2.0 ** (-5.0 - jnp.arange(H, dtype=f32)))
    q = q.astype(f32).reshape(B, n, C, H, dk) * (dk ** -0.5)
    k = k.astype(f32).reshape(B, n, C, H, dk)
    v = v.astype(f32).reshape(B, n, C, H, dv)
    idx = jnp.arange(C, dtype=f32)
    rel = idx[:, None] - idx[None, :]
    dmat = jnp.where(rel >= 0, jnp.exp(jnp.maximum(rel, 0.0)[None] * log_gamma[:, None, None]), 0.0)
    scores = jnp.einsum('bnihd,bnjhd->bnhij', q, k) * dmat
    o_intra = jnp.einsum('bnhij,bnjhe->bnihe', scores, v)
    w_state = jnp.exp((C - 1.0 - idx)[None] * log_gamma[:, None])
    chunk_state = jnp.einsum('bnjhd,hj,bnjhe->bnhde', k, w_state, v)
    chunk_decay = jnp.exp(C * log_gamma)[None, None, :, None, None]
    chunk_decay = jnp.broadcast_to(chunk_decay, (B, n, H, 1, 1))
    s_in = _chunk_scan(jnp.moveaxis(chunk_decay, 1, 0), jnp.moveaxis(chunk_state, 1, 0))
    s_in = jnp.moveaxis(s_in, 0, 1)
    w_inter = jnp.exp((idx + 1.0)[None] * log_gamma[:, None])
    o_inter = jnp.einsum('bnihd,hi,bnhde->bnihe', q, w_inter, s_in)
    return (o_intra + o_inter).reshape(B, S, H, dv)

def _multiscale_pool(p, w_pool, scale):
    B, S, _ = p.shape
    pf = p.astype(jnp.float32)
    cs = jnp.concatenate([jnp.zeros((B, 1, BRANCH), jnp.float32), jnp.cumsum(pf, axis=1)], axis=1)
    t = jnp.arange(S)
    outs = []
    for g, w in enumerate(POOL_WINDOWS):
        lo, hi = g * POOL_CH, (g + 1) * POOL_CH
        start = jnp.maximum(t + 1 - w, 0)
        win_sum = cs[:, 1:, lo:hi] - cs[:, start, lo:hi]
        cnt = jnp.minimum(t + 1, w).astype(jnp.float32)[None, :, None]
        outs.append(win_sum / cnt - pf[..., lo:hi])
    pooled = jnp.concatenate(outs, axis=-1).reshape(B, S, len(POOL_WINDOWS), POOL_CH)
    y = jnp.einsum('bsgc,gcd->bsgd', pooled, w_pool).reshape(B, S, BRANCH) * scale
    return y.astype(p.dtype)

def _even_layer(x, w_in, w_a2, b_a, gla_norm_g, sgu_ln_g, sgu_ln_b, w_s, b_s, w_out, ln_g, ln_b):
    B, S, _ = x.shape
    h = x @ w_in
    q, k, v, g_a, a_lr, u, sv, g_b = _split(h, EVEN_SIZES)
    log_a = jax.nn.log_sigmoid((a_lr @ w_a2 + b_a).astype(jnp.float32)) / GLA_TAU
    o = _gla(q.reshape(B, S, GLA_HEADS, GLA_DK), k.reshape(B, S, GLA_HEADS, GLA_DK),
             v.reshape(B, S, GLA_HEADS, GLA_DV), log_a.reshape(B, S, GLA_HEADS, GLA_DK))
    o_a = _head_rmsnorm(o, gla_norm_g).reshape(B, S, BRANCH).astype(x.dtype) * jax.nn.silu(g_a)
    o_b = _spatial_gating(jax.nn.gelu(u), jax.nn.gelu(sv), sgu_ln_g, sgu_ln_b, w_s, b_s) * jax.nn.silu(g_b)
    y = jnp.concatenate([o_a, o_b], axis=-1) @ w_out
    return _layer_norm(DN_ALPHA * x + y, ln_g, ln_b)

def _odd_layer(x, positions, w_in, ret_norm_g, w_pool, pool_scale, w_out, ln_g, ln_b):
    B, S, _ = x.shape
    h = x @ w_in
    q, k, v, g_c, p, g_d = _split(h, ODD_SIZES)
    qr = _rotary(q.reshape(B, S, RET_HEADS, RET_DK), positions)
    kr = _rotary(k.reshape(B, S, RET_HEADS, RET_DK), positions)
    o = _retention(qr, kr, v.reshape(B, S, RET_HEADS, RET_DV))
    o_c = _head_groupnorm(o, ret_norm_g).reshape(B, S, BRANCH).astype(x.dtype) * jax.nn.silu(g_c)
    o_d = _multiscale_pool(p, w_pool, pool_scale) * jax.nn.silu(g_d)
    y = jnp.concatenate([o_c, o_d], axis=-1) @ w_out
    return _layer_norm(DN_ALPHA * x + y, ln_g, ln_b)

def second_inputs(seed: int = 0) -> dict:
    key = jax.random.key(seed)
    ks = jax.random.split(key, 24)
    f32 = jnp.float32
    nrm = lambda k, shape, s: jax.random.normal(k, shape, f32) * s
    d_even = sum(EVEN_SIZES)
    d_odd = sum(ODD_SIZES)
    return {
        "x": jax.random.normal(ks[0], (BATCH, SEQ, D_MODEL), f32),
        "positions": jnp.broadcast_to(jnp.arange(SEQ, dtype=jnp.int32), (BATCH, SEQ)),
        "l0_w_in": nrm(ks[1], (D_MODEL, d_even), D_MODEL ** -0.5),
        "l0_w_a2": nrm(ks[2], (GLA_RANK, GLA_HEADS * GLA_DK), GLA_RANK ** -0.5),
        "l0_b_a": nrm(ks[3], (GLA_HEADS * GLA_DK,), 0.1),
        "l0_gla_norm_g": 1.0 + nrm(ks[4], (GLA_HEADS, GLA_DV), 0.1),
        "l0_sgu_ln_g": 1.0 + nrm(ks[5], (SGU_GROUPS, SGU_CH), 0.1),
        "l0_sgu_ln_b": nrm(ks[6], (SGU_GROUPS, SGU_CH), 0.02),
        "l0_w_s": nrm(ks[7], (SGU_GROUPS, SGU_CHUNK, SGU_CHUNK), 0.5 * SGU_CHUNK ** -0.5),
        "l0_b_s": 1.0 + nrm(ks[8], (SGU_GROUPS, SGU_CHUNK), 0.1),
        "l0_w_out": nrm(ks[9], (MIX_WIDTH, D_MODEL), DN_BETA * MIX_WIDTH ** -0.5),
        "l0_ln_g": 1.0 + nrm(ks[10], (D_MODEL,), 0.1),
        "l0_ln_b": nrm(ks[11], (D_MODEL,), 0.02),
        "l1_w_in": nrm(ks[12], (D_MODEL, d_odd), D_MODEL ** -0.5),
        "l1_ret_norm_g": 1.0 + nrm(ks[13], (RET_HEADS, RET_DV), 0.1),
        "l1_w_pool": nrm(ks[14], (len(POOL_WINDOWS), POOL_CH, POOL_CH), POOL_CH ** -0.5),
        "l1_pool_scale": 0.5 + nrm(ks[15], (BRANCH,), 0.05),
        "l1_w_out": nrm(ks[16], (MIX_WIDTH, D_MODEL), DN_BETA * MIX_WIDTH ** -0.5),
        "l1_ln_g": 1.0 + nrm(ks[17], (D_MODEL,), 0.1),
        "l1_ln_b": nrm(ks[18], (D_MODEL,), 0.02),
    }

def second_block(x, positions, l0_w_in, l0_w_a2, l0_b_a, l0_gla_norm_g, l0_sgu_ln_g, l0_sgu_ln_b,
              l0_w_s, l0_b_s, l0_w_out, l0_ln_g, l0_ln_b, l1_w_in, l1_ret_norm_g, l1_w_pool,
              l1_pool_scale, l1_w_out, l1_ln_g, l1_ln_b):
    even_params = [(l0_w_in, l0_w_a2, l0_b_a, l0_gla_norm_g, l0_sgu_ln_g, l0_sgu_ln_b,
                    l0_w_s, l0_b_s, l0_w_out, l0_ln_g, l0_ln_b)]
    odd_params = [(l1_w_in, l1_ret_norm_g, l1_w_pool, l1_pool_scale, l1_w_out, l1_ln_g, l1_ln_b)]
    for layer in range(DEPTH):
        if layer % 2 == 0:
            x = _even_layer(x, *even_params[layer // 2])
        else:
            x = _odd_layer(x, positions, *odd_params[layer // 2])
    return x


def setup_inputs(seed=0):
    out = dict(first_inputs(seed))
    for name, value in second_inputs(seed + 1).items():
        if name != "x":
            out[name + "_2"] = value
    return out


def reference(
    x, g_mix, g_ffn, rw_mu, rw_w_r, rw_w_k, rw_w_v, rw_w_o, rw_w0, rw_w1, rw_w2, rw_a0, rw_a1,
    rw_a2, rw_g1, rw_g2, rw_k_k, rw_k_a, rw_r_k, rw_lnx_w, rw_lnx_b, kv_g, kv_w, k_norm_g,
    da_w_q, da_q_norm_g, da_lam_q1, da_lam_k1, da_lam_q2, da_lam_k2, da_subln_g, da_w_o,
    ffn_w_gu, ffn_w_down, positions_2, l0_w_in_2, l0_w_a2_2, l0_b_a_2, l0_gla_norm_g_2,
    l0_sgu_ln_g_2, l0_sgu_ln_b_2, l0_w_s_2, l0_b_s_2, l0_w_out_2, l0_ln_g_2, l0_ln_b_2,
    l1_w_in_2, l1_ret_norm_g_2, l1_w_pool_2, l1_pool_scale_2, l1_w_out_2, l1_ln_g_2, l1_ln_b_2,
):
    x = first_block(
        x, g_mix, g_ffn, rw_mu, rw_w_r, rw_w_k, rw_w_v, rw_w_o, rw_w0, rw_w1, rw_w2, rw_a0,
        rw_a1, rw_a2, rw_g1, rw_g2, rw_k_k, rw_k_a, rw_r_k, rw_lnx_w, rw_lnx_b, kv_g, kv_w,
        k_norm_g, da_w_q, da_q_norm_g, da_lam_q1, da_lam_k1, da_lam_q2, da_lam_k2, da_subln_g,
        da_w_o, ffn_w_gu, ffn_w_down,
    )
    return second_block(
        x, positions_2, l0_w_in_2, l0_w_a2_2, l0_b_a_2, l0_gla_norm_g_2, l0_sgu_ln_g_2,
        l0_sgu_ln_b_2, l0_w_s_2, l0_b_s_2, l0_w_out_2, l0_ln_g_2, l0_ln_b_2, l1_w_in_2,
        l1_ret_norm_g_2, l1_w_pool_2, l1_pool_scale_2, l1_w_out_2, l1_ln_g_2, l1_ln_b_2,
    )


_drawn_inputs = setup_inputs


def setup_inputs(seed=0):
    import zlib

    import numpy as np

    out = dict(_drawn_inputs(seed))
    spreads = {}
    factors = {'rw_w1': 3.249,
     'rw_w2': 3.244,
     'rw_lnx_w': 3.751,
     'kv_g': 3.315,
     'k_norm_g': 5.156,
     'da_q_norm_g': 4.976,
     'da_lam_q2': 3.169,
     'da_subln_g': 5.336,
     'l0_b_a_2': 8.0,
     'l0_gla_norm_g_2': 3.67,
     'l0_sgu_ln_g_2': 8.0,
     'l0_sgu_ln_b_2': 31.238,
     'l0_b_s_2': 3.28,
     'l1_ret_norm_g_2': 3.806,
     'l1_pool_scale_2': 8.0,
     'l1_ln_b_2': 2.806}
    for name, (base, spread) in spreads.items():
        noise = np.random.default_rng([zlib.crc32(name.encode()), seed]).standard_normal(out[name].shape)
        drawn = base * np.exp(spread * noise) if base else spread * noise
        out[name] = __import__('jax').numpy.asarray(drawn.astype(out[name].dtype))
    for name, factor in factors.items():
        out[name] = (out[name] * factor).astype(out[name].dtype)
    return out
```

```python
from contextlib import ExitStack

import numpy as np

import concourse.bass as bass
from concourse import mybir

F32 = mybir.dt.float32
F32R = mybir.dt.float32r
BF16 = mybir.dt.bfloat16
I32 = mybir.dt.int32
ALU = mybir.AluOpType
ACT = mybir.ActivationFunctionType
AX = mybir.AxisListType

P = 128
S = 512
D = 1024
KT = D // P
TT = S // P
F = 2816
FT = F // P
HEADS, HN = 16, 64
CH = 64
NCH = S // CH
LAM_INIT = 0.8 - 0.6 * float(np.exp(-0.3))
ALPHA = 4.0 ** 0.25
EXPW = float(np.exp(-0.5))
POOL_WINDOWS = (2, 4, 8, 16)
HEAD_SLOT = (0, 2, 1, 3)
ROUND = 12582912.0
TWO_PI = (6.28125, 0.0019350051879882812, float(2.0 * np.pi - 6.28125 - 0.0019350051879882812))

LEVELS = (1, 2, 4, 8, 16, 32)
CST_PARTS = ("ident", "ones", "blkmean", "allmean", "sel64", "sel128", "rot1", "rot2", "incl", "causal", "blk")
CST = {n: i * P for i, n in enumerate(CST_PARTS)}
MISC = len(CST_PARTS) * P
C_EPS6, C_EPSL, C_EPS5, C_INVF, C_WST, C_CNT = MISC, MISC + 1, MISC + 2, MISC + 3, MISC + 4, MISC + 8
NCST = C_CNT + 4 * 16
LOG_GAMMA = np.log(1.0 - 2.0 ** (-5.0 - np.arange(4)))
GAMMA_CHUNK = [float(np.exp(P * g)) for g in LOG_GAMMA]


def host_constants():
    p = np.arange(P)
    same = (p[:, None] // 64) == (p[None, :] // 64)
    up = p[:, None] <= p[None, :]
    c = np.zeros((P, NCST), np.float32)

    def put(name, m):
        c[:, CST[name]:CST[name] + P] = m

    put("ident", np.eye(P))
    put("ones", 1.0)
    put("blkmean", same / 64.0)
    put("allmean", 1.0 / P)
    sel64 = np.zeros((P, KT, 16))
    sel128 = np.zeros((P, KT, 16))
    for k in range(KT):
        sel64[:64, k, 2 * k] = 1.0
        sel64[64:, k, 2 * k + 1] = 1.0
        sel128[:, k, 2 * k:2 * k + 2] = 1.0
    put("sel64", sel64.reshape(P, P))
    put("sel128", sel128.reshape(P, P))
    rot1 = np.zeros((P, P))
    rot2 = np.zeros((P, P))
    for b in (0, 64):
        for i in range(8):
            rot1[b + 8 + i, b + i] = -1.0
            rot1[b + i, b + 8 + i] = 1.0
        for i in range(32):
            rot2[b + 32 + i, b + i] = -1.0
            rot2[b + i, b + 32 + i] = 1.0
    put("rot1", rot1)
    put("rot2", rot2)
    put("incl", same & up)
    put("causal", up)
    put("blk", same)
    c[:, C_EPS6] = 1e-6
    c[:, C_EPSL] = 64e-5
    c[:, C_EPS5] = 1e-5
    c[:, C_INVF] = (10000.0 ** (-(p % 32).astype(np.float32) / np.float32(32))).astype(np.float32)
    for h in range(4):
        c[:, C_WST + h] = np.exp((P - 1.0 - p) * LOG_GAMMA[h])
    for g, w in enumerate(POOL_WINDOWS):
        c[:, C_CNT + 16 * g:C_CNT + 16 * g + 16] = 1.0 / np.minimum(np.arange(16) + 1, w)
    heads = np.zeros((16, D), np.float32)
    for h in range(16):
        heads[h, 64 * h:64 * h + 64] = 1.0
    lv = np.zeros((P, 7, P), np.float32)
    lv[:, 0] = same & (p[:, None] < p[None, :])
    for n, s in enumerate(LEVELS):
        lv[:, n + 1] = ((p[:, None] // (2 * s)) == (p[None, :] // (2 * s))) & (p[:, None] % (2 * s) < s) & (p[None, :] % (2 * s) >= s)
    keep = np.ones((P, S), np.float32)
    keep[:, ::CH] = 0.0
    inv = 500000.0 ** (-np.arange(0, 16, 2, dtype=np.float32) / np.float32(16))
    ang = np.arange(S, dtype=np.float32)[None, :] * inv.astype(np.float32)[:, None]
    rope = np.zeros((P, 2, S), np.float32)
    rope[:, 0] = 1.0
    for b in (0, 64):
        for r in (0, 8):
            rope[b + r:b + r + 8, 0] = np.cos(ang)
            rope[b + r:b + r + 8, 1] = np.sin(ang)
    ret = np.zeros((P, 4 * P + 2 * S), np.float32)
    for h in range(4):
        rel = p[None, :] - p[:, None]
        at = P * HEAD_SLOT[h]
        ret[:, at:at + P] = 0.125 * np.where(rel >= 0, np.exp(np.maximum(rel, 0) * LOG_GAMMA[h]), 0.0)
        t, b = h // 2, 64 * (h % 2)
        ret[b:b + 64, 4 * P + t * S:4 * P + t * S + S] = 0.125 * np.exp((np.arange(S) % P + 1.0) * LOG_GAMMA[h])[None, :]
    return {"c_main": c, "c_heads": heads, "c_levels": lv.reshape(P, 7 * P), "c_keep": keep, "c_rope": rope.reshape(P, 2 * S),
            "c_ret": ret}


ROWS_A = (("g_mix", 16), ("g_ffn", 16), ("rw_mu", 48), ("rw_w0", 8), ("rw_a0", 8), ("rw_k_k", 8), ("rw_k_a", 8),
          ("rw_r_k", 8), ("rw_lnx_w", 8))
ROWS_B = (("rw_lnx_b", 8), ("kv_g", 8), ("l0_ln_g_2", 8), ("l0_ln_b_2", 8), ("l1_ln_g_2", 8), ("l1_ln_b_2", 8),
          ("l0_b_a_2", 2), ("l0_gla_norm_g_2", 4), ("l0_sgu_ln_g_2", 4), ("l0_sgu_ln_b_2", 4), ("l1_ret_norm_g_2", 4),
          ("l1_pool_scale_2", 4), ("da_subln_g", 1), ("k_norm_g", 1), ("da_q_norm_g", 1))
PV = {}
for _base, _rows in ((0, ROWS_A), (P, ROWS_B)):
    _at = _base
    for _name, _n in _rows:
        PV[_name] = _at
        _at += _n
NROWS_B = sum(n for _, n in ROWS_B)
MU_R, MU_W, MU_K, MU_V, MU_A, MU_G = range(6)


class Plan:
    def __init__(self):
        self.slots = []
        self.steps = []
        self.first = {}
        self.count = {}
        self.first_slot = {}
        self.kstart = [0]
        self.taken = []
        self.last_step_of_slot = {}
        self.n_taken = {"A": 0, "D": 0}

    def product(self, name, slots, steps, slots_per_step, ksteps, taker, reuse=False):
        self.first[name], self.count[name] = len(self.steps), steps
        s0 = len(self.slots) - (slots if reuse else 0)
        self.first_slot[name] = s0
        if not reuse:
            self.slots += [(name, i) for i in range(slots)]
        for i in range(steps):
            at = s0 + (i * slots_per_step if slots_per_step else 0)
            n = slots_per_step or 1
            self.steps.append((name, at, n, ksteps))
            self.kstart.append(self.kstart[-1] + ksteps)
            self.n_taken[taker] += 1
            self.taken.append((taker, self.n_taken[taker]))
            for q in range(at, at + n):
                self.last_step_of_slot[q] = len(self.steps) - 1


def make_plan():
    pl = Plan()
    pl.product("k", 4, 4, 1, 8, "A")
    pl.product("v", 4, 4, 1, 8, "A")
    pl.product("r", 4, 4, 1, 8, "A")
    pl.product("g1", 1, 1, 1, 8, "A")
    pl.product("a1", 1, 1, 1, 8, "A")
    pl.product("w1", 1, 1, 1, 8, "A", reuse=True)
    pl.product("a2", 1, 4, 0, 1, "A")
    pl.product("w2", 1, 4, 0, 1, "A", reuse=True)
    pl.product("g2", 1, 4, 0, 1, "D")
    pl.product("o", 4, 4, 1, 8, "D")
    pl.product("gu0", 22, 22, 1, 8, "D")
    pl.product("dn0", 12, 4, 3, 22, "D")
    pl.product("kk", 4, 4, 1, 8, "A")
    pl.product("kv", 4, 4, 1, 8, "A")
    pl.product("q", 4, 4, 1, 8, "A")
    pl.product("ao", 4, 4, 1, 8, "D")
    pl.product("gu1", 22, 22, 1, 8, "D")
    pl.product("dn1", 12, 4, 3, 22, "D")
    for n, c in (("eq", 1), ("ek", 1), ("elr", 1), ("ev", 2), ("ega", 2), ("esv", 2), ("eu", 2), ("egb", 2)):
        pl.product(n, c, c, 1, 8, "A")
    pl.product("eo", 4, 4, 1, 8, "D")
    for n, c in (("oq", 1), ("ok", 1), ("ov", 2), ("ogc", 2), ("op", 2), ("ogd", 2)):
        pl.product(n, c, c, 1, 8, "A")
    pl.product("oo", 4, 4, 1, 8, "D")
    return pl


PL = make_plan()
X_LAST = ("k", "v", "r", "g1", "a1", "w1", "o", "gu0", "kv", "q", "ao", "gu1", "egb", "eo", "ogd", "oo")
XV = {n: i for i, n in enumerate(("xk", "xv", "xr", "xg", "xa", "xw", "y", "ffn0", "kvin", "qin", "attn", "ffn1",
                                  "even", "evenmix", "odd", "oddmix"))}


NO_XF = ("attn", "even", "evenmix", "odd", "oddmix")
NORM_AT = (0, 8, 16, 24, 28, 32)


def step_end(s):
    return PL.kstart[s + 1]


def slot_end(n):
    s = PL.last_step_of_slot[n]
    name, at, cnt, ks = PL.steps[s]
    return PL.kstart[s] + min(ks, 8 * (n - at + 1))


def xv_last_k(v, k):
    name = X_LAST[v]
    s = PL.first[name] + PL.count[name] - 1
    return PL.kstart[s] + k + 1


class Jobs:
    def __init__(self):
        self.order = []
        self.info = {}
        self.n = {"A": 0, "D": 0}
        self.before = {}
        self.user = {}

    def add(self, key, banks, eng):
        banks = (banks,) if isinstance(banks, int) else tuple(banks)
        self.n[eng] += 1
        self.info[key] = (banks, eng, len(self.order), self.n[eng])
        self.before[key] = [self.user[b] for b in banks if b in self.user]
        for b in banks:
            self.user[b] = ("job", key)
        self.order.append(key)

    def step(self, name):
        for i in range(PL.count[name]):
            s = PL.first[name] + i
            pair = (2 * (s % 2), 2 * (s % 2) + 1)
            self.before[("step", s)] = [self.user[b] for b in pair if b in self.user]
            for b in pair:
                self.user[b] = ("step", s)


GROUPS = 4
NL = len(LEVELS)


def make_jobs():
    j = Jobs()
    j.add(("pv",), 7, "A")
    for k in range(KT):
        j.add(("xt", k), 4 + k % 2, "A")
    j.add(("rms", 0), 6, "A")
    for n in ("k", "v", "r", "g1", "a1", "w1", "a2", "w2"):
        j.step(n)
    j.add(("ksq",), 4, "A")
    j.add(("bonus",), 5, "A")
    for k in range(KT):
        j.add(("kinv", k), 6 + k % 2, "D")
    ring = [0]

    def core(key, eng):
        j.add(key, ring[0] % 8, eng)
        ring[0] += 1

    for tt in range(TT):
        for i in range(2):
            core(("bt", tt, i), "A")
        for i in range(2):
            core(("kt", tt, i), "D")
        for pair in range(2):
            gs = (2 * pair, 2 * pair + 1)
            for g in gs:
                for m in ("At", "Rb", "Ak", "Rk"):
                    core((m, tt, g), "D")
            for g in gs:
                core(("T1", tt, g), "A")
            for g in gs:
                core(("AV", tt, g), "A")
            for lv in range(1, NL):
                for g in gs:
                    core(("G", tt, g, lv), "A")
                for g in gs:
                    if lv < NL - 1:
                        core(("TG", tt, g, lv), "D")
                    core(("TGt", tt, g, lv), "D")
        for c in (2 * tt, 2 * tt + 1):
            for hh in range(2):
                core(("X", c, hh), "D")
            for hh in range(2):
                core(("U", c, hh), "A")
            for hh in range(2):
                core(("SU", c, hh), "D")
            core(("Y", c), "A")
    for k in range(KT):
        j.add(("gmean", k), 6 + k % 2, "D")
    j.add(("gvar",), 5, "A")
    for k in range(KT):
        j.add(("grstd", k), 4, "D")
        j.add(("vT", k), 5, "D")
        j.add(("bb", k), 6, "A")
        if k % 2:
            s = PL.first["g2"] + k // 2
            pr = (2 * (s % 2), 2 * (s % 2) + 1)
            j.before[("step", s)] = [j.user[b] for b in pr if b in j.user]
            for b in pr:
                j.user[b] = ("step", s)
    j.step("o")
    j.add(("rms", 1), 6, "A")
    j.step("gu0")
    j.step("dn0")
    j.add(("lam",), 7, "A")
    j.add(("rms", 2), 6, "A")
    j.step("kk")
    j.step("kv")
    j.step("q")
    for w in "kq":
        j.add(("hsq", w), 4, "A")
        for k in range(KT + 1):
            if k < KT:
                j.add(("hinv", w, k), 4 + k % 2, "D")
            if k:
                j.add(("rot", w, k - 1), 6 + (k - 1) % 2, "D")

    def sc(i):
        j.add(("sc", i), (0, 1) if i % 2 == 0 else (2, 3), "A")

    sc(0)
    for i in range(HEADS // 2 * TT):
        if i + 1 < HEADS // 2 * TT:
            sc(i + 1)
        if i and i % TT == 0:
            j.add(("ot", i // TT - 1), 6 + (i // TT - 1) % 2, "A")
        j.add(("pt", i), 4 + i % 2, "A")
    j.add(("ot", HEADS // 2 - 1), 7, "A")
    j.add(("osq",), 4, "A")
    for k in range(KT):
        j.add(("oinv", k), 5 + k % 2, "D")
    j.step("ao")
    j.add(("rms", 3), 6, "A")
    j.step("gu1")
    j.step("dn1")
    for n in ("eq", "ek", "elr"):
        j.step(n)
    j.add(("za", 0), 4, "D")
    j.add(("za", 1), 5, "D")
    for n in ("ev", "ega", "esv", "eu", "egb"):
        j.step(n)
    j.add(("wsT",), 7, "D")
    for t in range(-1, TT):
        if t + 1 < TT:
            j.add(("gkt", t + 1), 4, "A")
            j.add(("gs", t + 1), (6, 7), "D")
        if t >= 0:
            for c in (2 * t, 2 * t + 1):
                j.add(("gu", c), 2 + c % 2, "D")
            for c in (2 * t, 2 * t + 1):
                j.add(("go", c), c % 2, "A")
    for g in range(4):
        j.add(("smean", g), g % 2, "D")
    j.add(("gosq",), 4, "A")
    j.add(("svar",), 5, "A")
    for g in range(4):
        j.add(("gorb", g), 6 + g % 2, "D")
    for g in range(4):
        j.add(("srb", g), g % 2, "D")
    for g in range(4):
        j.add(("svT", g), 2 + g % 2, "A")
        j.add(("sg", g), 4 + g % 2, "D")
    j.step("eo")
    j.add(("lm", 0), 6, "D")
    j.add(("lv", 0), 7, "A")
    for n in ("oq", "ok"):
        j.step(n)
    for i in range(4):
        j.add(("rt", i), 4 + i % 2, "D")
    for n in ("ov", "ogc", "op", "ogd"):
        j.step(n)
    for g in range(4):
        j.add(("pool", g), 5, "D")
    for t in range(-1, TT):
        if t + 1 < TT:
            j.add(("rkt", t + 1), 4, "D")
            j.add(("rs", t + 1), (6, 7), "D")
        if t >= 0:
            j.add(("ru", t), 2 + t % 2, "D")
            j.add(("ro", t), t % 2, "A")
    for h in range(4):
        j.add(("rmean", h), h % 2, "D")
    j.add(("rvar",), 4, "A")
    for h in range(4):
        j.add(("rrb", h), 6 + h % 2, "D")
    j.step("oo")
    j.add(("lm", 1), 6, "D")
    j.add(("lv", 1), 7, "A")
    for t in range(TT):
        for i in range(2):
            j.add(("out", t, i), 4 + i, "A")
    return j


NDMA = {"g1": 1, "elr": 1}


def raw_count(n):
    return sum(NDMA.get(PL.slots[q][0], 2) for q in range(n % 2, n + 1, 2))


def regions(n, t):
    name = PL.slots[n][0]
    v = t[:, :].rearrange("p (k c) -> p k c", k=8)
    if name in ("a1", "elr"):
        return [v[:, :, 0:128]]
    if name == "g1":
        return [v[:, :, 0:160]]
    if name == "a2":
        return [t[:, 0:1024]]
    if name == "g2":
        return [t[:, 0:1024], t[96:128, 1024:2048]]
    if name in ("dn0", "dn1") and PL.slots[n][1] % 3 == 2:
        return [v[:, 0:6, :]]
    return [t[:, :]]


def build(nc, t, out):
    JB = make_jobs()
    ctx = ExitStack()
    with ctx:
        base = (nc.sbuf_base + 31) // 32 * 32
        end = nc.sbuf_usable_end
        top = [base]

        def size(shape, dt):
            n = 2 if dt == BF16 else 4
            for s in shape[1:]:
                n *= s
            return (n + 31) // 32 * 32

        def at(name, shape, dt, offset):
            assert offset + size(shape, dt) <= end, (name, offset + size(shape, dt) - end)
            return nc.alloc_sbuf_tensor_at(name, shape, dt, offset=offset)

        def sb(name, shape, dt=F32):
            r = at(name, shape, dt, top[0])
            top[0] += size(shape, dt)
            return r

        def sem(name):
            return ctx.enter_context(nc.semaphore(name))

        x = sb("x", [P, KT, S])
        xf = sb("xf", [P, 2, S])
        rt = sb("rt", [P, S])
        cst = sb("cst", [P, NCST])
        heads_r = sb("heads_r", [16, D], F32R)
        pv = sb("pv", [P, P + NROWS_B])
        omu = sb("omu", [P, 48])
        col = sb("col", [P, 16])
        raw_at = top[0]
        weight_raw = [sb(f"weight_raw{i}", [P, 2048]) for i in range(2)]
        w_at = top[0]
        w_hi = [sb(f"w_hi{i}", [P, 2048], F32R) for i in range(2)]
        w_lo = [sb(f"w_lo{i}", [P, 2048], F32R) for i in range(2)]
        x_at = top[0]
        X_hi = sb("X_hi", [P, KT, S], F32R)
        X_lo = sb("X_lo", [P, KT, S], F32R)
        arena = top[0]

        def here(offset):
            spot = [offset]

            def alloc(name, shape, dt=F32):
                r = at(name, shape, dt, spot[0])
                spot[0] += size(shape, dt)
                return r
            alloc.spot = spot
            return alloc

        a_ = here(arena)
        xtok = a_("xtok", [P, TT, D])
        prow = [a_("prow0", [P, P]), a_("prow1", [NROWS_B, P])]
        heads_f = a_("heads_f", [16, D])
        lamr = a_("lamr", [1, 256])
        lamp = a_("lamp", [1, 128])
        a_ = here(arena)
        h_sb = a_("h_sb", [P, KT, S + 1])
        kf = a_("kf", [P, KT, S])
        rf = a_("rf", [P, KT, S])
        af = a_("af", [P, KT, S])
        vt = a_("vt", [P, TT, D])
        sgf = a_("sgf", [P, 2, S])
        keep = a_("keep", [P, S])
        pchunk = a_("pchunk", [P, KT, NCH])
        mid_hi = a_("mid_hi", [P, S], F32R)
        mid_lo = a_("mid_lo", [P, S], F32R)
        midf_at = a_.spot[0]
        midf = a_("midf", [P, S])
        lvl = here(midf_at)("lvl", [P, 7, P])
        xs = here(midf_at - 2 * size([P, S], F32))("xs", [P, D])
        b_ = here(x_at)
        u0 = b_("u0", [P, KT, S])
        u1 = b_("u1", [P, KT, S])
        b_ = here(x_at + size([P, KT, S], F32))
        btok = b_("btok", [P, D])
        ktok = b_("ktok", [P, D])
        state = [b_(f"state{i}", [P, KT, P]) for i in range(2)]
        b_ = here(w_at)
        Tt = b_("Tt", [P, 4, GROUPS * P])
        Rb = b_("Rb", [P, 4, GROUPS * P])
        Rk = b_("Rk", [P, 4, GROUPS * P])
        AV = b_("AV", [P, D])
        us = b_("us", [P, D])
        b_ = here(raw_at)
        tmp = b_("tmp", [P, 8, S])
        b_ = here(raw_at)
        At = b_("At", [P, 2, S])
        Tn = b_("Tn", [P, 2, S])
        Gs = b_("Gs", [P, 2, S])
        Lm = b_("Lm", [P, 2, S])
        Ak = xf
        b_ = here(arena + size([P, KT, S + 1], F32))
        sg_hi = b_("sg_hi", [P, 2, S], F32R)
        sg_lo = b_("sg_lo", [P, 2, S], F32R)
        gn_hi = b_("gn_hi", [16, S], F32R)
        gn_lo = b_("gn_lo", [16, S], F32R)
        bon_hi = b_("bon_hi", [16, S], F32R)
        bon_lo = b_("bon_lo", [16, S], F32R)
        b_ = here(arena + size([P, KT, S + 1], F32) + 2 * size([P, KT, S], F32))
        pt8 = b_("pt8", [P, 8, S])
        a_ = here(arena)
        hb_hi = a_("hb_hi", [P, FT, S], F32R)
        hb_lo = a_("hb_lo", [P, FT, S], F32R)
        sgate = a_("sgate", [P, 2, S])
        a_ = here(arena)
        ak = a_("ak", [P, KT, S])
        aq = a_("aq", [P, KT, S])
        av = a_("av", [P, TT, D])
        oT = a_("oT", [P, KT, S])
        rope = a_("rope", [P, 2, S])
        Pb = a_("Pb", [P, 4, S])
        PTs = a_("PTs", [P, 2, S])
        tq2 = a_("tq2", [P, 2, S])
        n_hi = a_("n_hi", [16, S], F32R)
        n_lo = a_("n_lo", [16, S], F32R)
        a_ = here(arena)
        mix = a_("mix", [P, KT, S])
        eqk = a_("eqk", [P, 4, S])
        ev = a_("ev", [P, TT, S])
        ega = a_("ega", [P, 4, S])
        esv = a_("esv", [P, 4, S])
        egb = a_("egb", [P, 4, S])
        elr = a_("elr", [16, S])
        gw = a_("gw", [P, 4, S])
        gcum = a_("gcum", [P, 2, S])
        gend = a_("gend", [P, 2, NCH])
        keep_e = a_("keep_e", [P, S])
        en_hi = a_("en_hi", [16, S], F32R)
        en_lo = a_("en_lo", [16, S], F32R)
        wa2 = a_("wa2", [16, 256])
        ws = a_("ws", [P, 4, P])
        wsT = a_("wsT", [P, 4, P])
        bsr = a_("bsr", [1, S])
        svt = a_("svt", [P, 2, S])
        b_ = here(x_at)
        kt2 = b_("kt2", [P, 2, 256])
        sT = b_("sT", [P, 2, S])
        est = [b_(f"est{i}", [P, 4, P]) for i in range(2)]
        a_ = here(arena)
        omix = a_("omix", [P, KT, S])
        oqk = a_("oqk", [P, 4, S])
        ov = a_("ov", [P, TT, S])
        ogc = a_("ogc", [P, 4, S])
        ogd = a_("ogd", [P, 4, S])
        PAD = max(POOL_WINDOWS)
        opp = a_("opp", [P, 4, PAD + S])
        psh = a_("psh", [P, 2, PAD + S])
        csn = a_("csn", [P, 2, S])
        cret = a_("cret", [P, 4 * P + 2 * S])
        oqi = a_("oqi", [P, 2, S])
        orw = a_("orw", [P, 2, S])
        pool16 = a_("pool16", [P, 16])
        posi = a_("posi", [P, S], I32)
        on_hi = a_("on_hi", [16, S], F32R)
        on_lo = a_("on_lo", [16, S], F32R)
        wpl = a_("wpl", [P, 4, P])
        a_ = here(arena)
        ost = a_("ost", [P, TT, D])
        psum = ctx.enter_context(nc.psum_tensor("psum", [P, 8, S], F32))

        cst_in = sem("cst_in")
        rows_in = sem("rows_in")
        x_in = sem("x_in")
        heads_in = sem("heads_in")
        keep_in = sem("keep_in")
        lvl_in = sem("lvl_in")
        raw_full = [sem("raw_full0"), sem("raw_full1")]
        hi_ready = sem("hi_ready")
        lo_ready = sem("lo_ready")
        kstep = sem("kstep")
        step_a, step_d = sem("step_a"), sem("step_d")
        job_done = sem("job_done")
        job_a, job_d = sem("job_a"), sem("job_d")
        xf_ready = sem("xf_ready")
        xhi_ready, xlo_ready = sem("xhi_ready"), sem("xlo_ready")
        sq_ready, sq_used = sem("sq_ready"), sem("sq_used")
        heads_ready = sem("heads_ready")
        dve_seq = sem("dve_seq")
        act_seq = sem("act_seq")
        pool_seq = sem("pool_seq")
        mid_f, mid_h, mid_l = sem("mid_f"), sem("mid_h"), sem("mid_l")
        prep_a, prep_d, prep_p, prep_pe = sem("prep_a"), sem("prep_d"), sem("prep_p"), sem("prep_pe")
        kn_f, kn_h, kn_l = sem("kn_f"), sem("kn_h"), sem("kn_l")
        at_ready = sem("at_ready")
        zero_ready = sem("zero_ready")
        level_ready = sem("level_ready")
        t_init = sem("t_init")
        s_new = sem("s_new")
        sg_h, sg_l = sem("sg_h"), sem("sg_l")
        gn_q, gn_pe, gn_aff = sem("gn_q"), sem("gn_pe"), sem("gn_aff")
        ff_gate, ff_hi, ff_lo = sem("ff_gate"), sem("ff_hi"), sem("ff_lo")
        out_sem = sem("out_sem")
        hn_a, hn_pe = sem("hn_a"), sem("hn_pe")
        rope_in, lam_in = sem("rope_in"), sem("lam_in")
        lam_row, lam_ready = sem("lam_row"), sem("lam_ready")
        sc_max = sem("sc_max")
        pc_ready = sem("pc_ready")
        hn_rot = sem("hn_rot")
        small_in = sem("small_in")
        gl_a, gl_d = sem("gl_a"), sem("gl_d")
        g_state = sem("g_state")
        sv_ready = sem("sv_ready")
        gate_p = sem("gate_p")
        mix_a = sem("mix_a")
        ln_x, ln_c, ln_g, ln_b = sem("ln_x"), sem("ln_c"), sem("ln_g"), sem("ln_b")
        odd_in, pos_in = sem("odd_in"), sem("pos_in")
        ang_d, ang_a = sem("ang_d"), sem("ang_a")
        rot_done = sem("rot_done")
        r_state = sem("r_state")
        win_p, win_d = sem("win_p"), sem("win_d")
        omix_a = sem("omix_a")

        def bank(i, n=S):
            return psum[:, i, 0:n]

        def job_banks(key):
            return JB.info[key][0]

        def wait_done(eng, key):
            eng.wait_ge(job_done, JB.info[key][2] + 1)

        def wait_job(eng, key):
            _, who, _, n = JB.info[key]
            eng.wait_ge(job_a if who == "A" else job_d, n)

        def wait_step(eng, s):
            who, n = PL.taken[s]
            eng.wait_ge(step_a if who == "A" else step_d, n)

        def wait_product(eng, name):
            wait_step(eng, PL.first[name] + PL.count[name] - 1)

        def wait_banks(eng, key):
            for kind, what in JB.before[key]:
                if kind == "job":
                    wait_job(eng, what)
                else:
                    wait_step(eng, what)

        def step_banks(s):
            return 2 * (s % 2), 2 * (s % 2) + 1

        def pcol(name, i=0, rows=slice(0, P)):
            return pv[rows, PV[name] + i:PV[name] + i + 1]

        def c_(name, n=P, o=0):
            return cst[:, CST[name] + o:CST[name] + o + n]

        def wv(tile):
            return tile[:, :].rearrange("p (k c) -> p k c", k=8)

        def xready(v, k):
            return 8 * v + k + 1

        def xf_count(v, k):
            return 8 * (v - sum(1 for n in NO_XF if XV[n] < v)) + k + 1

        def group_head(g, j):
            return 8 * (g // 2) + 2 * j + g % 2

        def head_group(hd):
            return 2 * (hd // 8) + hd % 2, hd % 8 // 2

        def hn_pe_count(at, k):
            return at - NORM_AT.index(at) + k + 1

        block = ctx.enter_context(nc.Block())

        @block.sync
        def _(sp):
            def weight_src(n):
                name, i = PL.slots[n]
                square = {"k": t["rw_w_k"][0], "v": t["rw_w_v"][0], "r": t["rw_w_r"][0], "o": t["rw_w_o"][0],
                          "kk": t["kv_w"][:, 0:D], "kv": t["kv_w"][:, D:2 * D], "q": t["da_w_q"][0],
                          "ao": t["da_w_o"][0], "eo": t["l0_w_out_2"], "oo": t["l1_w_out_2"]}
                inner = {"eq": ("l0_w_in_2", 0), "ek": ("l0_w_in_2", 256), "ev": ("l0_w_in_2", 512),
                         "ega": ("l0_w_in_2", 1024), "eu": ("l0_w_in_2", 1552), "esv": ("l0_w_in_2", 2064),
                         "egb": ("l0_w_in_2", 2576), "oq": ("l1_w_in_2", 0), "ok": ("l1_w_in_2", 256),
                         "ov": ("l1_w_in_2", 512), "ogc": ("l1_w_in_2", 1024), "op": ("l1_w_in_2", 1536),
                         "ogd": ("l1_w_in_2", 2048)}
                r = weight_raw[n % 2]
                w3 = wv(r)
                if name in square:
                    src = square[name][:, 256 * i:256 * i + 256].rearrange("(k p) c -> p k c", p=P)
                    return [(w3[:, 0:4, :], src[:, 0:4, :]), (w3[:, 4:8, :], src[:, 4:8, :])]
                if name in inner:
                    w, c0 = inner[name]
                    src = t[w][:, c0 + 256 * i:c0 + 256 * i + 256].rearrange("(k p) c -> p k c", p=P)
                    return [(w3[:, 0:4, :], src[:, 0:4, :]), (w3[:, 4:8, :], src[:, 4:8, :])]
                if name == "elr":
                    return [(w3[:, :, 0:128], t["l0_w_in_2"][:, 1536:1664].rearrange("(k p) c -> p k c", p=P))]
                if name == "g1":
                    return [(w3[:, :, 0:160], t["rw_g1"][0].rearrange("(k p) c -> p k c", p=P))]
                if name == "a1":
                    return [(w3[:, :, 0:64], t["rw_w1"][0].rearrange("(k p) c -> p k c", p=P)),
                            (w3[:, :, 64:128], t["rw_a1"][0].rearrange("(k p) c -> p k c", p=P))]
                if name == "a2":
                    return [(r[0:64, 0:1024], t["rw_w2"][0]), (r[64:128, 0:1024], t["rw_a2"][0])]
                if name == "g2":
                    return [(r[:, 0:1024], t["rw_g2"][0, 0:128, :]), (r[96:128, 1024:2048], t["rw_g2"][0, 128:160, :])]
                raise AssertionError(name)

            def fill(n):
                if n >= 2:
                    sp.wait_ge(lo_ready, n - 1)
                for dst, src in weight_src(n):
                    sp.dma_start(dst, src).then_inc(raw_full[n % 2], 16)

            def fill_product(name):
                for i in range(sum(1 for q in PL.slots if q[0] == name)):
                    fill(PL.first_slot[name] + i)

            def fill_ffn(layer):
                n0 = PL.first_slot[f"gu{layer}"]
                src = t["ffn_w_gu"][layer].rearrange("(k p) (g c) -> p k g c", p=P, g=2)
                with sp.Fori(0, FT // 2) as i:
                    for j in range(2):
                        sp.wait_ge(lo_ready, n0 + j - 1 + 2 * i)
                        d3 = wv(weight_raw[(n0 + j) % 2])
                        for g in range(2):
                            sp.dma_start(d3[:, :, P * g:P * g + P],
                                         src[:, :, g, bass.ds(256 * i + 128 * j, 128)]).then_inc(
                                             raw_full[(n0 + j) % 2], 16)
                n0 = PL.first_slot[f"dn{layer}"]
                wd = t["ffn_w_down"][layer].rearrange("(k p) c -> p k c", p=P)
                with sp.Fori(0, 2) as i:
                    for j in range(6):
                        sp.wait_ge(lo_ready, n0 + j - 1 + 6 * i)
                        ks = 8 if j % 3 < 2 else 6
                        for k0, k1 in ((0, 4), (4, ks)):
                            sp.dma_start(wv(weight_raw[(n0 + j) % 2])[:, k0:k1, :],
                                         wd[:, 8 * (j % 3) + k0:8 * (j % 3) + k1,
                                            bass.ds(512 * i + 256 * (j // 3), 256)]
                                         ).then_inc(raw_full[(n0 + j) % 2], 16)

            sp.dma_start(cst[:, :], t["c_main"]).then_inc(cst_in, 16)
            for i in range(2):
                sp.dma_start(xtok[:, 2 * i:2 * i + 2, :],
                             t["x"][0].rearrange("(t p) d -> p t d", p=P)[:, 2 * i:2 * i + 2, :]).then_inc(x_in, 16)
            for i, rows in enumerate((ROWS_A, ROWS_B)):
                r = 0
                for name, n in rows:
                    src = t[name]
                    if name in ("k_norm_g", "da_q_norm_g"):
                        src = src if len(src.shape) == 1 else src[0]
                        for half in range(2):
                            sp.dma_start(prow[i][r:r + 1, 64 * half:64 * half + 64],
                                         src.rearrange("(a b) -> a b", a=1)).then_inc(rows_in, 16)
                    else:
                        dims = " ".join("abc"[:len(src.shape)])
                        flat = src.rearrange(f"{dims} -> ({dims})") if len(src.shape) > 1 else src
                        sp.dma_start(prow[i][r:r + n, :], flat.rearrange("(r c) -> r c", c=P)).then_inc(rows_in, 16)
                    r += n
            for i, name in enumerate(("da_lam_q1", "da_lam_k1", "da_lam_q2", "da_lam_k2")):
                sp.dma_start(lamr[0:1, 64 * i:64 * i + 64], t[name]).then_inc(lam_in, 16)
            sp.dma_start(heads_f[:, :], t["c_heads"]).then_inc(heads_in, 16)
            for name in ("k", "v", "r", "g1", "a1", "a2"):
                fill_product(name)
                if name == "k":
                    sp.dma_start(keep[:, :], t["c_keep"]).then_inc(keep_in, 16)
            wait_product(sp, "w2")
            sp.wait_ge(mid_l, 2)
            sp.dma_start(lvl[:, :, :], t["c_levels"].rearrange("p (n c) -> p n c", c=P)).then_inc(lvl_in, 16)
            wait_job(sp, ("Y", NCH - 1))
            fill_product("g2")
            fill_product("o")
            fill_ffn(0)
            fill_product("kk")
            wait_product(sp, "dn0")
            sp.dma_start(rope[:, :, :], t["c_rope"].rearrange("p (a s) -> p a s", a=2)).then_inc(rope_in, 16)
            for name in ("kv", "q", "ao"):
                fill_product(name)
            fill_ffn(1)
            wait_product(sp, "dn1")
            sp.dma_start(keep_e[:, :], t["c_keep"]).then_inc(small_in, 16)
            sp.dma_start(wa2[:, :], t["l0_w_a2_2"]).then_inc(small_in, 16)
            sp.dma_start(ws[:, :, :], t["l0_w_s_2"].rearrange("g t s -> t g s")).then_inc(small_in, 16)
            sp.dma_start(bsr[0:1, :], t["l0_b_s_2"].rearrange("(a g) t -> a (g t)", a=1)).then_inc(small_in, 16)
            for name in ("eq", "ek", "elr", "ev", "ega", "esv", "eu", "egb", "eo"):
                fill_product(name)
            wait_product(sp, "eo")
            sp.dma_start(posi[:, :], t["positions_2"].to_broadcast([P, S])).then_inc(pos_in, 16)
            sp.dma_start(cret[:, :], t["c_ret"]).then_inc(odd_in, 16)
            sp.dma_start(wpl[:, :, :], t["l1_w_pool_2"].rearrange("g c d -> c g d")).then_inc(odd_in, 16)
            for name in ("oq", "ok", "ov", "ogc", "op", "ogd", "oo"):
                fill_product(name)
            for tt in range(TT):
                wait_job(sp, ("out", tt, 1))
                sp.dma_start(out.rearrange("a (t p) d -> p (a t) d", p=P)[:, tt, :], ost[:, tt, :]).then_inc(out_sem, 16)
            sp.wait_ge(out_sem, 16 * TT)

        @block.gpsimd
        def _(pool):
            seq = [0]

            def link(ins):
                seq[0] += 1
                ins.then_inc(pool_seq, 1)
                pool.wait_ge(pool_seq, seq[0])

            def low(n, dyn=0):
                pool.wait_ge(hi_ready, n + 1 + dyn)
                parts = list(zip(regions(n, weight_raw[n % 2]), regions(n, w_hi[n % 2]), regions(n, w_lo[n % 2])))
                for i, (r, h, l) in enumerate(parts):
                    ins = pool.tensor_tensor(l, r, h.bitcast(F32), ALU.subtract)
                    if i < len(parts) - 1:
                        link(ins)
                ins.then_inc(lo_ready, 1)
                if len(parts) > 1:
                    pool.wait_ge(lo_ready, n + 1)

            def low_product(name):
                for i in range(sum(1 for q in PL.slots if q[0] == name)):
                    low(PL.first_slot[name] + i)

            def low_ffn(layer):
                n0 = PL.first_slot[f"gu{layer}"]
                with pool.Fori(0, FT // 2) as i:
                    for j in range(2):
                        low(n0 + j, 2 * i)
                n0 = PL.first_slot[f"dn{layer}"]
                with pool.Fori(0, 2) as i:
                    for j in range(6):
                        low(n0 + j, 6 * i)

            for name in ("k", "v", "r", "g1", "a1", "a2"):
                low_product(name)
            for k in range(KT):
                pool.wait_ge(prep_d, 6 * k + 1)
                pool.tensor_tensor(h_sb[:, k, 0:S], u1[:, k, :], h_sb[:, k, 0:S], ALU.subtract).then_inc(prep_p, 1)
                pool.wait_ge(prep_a, 5 * k + 3)
                pool.wait_ge(prep_d, 6 * k + 4)
                pool.tensor_tensor(rf[:, k, :], rf[:, k, :], tmp[:, 4 + k % 2, :], ALU.mult).then_inc(prep_p, 1)
            pool.wait_ge(lvl_in, 16)
            for tt in range(TT):
                for pair in range(2):
                    for g in (2 * pair, 2 * pair + 1):
                        wait_job(pool, ("At", tt, g))
                        if tt:
                            wait_done(pool, ("Y", 2 * tt - 1))
                        gb = g % 2
                        a3 = At[:, gb, :].rearrange("p (h c) -> p h c", h=GROUPS)
                        t3 = Tt[:, g, :].rearrange("p (h c) -> p h c", h=GROUPS)
                        link(pool.tensor_tensor(t3, a3, lvl[:, 1:2, :].to_broadcast([P, GROUPS, P]), ALU.mult))
                        pool.tensor_tensor(t3, t3, c_("ident")[:, None, :].to_broadcast([P, GROUPS, P]),
                                           ALU.add).then_inc(t_init, 1)
                    for lv in range(1, NL):
                        for g in (2 * pair, 2 * pair + 1):
                            gb = g % 2
                            if lv > 1:
                                wait_done(pool, ("G", tt, g, lv - 1))
                            elif tt or pair:
                                wait_done(pool, ("G", tt if pair else tt - 1, (g + 2) % 4, NL - 1))
                            pool.tensor_tensor(Lm[:, gb, :].rearrange("p (h c) -> p h c", h=GROUPS),
                                               At[:, gb, :].rearrange("p (h c) -> p h c", h=GROUPS),
                                               lvl[:, lv + 1:lv + 2, :].to_broadcast([P, GROUPS, P]),
                                               ALU.mult).then_inc(level_ready, 1)
            low_product("g2")
            low_product("o")
            low_ffn(0)
            for name in ("kk", "kv", "q", "ao"):
                low_product(name)
            low_ffn(1)
            for name in ("eq", "ek", "elr", "ev", "ega", "esv", "eu", "egb"):
                low_product(name)
            wait_product(pool, "egb")
            for g in range(4):
                pool.tensor_tensor(mix[:, 4 + g, :], mix[:, 4 + g, :], egb[:, g, :], ALU.mult).then_inc(gate_p, 1)
            low_product("eo")
            wait_product(pool, "eo")
            pool.memset(opp[:, :, 0:PAD], 0.0)
            link(pool.memset(psh[:, :, 0:PAD], 0.0))
            for name in ("oq", "ok", "ov", "ogc", "op", "ogd"):
                low_product(name)
            low(PL.first_slot["oo"])
            wait_product(pool, "op")
            for g in range(4):
                if g >= 1:
                    pool.wait_ge(win_d, g)
                src = opp[:, g, :]
                for i in range(g + 1):
                    dst = psh[:, i % 2, :]
                    sh = 1 << i
                    ins = pool.tensor_tensor(dst[:, PAD:PAD + S], src[:, PAD:PAD + S],
                                             src[:, PAD - sh:PAD - sh + S], ALU.add)
                    if i < g:
                        link(ins)
                    src = dst
                ins.then_inc(win_p, 1)
            for i in range(1, 4):
                low(PL.first_slot["oo"] + i)

        @block.scalar
        def _(act):
            seq = [0]

            def link(ins):
                seq[0] += 1
                ins.then_inc(act_seq, 1)
                act.wait_ge(act_seq, seq[0])

            def ffn(layer):
                s0, n0 = PL.first[f"gu{layer}"], PL.first_slot[f"gu{layer}"]
                with act.Fori(0, FT // 2) as i:
                    for j in range(2):
                        high(n0 + j + 1, 32 * i, 16 * i)
                        act.wait_ge(kstep, step_end(s0 + j) + 16 * i)
                        act.activation(sgate[:, j, :], bank(step_banks(s0 + j)[0]), ACT.Silu).then_inc(ff_gate, 1)
                        act.wait_ge(step_d, PL.taken[s0 + j][1] + 2 * i)
                        act.activation(hb_hi[:, bass.ds(2 * i + j, 1), :], xf[:, j:j + 1, :],
                                       ACT.Copy).then_inc(ff_hi, 1)
                n0 = PL.first_slot[f"dn{layer}"]
                with act.Fori(0, 2) as i:
                    for j in range(6):
                        high(n0 + j + 1, 96 * i, 44 * i)

            def high(n, raw_dyn=0, k_dyn=0):
                act.wait_ge(raw_full[n % 2], 16 * raw_count(n) + raw_dyn)
                if n >= 2:
                    act.wait_ge(kstep, slot_end(n - 2) + k_dyn)
                for r, h in zip(regions(n, weight_raw[n % 2]), regions(n, w_hi[n % 2])):
                    last = act.activation(h, r, ACT.Copy)
                last.then_inc(hi_ready, 1)

            def next_slot(s):
                n = PL.steps[s][1]
                if n + 1 < len(PL.slots) and (s == 0 or PL.steps[s - 1][1] != n):
                    high(n + 1)

            def empty(key, out_, func=ACT.Copy, **kw):
                wait_done(act, key)
                act.activation(out_, bank(job_banks(key)[0]), func, **kw).then_inc(job_a, 1)

            def x_high1(v, k, src=None):
                if src is None:
                    act.wait_ge(xf_ready, xf_count(v, k))
                if v:
                    act.wait_ge(kstep, xv_last_k(v - 1, k))
                act.activation(X_hi[:, k, :], src[:, k, :] if src is not None else xf[:, (8 * v + k) % 2, :],
                               ACT.Copy).then_inc(xhi_ready, 1)

            def x_high(v, src=None):
                for k in range(KT):
                    x_high1(v, k, src)

            def norm_squares(i):
                for k in range(KT):
                    if i == 0:
                        wait_job(act, ("xt", k))
                    elif k % 2 == 0:
                        wait_step(act, PL.first[("", "o", "dn0", "ao")[i]] + k // 2)
                    if k >= 2:
                        act.wait_ge(sq_used, 7 * i + k - 1)
                    act.activation(xf[:, k % 2, :], x[:, k, :], ACT.Square).then_inc(sq_ready, 1)
                wait_done(act, ("rms", i))
                act.activation(rt[:, :], bank(6), ACT.Sqrt, bias=cst[:, C_EPS6:C_EPS6 + 1],
                               scale=1.0 / D).then_inc(job_a, 1)

            def plain_last(name, dst, then=None, func=ACT.Copy, tokens=False):
                for i in range(PL.count[name]):
                    s = PL.first[name] + i
                    next_slot(s)
                    if i == PL.count[name] - 1 and then is not None:
                        x_high(then)
                    act.wait_ge(kstep, step_end(s))
                    b = step_banks(s)
                    if tokens:
                        for m in range(2):
                            last = act.activation(dst[:, 2 * m:2 * m + 2, 256 * i:256 * i + 256],
                                                  psum[:, b[m], :].rearrange("p (t c) -> p t c", t=2), func)
                    else:
                        for m in range(2):
                            last = act.activation(dst[:, 2 * i + m, 0:S], bank(b[m]), func)
                    last.then_inc(step_a, 1)

            def head_scale(src, n, at, key, scale, eps, ready, count, hi, before=None, free=None):
                for k in range(n):
                    if before is not None:
                        before(k)
                    if k >= 2:
                        act.wait_ge(hn_pe, hn_pe_count(at, k - 2))
                    act.activation(xf[:, k % 2, :], src[:, k, 0:S], ACT.Square).then_inc(hn_a, 1)
                wait_done(act, key)
                act.activation(rt[0:16, :], psum[0:16, job_banks(key)[0], :], ACT.Sqrt, bias=cst[0:16, eps:eps + 1],
                               scale=scale).then_inc(job_a, 1)
                act.wait_ge(ready, count)
                if free is not None:
                    wait_done(act, free)
                act.activation(hi[:, :], rt[0:16, :], ACT.Copy).then_inc(kn_h, 1)

            def layer_norm(n):
                name = ("eo", "oo")[n]
                for i in range(PL.count[name]):
                    next_slot(PL.first[name] + i)
                for k in range(KT):
                    act.wait_ge(ln_c, 8 * n + k + 1)
                    if k >= 2:
                        act.wait_ge(sq_used, 7 * (4 + n) + k - 1)
                    act.activation(xf[:, k % 2, :], x[:, k, :], ACT.Square).then_inc(sq_ready, 1)
                wait_done(act, ("lv", n))
                act.activation(rt[:, :], bank(7), ACT.Sqrt, bias=cst[:, C_EPS5:C_EPS5 + 1],
                               scale=1.0 / D).then_inc(job_a, 1)
                for k in range(KT):
                    act.wait_ge(ln_g, 8 * n + k + 1)
                    act.activation(x[:, k, :], x[:, k, :], ACT.Identity,
                                   bias=pcol(f"l{n}_ln_b_2", k)).then_inc(ln_b, 1)

            def odd_angles():
                act.wait_ge(ang_d, 1)
                act.activation(csn[:, 1, :], orw[:, 0, :], ACT.Sin)
                act.activation(csn[:, 0, :], orw[:, 0, :], ACT.Sin, scale=0.5).then_inc(ang_a, 1)

            high(0)
            act.wait_ge(heads_in, 16)
            act.activation(heads_r[:, :], heads_f[:, :], ACT.Copy).then_inc(heads_ready, 1)
            wait_done(act, ("pv",))
            act.activation(pv[:, :], psum[:, 7, 0:P + NROWS_B], ACT.Copy).then_inc(job_a, 1)
            for k in range(KT):
                empty(("xt", k), x[:, k, :])
            norm_squares(0)
            x_high(0)
            plain_last("k", kf, 1)
            plain_last("v", vt, 2, tokens=True)
            plain_last("r", rf, 3)
            s = PL.first["g1"]
            next_slot(s)
            x_high(4)
            act.wait_ge(kstep, step_end(s))
            b = step_banks(s)
            act.activation(sgf[:, 0, :], bank(b[0]), ACT.Sigmoid)
            act.activation(sgf[96:128, 1, :], psum[96:128, b[1], :], ACT.Sigmoid).then_inc(step_a, 1)
            s = PL.first["a1"]
            next_slot(s)
            x_high(5)
            act.wait_ge(kstep, step_end(s))
            act.activation(midf[64:128, :], psum[64:128, step_banks(s)[0], :], ACT.Copy).then_inc(step_a, 1)
            wait_step(act, s)
            act.activation(mid_hi[64:128, :], midf[64:128, :], ACT.Copy).then_inc(mid_h, 1)
            s = PL.first["w1"]
            act.wait_ge(kstep, step_end(s))
            act.activation(midf[0:64, :], psum[0:64, step_banks(s)[0], :], ACT.Tanh).then_inc(step_a, 1)
            wait_step(act, s)
            act.activation(mid_hi[0:64, :], midf[0:64, :], ACT.Copy).then_inc(mid_h, 1)
            act.wait_ge(xlo_ready, xready(5, 7))
            for name, dst, vec in (("a2", af, "rw_a0"), ("w2", h_sb, "rw_w0")):
                for i in range(4):
                    s = PL.first[name] + i
                    act.wait_ge(kstep, step_end(s))
                    for m in range(2):
                        last = act.activation(dst[:, 2 * i + m, 0:S], bank(step_banks(s)[m]), ACT.Sigmoid,
                                              bias=pcol(vec, 2 * i + m))
                    last.then_inc(step_a, 1)
            wait_product(act, "w2")
            for k in range(KT):
                if k >= 2:
                    act.wait_ge(prep_pe, 2 * (k - 2) + 1)
                act.activation(tmp[:, k % 2, :], kf[:, k, :], ACT.Square, scale=pcol("rw_k_k", k)).then_inc(prep_a, 1)
                act.activation(u0[:, k, :], kf[:, k, :], ACT.Copy, scale=pcol("rw_k_k", k)).then_inc(prep_a, 1)
                act.wait_ge(prep_d, 6 * k + 1)
                if k >= 2:
                    act.wait_ge(prep_p, 2 * (k - 2) + 2)
                act.activation(pchunk[:, k, :], u1[:, k, CH - 1:S:CH], ACT.Exp, scale=-EXPW)
                act.activation(tmp[:, 4 + k % 2, :], u1[:, k, :], ACT.Exp, scale=-EXPW).then_inc(prep_a, 1)
                if k >= 2:
                    act.wait_ge(prep_d, 6 * (k - 2) + 6)
                act.activation(tmp[:, 6 + k % 2, :], u1[:, k, :], ACT.Exp, scale=EXPW).then_inc(prep_a, 1)
                act.wait_ge(prep_p, 2 * k + 1)
                act.activation(h_sb[:, k, 0:S], h_sb[:, k, 0:S], ACT.Exp, scale=-EXPW).then_inc(prep_a, 1)
            wait_done(act, ("ksq",))
            rn = xf[0:16, 1, :]
            act.activation(rn, psum[0:16, 4, :], ACT.Sqrt).then_inc(job_a, 1)
            act.wait_ge(kn_f, 1)
            act.activation(mid_hi[0:16, :], rn, ACT.Copy).then_inc(kn_h, 1)
            wait_done(act, ("bonus",))
            act.activation(rt[0:16, :], psum[0:16, 5, :], ACT.Copy).then_inc(job_a, 1)
            for tt in range(TT):
                for i in range(2):
                    if tt:
                        wait_done(act, ("SU", 2 * tt - 1, 1))
                    empty(("bt", tt, i), btok[:, S * i:S * i + S])
                for pair in range(2):
                    gs = (2 * pair, 2 * pair + 1)
                    for g in gs:
                        empty(("T1", tt, g), Tn[:, g % 2, :])
                    for g in gs:
                        key = ("AV", tt, g)
                        wait_done(act, key)
                        if tt:
                            wait_job(act, ("X", 2 * tt - 1, 1))
                        h0 = group_head(g, 0)
                        act.activation(AV[:, :].rearrange("p (h c) -> p h c", h=HEADS)[:, h0:h0 + 7:2, :],
                                       bank(job_banks(key)[0], 256).rearrange("p (h c) -> p h c", h=GROUPS),
                                       ACT.Copy).then_inc(job_a, 1)
                    for lv in range(1, NL):
                        for g in gs:
                            empty(("G", tt, g, lv), Gs[:, g % 2, :])
                for c in (2 * tt, 2 * tt + 1):
                    rb = slice(64 * (c % 2), 64 * (c % 2) + 64)
                    for hh in range(2):
                        key = ("U", c, hh)
                        wait_done(act, key)
                        act.activation(us[rb, S * hh:S * hh + S], psum[rb, job_banks(key)[0], :],
                                       ACT.Copy).then_inc(job_a, 1)
                    key = ("Y", c)
                    wait_done(act, key)
                    act.activation(h_sb[:, :, 1 + CH * c:1 + CH * c + CH],
                                   bank(job_banks(key)[0]).rearrange("p (k c) -> p k c", k=KT),
                                   ACT.Copy).then_inc(job_a, 1)
            act.activation(sg_hi[:, 0, :], sgf[:, 0, :], ACT.Copy)
            act.activation(sg_hi[96:128, 1, :], sgf[96:128, 1, :], ACT.Copy)
            act.activation(bon_hi[:, :], rt[0:16, :], ACT.Copy).then_inc(sg_h, 1)
            high(PL.first_slot["g2"])
            high(PL.first_slot["g2"] + 1)
            for k in range(KT):
                wait_job(act, ("gmean", k))
                if k >= 2:
                    act.wait_ge(gn_pe, k - 1)
                act.activation(pt8[:, k % 2, :], h_sb[:, k, 1:S + 1], ACT.Square).then_inc(gn_q, 1)
            wait_done(act, ("gvar",))
            act.activation(rn, psum[0:16, 5, :], ACT.Sqrt, bias=cst[0:16, C_EPSL:C_EPSL + 1],
                           scale=1.0 / HN).then_inc(job_a, 1)
            act.wait_ge(kn_f, 2)
            act.activation(gn_hi[:, :], rn, ACT.Copy).then_inc(kn_h, 1)
            for k in range(KT):
                wait_job(act, ("grstd", k))
                if k >= 2:
                    act.wait_ge(xf_ready, xf_count(XV["y"], k - 2))
                act.activation(pt8[:, 2 + k % 2, :], h_sb[:, k, 1:S + 1], ACT.Identity, bias=pcol("rw_lnx_b", k),
                               scale=pcol("rw_lnx_w", k)).then_inc(gn_aff, 1)
                empty(("bb", k), pt8[:, 4 + k % 2, :])
                if k >= 1:
                    x_high1(XV["y"], k - 1)
            x_high1(XV["y"], KT - 1)
            for i in range(4):
                if PL.first_slot["o"] + 1 + i < len(PL.slots):
                    high(PL.first_slot["o"] + 1 + i)
            norm_squares(1)
            x_high(XV["ffn0"])
            ffn(0)
            act.wait_ge(lam_row, 1)
            wait_done(act, ("lam",))
            act.activation(col[:, 0:2], psum[:, 7, 0:2], ACT.Exp).then_inc(job_a, 1)
            norm_squares(2)
            x_high(XV["kvin"])
            plain_last("kk", ak)
            plain_last("kv", av, XV["qin"], tokens=True)
            plain_last("q", aq)
            for n, (w, src) in enumerate((("k", ak), ("q", aq))):
                head_scale(src, KT, 8 * n, ("hsq", w), 1.0 / HN, C_EPS6, kn_f, 3 + n, n_hi)
            for i in range(-1, HEADS // 2 * TT):
                if i + 1 < HEADS // 2 * TT:
                    hd, tq = (i + 1) // TT, (i + 1) % TT
                    b = job_banks(("sc", i + 1))
                    act.wait_ge(sc_max, i + 2)
                    if i >= 1:
                        wait_done(act, ("pt", i - 1))
                    for sub in range(2):
                        q = 2 * ((i + 1) % 2) + sub
                        ins = act.activation(Pb[:, q, 0:P * (tq + 1)], psum[:, b[sub], 0:P * (tq + 1)], ACT.Exp,
                                             bias=col[:, 4 + q:5 + q], scale=HN ** -0.5,
                                             accum_out=col[:, 8 + q:9 + q])
                    ins.then_inc(job_a, 1)
                if i >= 0:
                    if i >= 1 and (i - 1) % TT == TT - 1:
                        empty(("ot", (i - 1) // TT), oT[:, (i - 1) // TT, :])
                    hd, tq = i // TT, i % TT
                    key = ("pt", i)
                    wait_done(act, key)
                    act.activation(PTs[:, i % 2, 0:P * (tq + 1)], bank(job_banks(key)[0], P * (tq + 1)),
                                   ACT.Copy).then_inc(job_a, 1)
            empty(("ot", HEADS // 2 - 1), oT[:, HEADS // 2 - 1, :])
            wait_job(act, ("ot", HEADS // 2 - 1))
            head_scale(oT, KT, 16, ("osq",), 1.0 / P, C_EPS5, kn_f, 5, n_hi)
            for k in range(KT):
                wait_job(act, ("oinv", k))
                x_high1(XV["attn"], k, oT)
            for i in range(PL.count["ao"]):
                next_slot(PL.first["ao"] + i)
            norm_squares(3)
            x_high(XV["ffn1"])
            ffn(1)
            wait_product(act, "dn1")
            x_high(XV["even"], x)
            plain_last("eq", eqk)
            plain_last("ek", eqk[:, 2:4, :])
            s = PL.first["elr"]
            next_slot(s)
            act.wait_ge(kstep, step_end(s))
            act.activation(elr[:, :], psum[0:16, step_banks(s)[0], :], ACT.Copy).then_inc(step_a, 1)
            plain_last("ev", ev, tokens=True)
            for m in range(2):
                key = ("za", m)
                wait_done(act, key)
                link(act.activation(gw[:, m, :], bank(job_banks(key)[0]), ACT.Abs, bias=pcol("l0_b_a_2", m)))
                link(act.activation(gw[:, m, :], gw[:, m, :], ACT.Exp, scale=-1.0))
                act.activation(gw[:, m, :], gw[:, m, :], ACT.Ln, bias=cst[:, CST["ones"]:CST["ones"] + 1]
                               ).then_inc(gl_a, 1)
            plain_last("ega", ega, func=ACT.Silu)
            for m in range(2):
                act.wait_ge(gl_d, m + 1)
                act.activation(gend[:, m, :], gcum[:, m, CH - 1:S:CH], ACT.Exp, scale=1.0 / 16)
                act.activation(gw[:, m, :], gcum[:, m, :], ACT.Exp, scale=1.0 / 16)
                act.activation(gw[:, 2 + m, :], gcum[:, m, :], ACT.Exp, scale=-1.0 / 16).then_inc(gl_a, 1)
            plain_last("esv", esv, func=ACT.Gelu_apprx_tanh)
            plain_last("eu", mix[:, 4:8, :], func=ACT.Gelu_apprx_tanh)
            plain_last("egb", egb, func=ACT.Silu)
            for tt in range(-1, TT):
                if tt + 1 < TT:
                    if tt >= 1:
                        wait_done(act, ("gu", 2 * (tt - 1) + 1))
                    key = ("gkt", tt + 1)
                    wait_done(act, key)
                    act.activation(kt2[:, (tt + 1) % 2, :], bank(job_banks(key)[0], 256), ACT.Copy).then_inc(job_a, 1)
                if tt >= 0:
                    for c in (2 * tt, 2 * tt + 1):
                        key = ("go", c)
                        wait_done(act, key)
                        act.activation(mix[:, 0:4, CH * c:CH * c + CH],
                                       bank(job_banks(key)[0], 256).rearrange("p (h c) -> p h c", h=4),
                                       ACT.Copy).then_inc(job_a, 1)
            wait_job(act, ("go", NCH - 1))
            head_scale(mix, 4, 24, ("gosq",), 1.0 / P, C_EPS5, kn_f, 6, en_hi)
            act.wait_ge(kn_l, 6)
            head_scale(esv, 4, 28, ("svar",), 1.0 / P, C_EPS5, kn_f, 7, en_hi,
                       before=lambda k: wait_job(act, ("smean", k)), free=("gorb", 3))
            for g in range(4):
                key = ("svT", g)
                if g >= 2:
                    wait_done(act, ("sg", g - 2))
                empty(key, svt[:, g % 2, :])
            for k in range(KT):
                if k < 4:
                    act.wait_ge(mix_a, k + 1)
                else:
                    wait_job(act, ("sg", k - 4))
                x_high1(XV["evenmix"], k, mix)
            layer_norm(0)
            for k in range(KT):
                act.wait_ge(ln_b, k + 1)
                x_high1(XV["odd"], k, x)
            odd_angles()
            plain_last("oq", oqk)
            plain_last("ok", oqk[:, 2:4, :])
            plain_last("ov", ov, tokens=True)
            plain_last("ogc", ogc, func=ACT.Silu)
            plain_last("op", opp[:, :, PAD:PAD + S])
            plain_last("ogd", ogd, func=ACT.Silu)
            for tt in range(TT):
                key = ("ro", tt)
                wait_done(act, key)
                act.activation(omix[:, 0:4, P * tt:P * tt + P],
                               bank(job_banks(key)[0]).rearrange("p (h c) -> p h c", h=4), ACT.Copy).then_inc(job_a, 1)
            head_scale(omix, 4, 32, ("rvar",), 1.0 / P, C_EPS5, kn_f, 8, on_hi,
                       before=lambda k: wait_job(act, ("rmean", k)))
            for k in range(KT):
                if k < 4:
                    act.wait_ge(omix_a, k + 1)
                else:
                    wait_job(act, ("pool", k - 4))
                x_high1(XV["oddmix"], k, omix)
            layer_norm(1)
            for tt in range(TT):
                for i in range(2):
                    empty(("out", tt, i), ost[:, tt, S * i:S * i + S])

        @block.vector
        def _(dve):
            seq = [0]

            def link(ins):
                seq[0] += 1
                ins.then_inc(dve_seq, 1)
                dve.wait_ge(dve_seq, seq[0])

            def x_low1(v, k, src=None):
                dve.wait_ge(xhi_ready, xready(v, k))
                f = src[:, k, :] if src is not None else xf[:, (8 * v + k) % 2, :]
                dve.tensor_tensor(X_lo[:, k, :], f, X_hi[:, k, :].bitcast(F32), ALU.subtract).then_inc(xlo_ready, 1)

            def split(v, produce):
                for k in range(KT):
                    if 8 * v + k >= 2:
                        dve.wait_ge(xlo_ready, 8 * v + k - 1)
                    produce(k, xf[:, (8 * v + k) % 2, :]).then_inc(xf_ready, 1)
                    if k:
                        x_low1(v, k - 1)
                x_low1(v, KT - 1)

            def norm_scale(i):
                wait_job(dve, ("rms", i))
                link(dve.reciprocal(rt[:, :], rt[:, :]))

            def normed(gain, i0):
                def produce(k, f):
                    return dve.scalar_tensor_tensor(out=f, in0=x[:, k, :], scalar=pcol(gain, i0 + k), in1=rt[:, :],
                                                    op0=ALU.mult, op1=ALU.mult)
                return produce

            def residual(name):
                for i in range(4):
                    s = PL.first[name] + i
                    dve.wait_ge(kstep, step_end(s))
                    for m in range(2):
                        last = dve.tensor_tensor(x[:, 2 * i + m, :], x[:, 2 * i + m, :], bank(step_banks(s)[m]),
                                                 ALU.add)
                    last.then_inc(step_d, 1)

            def ffn(layer):
                s0 = PL.first[f"gu{layer}"]
                with dve.Fori(0, FT // 2) as i:
                    for j in range(2):
                        dve.wait_ge(kstep, step_end(s0 + j) + 16 * i)
                        dve.wait_ge(ff_gate, FT * layer + j + 1 + 2 * i)
                        dve.tensor_tensor(xf[:, j, :], sgate[:, j, :], bank(step_banks(s0 + j)[1]),
                                          ALU.mult).then_inc(step_d, 1)
                        dve.wait_ge(ff_hi, FT * layer + j + 1 + 2 * i)
                        h1 = bass.ds(2 * i + j, 1)
                        dve.tensor_tensor(hb_lo[:, h1, :], xf[:, j:j + 1, :], hb_hi[:, h1, :].bitcast(F32),
                                          ALU.subtract).then_inc(ff_lo, 1)
                        dve.wait_ge(ff_lo, FT * layer + j + 1 + 2 * i)
                residual(f"dn{layer}")

            def new_state(old, new, key):
                b = bank(job_banks(key)[0]).rearrange("p (h c) -> p h c", h=4)
                for half in range(2):
                    own = c_("blk")[:, 64 * half:64 * half + 1]
                    if old is not None:
                        ins = dve.scalar_tensor_tensor(out=new[:, half:4:2, :], in0=b[:, half:4:2, :], scalar=own,
                                                       in1=old[:, half:4:2, :], op0=ALU.mult, op1=ALU.add)
                    else:
                        ins = dve.tensor_scalar(new[:, half:4:2, :], b[:, half:4:2, :], own, None, ALU.mult)
                ins.then_inc(job_d, 1)

            def layer_norm(n):
                name = ("eo", "oo")[n]
                for i in range(4):
                    s = PL.first[name] + i
                    dve.wait_ge(kstep, step_end(s))
                    for m in range(2):
                        ins = dve.scalar_tensor_tensor(out=x[:, 2 * i + m, :], in0=x[:, 2 * i + m, :], scalar=ALPHA,
                                                       in1=bank(step_banks(s)[m]), op0=ALU.mult, op1=ALU.add)
                    ins.then_inc(step_d, 1)
                wait_done(dve, ("lm", n))
                dve.tensor_scalar(rt[:, :], bank(job_banks(("lm", n))[0]), 1.0 / D, None, ALU.mult).then_inc(job_d, 1)
                wait_job(dve, ("lm", n))
                for k in range(KT):
                    dve.tensor_tensor(x[:, k, :], x[:, k, :], rt[:, :], ALU.subtract).then_inc(ln_c, 1)
                wait_job(dve, ("lv", n))
                link(dve.reciprocal(rt[:, :], rt[:, :]))
                for k in range(KT):
                    dve.scalar_tensor_tensor(out=x[:, k, :], in0=x[:, k, :], scalar=pcol(f"l{n}_ln_g_2", k),
                                             in1=rt[:, :], op0=ALU.mult, op1=ALU.mult).then_inc(ln_g, 1)

            def head_inverse(key, count, hi, lo):
                wait_job(dve, key)
                dve.reciprocal(rt[0:16, :], rt[0:16, :]).then_inc(kn_f, 1)
                dve.wait_ge(kn_h, count)
                dve.tensor_tensor(lo[:, :], rt[0:16, :], hi[:, :].bitcast(F32), ALU.subtract).then_inc(kn_l, 1)

            wait_job(dve, ("pv",))
            link(dve.tensor_scalar(omu[:, :], pv[:, PV["rw_mu"]:PV["rw_mu"] + 48], -1.0, 1.0, ALU.mult, ALU.add))
            dve.wait_ge(lam_in, 64)
            l4 = lamr[0:1, :].rearrange("p (a b c) -> p a b c", a=2, b=2)
            link(dve.tensor_tensor(lamp[0:1, :].rearrange("p (a c) -> p a c", a=2), l4[:, :, 0, :], l4[:, :, 1, :],
                                   ALU.mult))
            dve.tensor_reduce(col[0:1, 14:16], lamp[0:1, :].rearrange("p (a c) -> p a c", a=2), AX.X,
                              ALU.add).then_inc(lam_row, 1)
            wait_done(dve, ("xt", KT - 1))
            dve.wait_ge(lam_row, 1)
            dve.memset(h_sb[:, :, 0:1], 0.0)
            norm_scale(0)
            for k in range(KT):
                ins = dve.scalar_tensor_tensor(out=h_sb[:, k, 1:S + 1], in0=x[:, k, :], scalar=pcol("g_mix", k),
                                               in1=rt[:, :], op0=ALU.mult, op1=ALU.mult)
            link(ins)

            def mixed(mu):
                def produce(k, f):
                    link(dve.tensor_scalar(f, h_sb[:, k, 1:S + 1], omu[:, 8 * mu + k:8 * mu + k + 1], None, ALU.mult))
                    return dve.scalar_tensor_tensor(out=f, in0=h_sb[:, k, 0:S], scalar=pcol("rw_mu", 8 * mu + k),
                                                    in1=f, op0=ALU.mult, op1=ALU.add)
                return produce

            for v, mu in enumerate((MU_K, MU_V, MU_R, MU_G, MU_A, MU_W)):
                split(v, mixed(mu))
            for n, rows in ((1, slice(64, 128)), (2, slice(0, 64))):
                dve.wait_ge(mid_h, n)
                dve.tensor_tensor(mid_lo[rows, :], midf[rows, :], mid_hi[rows, :].bitcast(F32),
                                  ALU.subtract).then_inc(mid_l, 1)
            wait_product(dve, "w2")
            dve.wait_ge(keep_in, 16)
            for k in range(KT):
                dve.tensor_tensor_scan(u1[:, k, :], keep[:, :], h_sb[:, k, 0:S], 0.0, ALU.mult,
                                       ALU.add).then_inc(prep_d, 1)
                dve.tensor_scalar(xf[:, 0, :], af[:, k, :], -1.0, pcol("rw_k_a", k), ALU.add,
                                  ALU.mult).then_inc(prep_d, 1)
                dve.wait_ge(prep_d, 6 * k + 2)
                dve.wait_ge(prep_a, 5 * k + 2)
                dve.scalar_tensor_tensor(out=kf[:, k, :], in0=xf[:, 0, :], scalar=1.0, in1=kf[:, k, :], op0=ALU.add,
                                         op1=ALU.mult).then_inc(prep_d, 1)
                dve.wait_ge(prep_d, 6 * k + 3)
                if k >= 2:
                    dve.wait_ge(prep_pe, 2 * (k - 2) + 2)
                dve.scalar_tensor_tensor(out=tmp[:, 2 + k % 2, :], in0=rf[:, k, :], scalar=pcol("rw_r_k", k),
                                         in1=kf[:, k, :], op0=ALU.mult, op1=ALU.mult).then_inc(prep_d, 1)
                dve.wait_ge(prep_a, 5 * k + 4)
                dve.wait_ge(prep_d, 6 * k + 4)
                dve.tensor_tensor(kf[:, k, :], kf[:, k, :], tmp[:, 6 + k % 2, :], ALU.mult).then_inc(prep_d, 1)
                dve.tensor_tensor(af[:, k, :], af[:, k, :], tmp[:, 6 + k % 2, :], ALU.mult).then_inc(prep_d, 1)
            wait_job(dve, ("ksq",))
            rn = xf[0:16, 1, :]
            link(dve.tensor_scalar(rn, rn, 1e-12, None, ALU.max))
            dve.reciprocal(rn, rn).then_inc(kn_f, 1)
            dve.wait_ge(kn_h, 1)
            dve.tensor_tensor(mid_lo[0:16, :], rn, mid_hi[0:16, :].bitcast(F32), ALU.subtract).then_inc(kn_l, 1)
            dve.wait_ge(prep_a, 5 * KT)
            for k in range(KT):
                wait_done(dve, ("kinv", k))
                dve.tensor_tensor(u0[:, k, :], u0[:, k, :], bank(job_banks(("kinv", k))[0]), ALU.mult).then_inc(job_d, 1)
                wait_job(dve, ("kinv", k))
                link(dve.tensor_tensor(af[:, k, :], af[:, k, :], u0[:, k, :], ALU.mult))
                ins = dve.scalar_tensor_tensor(out=u0[:, k, :], in0=u0[:, k, :], scalar=-1.0, in1=h_sb[:, k, 0:S],
                                               op0=ALU.mult, op1=ALU.mult)
                ins.then_inc(at_ready, 1)
            dve.memset(us[:, :], 0.0)
            for i in range(2):
                ins = dve.memset(state[i][:, :, :], 0.0)
            ins.then_inc(zero_ready, 1)
            dve.wait_ge(lvl_in, 16)
            incl = c_("incl")[:, None, :].to_broadcast([P, GROUPS, P])
            strict = lvl[:, 0:1, :].to_broadcast([P, GROUPS, P])
            blk4 = c_("blk")[:, None, :].to_broadcast([P, 4, P])

            def four(ap):
                return ap.rearrange("p (h c) -> p h c", h=4)

            for tt in range(TT):
                for i in range(2):
                    key = ("kt", tt, i)
                    wait_done(dve, key)
                    if tt:
                        wait_done(dve, ("SU", 2 * tt - 1, 1))
                    dve.tensor_copy(ktok[:, S * i:S * i + S], bank(job_banks(key)[0])).then_inc(job_d, 1)
                for pair in range(2):
                    gs = (2 * pair, 2 * pair + 1)
                    for g in gs:
                        for m, dst, mask in (("At", At[:, g % 2, :], strict), ("Rb", Rb[:, g, :], incl),
                                             ("Ak", Ak[:, g % 2, :], strict), ("Rk", Rk[:, g, :], incl)):
                            key = (m, tt, g)
                            wait_done(dve, key)
                            if m == "At" and (tt or pair):
                                dve.wait_ge(level_ready, (NL - 1) * 2 * (2 * tt + pair))
                            if m in ("Rb", "Rk") and tt:
                                wait_done(dve, ("Y", 2 * tt - 1))
                            if m == "Ak" and (tt or pair):
                                wait_done(dve, ("AV", tt if pair else tt - 1, (g + 2) % 4))
                            dve.tensor_tensor(four(dst), four(bank(job_banks(key)[0])), mask, ALU.mult).then_inc(job_d, 1)
                    for lv in range(1, NL):
                        for g in gs:
                            if lv < NL - 1:
                                key = ("TG", tt, g, lv)
                                wait_done(dve, key)
                                dve.tensor_tensor(Tn[:, g % 2, :], Tn[:, g % 2, :], bank(job_banks(key)[0]),
                                                  ALU.add).then_inc(job_d, 1)
                            key = ("TGt", tt, g, lv)
                            wait_done(dve, key)
                            dve.tensor_tensor(Tt[:, g, :], Tt[:, g, :], bank(job_banks(key)[0]), ALU.add).then_inc(job_d, 1)
                for c in (2 * tt, 2 * tt + 1):
                    rb = slice(64 * (c % 2), 64 * (c % 2) + 64)
                    old, new = state[c % 2], state[(c + 1) % 2]
                    for hh in range(2):
                        key = ("X", c, hh)
                        wait_done(dve, key)
                        wait_job(dve, ("AV", tt, 3))
                        if c:
                            wait_done(dve, ("U", c - 1, hh))
                        dve.tensor_tensor(xs[rb, S * hh:S * hh + S], psum[rb, job_banks(key)[0], :],
                                          AV[rb, S * hh:S * hh + S], ALU.add).then_inc(job_d, 1)
                    for hh in range(2):
                        key = ("SU", c, hh)
                        wait_done(dve, key)
                        o4, n4 = old[:, 4 * hh:4 * hh + 4, :], new[:, 4 * hh:4 * hh + 4, :]
                        if c:
                            wait_done(dve, ("Y", c - 1))
                        dve.tensor_tensor(n4, four(bank(job_banks(key)[0])), blk4, ALU.mult).then_inc(job_d, 1)
                        wait_job(dve, key)
                        link(dve.tensor_tensor(n4, n4, o4, ALU.add))
                        dve.tensor_tensor(n4, n4, pchunk[:, 4 * hh:4 * hh + 4, c:c + 1].to_broadcast([P, 4, P]),
                                          ALU.mult).then_inc(s_new, 1)
            dve.wait_ge(sg_h, 1)
            dve.tensor_tensor(sg_lo[:, 0, :], sgf[:, 0, :], sg_hi[:, 0, :].bitcast(F32), ALU.subtract)
            dve.tensor_tensor(sg_lo[96:128, 1, :], sgf[96:128, 1, :], sg_hi[96:128, 1, :].bitcast(F32), ALU.subtract)
            dve.tensor_tensor(bon_lo[:, :], rt[0:16, :], bon_hi[:, :].bitcast(F32), ALU.subtract).then_inc(sg_l, 1)
            for k in range(KT):
                key = ("gmean", k)
                wait_done(dve, key)
                dve.tensor_tensor(h_sb[:, k, 1:S + 1], h_sb[:, k, 1:S + 1], bank(job_banks(key)[0]),
                                  ALU.subtract).then_inc(job_d, 1)
            wait_job(dve, ("gvar",))
            dve.reciprocal(rn, rn).then_inc(kn_f, 1)
            dve.wait_ge(kn_h, 2)
            dve.tensor_tensor(gn_lo[:, :], rn, gn_hi[:, :].bitcast(F32), ALU.subtract).then_inc(kn_l, 1)
            v = XV["y"]
            for k in range(KT):
                key = ("grstd", k)
                wait_done(dve, key)
                dve.tensor_tensor(h_sb[:, k, 1:S + 1], h_sb[:, k, 1:S + 1], bank(job_banks(key)[0]),
                                  ALU.mult).then_inc(job_d, 1)
                key = ("vT", k)
                wait_done(dve, key)
                wait_job(dve, ("bb", k))
                dve.tensor_tensor(pt8[:, 4 + k % 2, :], pt8[:, 4 + k % 2, :], bank(job_banks(key)[0]),
                                  ALU.mult).then_inc(job_d, 1)
                wait_job(dve, key)
                dve.wait_ge(gn_aff, k + 1)
                link(dve.tensor_tensor(pt8[:, 2 + k % 2, :], pt8[:, 2 + k % 2, :], pt8[:, 4 + k % 2, :], ALU.add))
                s = PL.first["g2"] + k // 2
                dve.wait_ge(kstep, step_end(s))
                if k >= 2:
                    dve.wait_ge(xlo_ready, xready(v, k - 2))
                ins = dve.tensor_tensor(xf[:, (8 * v + k) % 2, :], pt8[:, 2 + k % 2, :], bank(step_banks(s)[k % 2]),
                                        ALU.mult)
                ins.then_inc(xf_ready, 1)
                dve.wait_ge(xf_ready, xf_count(v, k))
                if k % 2:
                    dve.sem_inc(step_d, 1)
                if k:
                    x_low1(v, k - 1)
            x_low1(v, KT - 1)
            residual("o")
            norm_scale(1)
            split(XV["ffn0"], normed("g_ffn", 0))
            ffn(0)
            wait_job(dve, ("lam",))
            link(dve.tensor_tensor(col[:, 2:3], col[:, 1:2], col[:, 0:1], ALU.subtract))
            dve.tensor_scalar(col[:, 3:4], col[:, 2:3], -LAM_INIT, None, ALU.add)
            link(dve.tensor_scalar(col[:, 12:13], pcol("da_subln_g"), 1.0 - LAM_INIT, None, ALU.mult))
            norm_scale(2)
            split(XV["kvin"], normed("kv_g", 0))
            split(XV["qin"], normed("g_mix", 8))
            dve.wait_ge(rope_in, 16)
            for n, (w, src, g) in enumerate((("k", ak, "k_norm_g"), ("q", aq, "da_q_norm_g"))):
                head_inverse(("hsq", w), 3 + n, n_hi, n_lo)

                def rotate(k):
                    key = ("rot", w, k)
                    link(dve.tensor_tensor(tq2[:, 0, :], src[:, k, :], rope[:, 0, :], ALU.mult))
                    wait_done(dve, key)
                    dve.tensor_tensor(tq2[:, 1, :], bank(job_banks(key)[0]), rope[:, 1, :], ALU.mult).then_inc(job_d, 1)
                    wait_job(dve, key)
                    dve.tensor_tensor(src[:, k, :], tq2[:, 0, :], tq2[:, 1, :], ALU.add).then_inc(hn_rot, 1)
                    dve.wait_ge(hn_rot, 8 * n + k + 1)

                for k in range(KT):
                    key = ("hinv", w, k)
                    wait_done(dve, key)
                    dve.scalar_tensor_tensor(out=src[:, k, :], in0=src[:, k, :], scalar=pcol(g),
                                             in1=bank(job_banks(key)[0]), op0=ALU.mult,
                                             op1=ALU.mult).then_inc(job_d, 1)
                    if k:
                        wait_job(dve, ("hinv", w, k - 1))
                        rotate(k - 1)
                wait_job(dve, ("hinv", w, KT - 1))
                rotate(KT - 1)
            n_i = HEADS // 2 * TT
            for i in range(-1, n_i):
                if i + 1 < n_i:
                    b = job_banks(("sc", i + 1))[0]
                    N = P * ((i + 1) % TT + 1)
                    q = 4 + 2 * ((i + 1) % 2)
                    wait_done(dve, ("sc", i + 1))
                    link(dve.memset(psum[0:64, b:b + 2, N - CH:N], -1e30))
                    link(dve.tensor_reduce(col[:, 14:16], psum[:, b:b + 2, 0:N], AX.X, ALU.max))
                    dve.tensor_scalar(col[:, q:q + 2], col[:, 14:16], -(HN ** -0.5), None,
                                      ALU.mult).then_inc(sc_max, 1)
                    dve.wait_ge(sc_max, i + 2)
                if i >= 0:
                    N = P * (i % TT + 1)
                    q = 2 * (i % 2)
                    wait_job(dve, ("sc", i))
                    link(dve.reciprocal(col[:, 8 + q:10 + q], col[:, 8 + q:10 + q]))
                    dve.tensor_scalar(Pb[:, q, 0:N], Pb[:, q, 0:N], col[:, 8 + q:9 + q], None, ALU.mult)
                    link(dve.tensor_tensor(col[:, 9 + q:10 + q], col[:, 9 + q:10 + q], col[:, 3:4], ALU.mult))
                    dve.scalar_tensor_tensor(out=Pb[:, q, 0:N], in0=Pb[:, q + 1, 0:N],
                                             scalar=col[:, 9 + q:10 + q], in1=Pb[:, q, 0:N], op0=ALU.mult,
                                             op1=ALU.add).then_inc(pc_ready, 1)
            head_inverse(("osq",), 5, n_hi, n_lo)
            for k in range(KT):
                key = ("oinv", k)
                wait_done(dve, key)
                dve.scalar_tensor_tensor(out=oT[:, k, :], in0=oT[:, k, :], scalar=col[:, 12:13],
                                         in1=bank(job_banks(key)[0]), op0=ALU.mult, op1=ALU.mult).then_inc(job_d, 1)
                if k:
                    x_low1(XV["attn"], k - 1, oT)
            x_low1(XV["attn"], KT - 1, oT)
            residual("ao")
            norm_scale(3)
            split(XV["ffn1"], normed("g_ffn", 8))
            ffn(1)
            for k in range(KT):
                x_low1(XV["even"], k, x)
            dve.wait_ge(small_in, 64)
            for m in range(2):
                key = ("za", m)
                wait_done(dve, key)
                dve.wait_ge(gl_a, m + 1)
                dve.tensor_scalar(gw[:, 2 + m, :], bank(job_banks(key)[0]), pcol("l0_b_a_2", m), 0.0, ALU.add,
                                  ALU.min).then_inc(job_d, 1)
                wait_job(dve, key)
                link(dve.tensor_tensor(gw[:, 2 + m, :], gw[:, 2 + m, :], gw[:, m, :], ALU.subtract))
                dve.tensor_tensor_scan(gcum[:, m, :], keep_e[:, :], gw[:, 2 + m, :], 0.0, ALU.mult,
                                       ALU.add).then_inc(gl_d, 1)
            wait_product(dve, "ek")
            for m in range(2):
                dve.wait_ge(gl_a, 3 + m)
                dve.scalar_tensor_tensor(out=eqk[:, m, :], in0=eqk[:, m, :], scalar=HN ** -0.5,
                                         in1=gw[:, m, :], op0=ALU.mult, op1=ALU.mult)
                dve.tensor_tensor(eqk[:, 2 + m, :], eqk[:, 2 + m, :], gw[:, 2 + m, :], ALU.mult).then_inc(gl_d, 1)
            dve.wait_ge(kstep, step_end(PL.first["egb"] + 1))
            dve.memset(est[0][:, :, :], 0.0).then_inc(g_state, 1)
            wait_done(dve, ("wsT",))
            dve.tensor_tensor(wsT[:, :, :], bank(job_banks(("wsT",))[0]).rearrange("p (g c) -> p g c", g=4),
                              c_("causal")[:, None, :].to_broadcast([P, 4, P]), ALU.mult).then_inc(job_d, 1)
            for tt in range(-1, TT):
                if tt + 1 < TT:
                    key = ("gs", tt + 1)
                    wait_done(dve, key)
                    if tt >= 1:
                        wait_done(dve, ("go", 2 * (tt - 1) + 1))
                    for half in range(2):
                        ins = dve.tensor_tensor(
                            sT[:, (tt + 1) % 2, 256 * half:256 * half + 256].rearrange("p (h c) -> p h c", h=2),
                            bank(job_banks(key)[half], 256).rearrange("p (h c) -> p h c", h=2),
                            c_("incl")[:, None, :].to_broadcast([P, 2, P]), ALU.mult)
                    ins.then_inc(job_d, 1)
                if tt >= 0:
                    for c in (2 * tt, 2 * tt + 1):
                        key = ("gu", c)
                        wait_done(dve, key)
                        if c:
                            wait_done(dve, ("go", c - 1))
                            dve.wait_ge(g_state, c + 1)
                        else:
                            dve.wait_ge(g_state, 1)
                        old, new = est[c % 2], est[(c + 1) % 2]
                        new_state(old, new, key)
                        wait_job(dve, key)
                        for half in range(2):
                            ins = dve.tensor_tensor(new[:, half:4:2, :], new[:, half:4:2, :],
                                                    gend[:, :, c:c + 1].to_broadcast([P, 2, P]), ALU.mult)
                        ins.then_inc(g_state, 1)
            for g in range(4):
                key = ("smean", g)
                wait_done(dve, key)
                dve.tensor_tensor(esv[:, g, :], esv[:, g, :], bank(job_banks(key)[0]), ALU.subtract).then_inc(job_d, 1)
            head_inverse(("gosq",), 6, en_hi, en_lo)
            for g in range(4):
                key = ("gorb", g)
                wait_done(dve, key)
                dve.scalar_tensor_tensor(out=mix[:, g, :], in0=mix[:, g, :], scalar=pcol("l0_gla_norm_g_2", g),
                                         in1=bank(job_banks(key)[0]), op0=ALU.mult, op1=ALU.mult).then_inc(job_d, 1)
                wait_job(dve, key)
                dve.tensor_tensor(mix[:, g, :], mix[:, g, :], ega[:, g, :], ALU.mult).then_inc(mix_a, 1)
            head_inverse(("svar",), 7, en_hi, en_lo)
            for g in range(4):
                key = ("srb", g)
                wait_done(dve, key)
                dve.scalar_tensor_tensor(out=esv[:, g, :], in0=esv[:, g, :], scalar=pcol("l0_sgu_ln_g_2", g),
                                         in1=bank(job_banks(key)[0]), op0=ALU.mult, op1=ALU.mult).then_inc(job_d, 1)
                wait_job(dve, key)
                dve.tensor_scalar(esv[:, g, :], esv[:, g, :], pcol("l0_sgu_ln_b_2", g), None,
                                  ALU.add).then_inc(sv_ready, 1)
            dve.wait_ge(gate_p, 4)
            for g in range(4):
                key = ("sg", g)
                wait_done(dve, key)
                dve.tensor_tensor(mix[:, 4 + g, :], mix[:, 4 + g, :], bank(job_banks(key)[0]),
                                  ALU.mult).then_inc(job_d, 1)
            for k in range(KT):
                x_low1(XV["evenmix"], k, mix)
            layer_norm(0)
            for k in range(KT):
                x_low1(XV["odd"], k, x)
            dve.wait_ge(pos_in, 16)
            link(dve.tensor_copy(orw[:, 0, :], posi[:, :]))
            link(dve.tensor_scalar(orw[:, 0, :], orw[:, 0, :], cst[:, C_INVF:C_INVF + 1], None, ALU.mult))
            link(dve.tensor_scalar(orw[:, 1, :], orw[:, 0, :], 1.0 / (2.0 * np.pi), None, ALU.mult))
            link(dve.tensor_scalar(orw[:, 1, :], orw[:, 1, :], ROUND, None, ALU.add))
            link(dve.tensor_scalar(orw[:, 1, :], orw[:, 1, :], -ROUND, None, ALU.add))
            for part in TWO_PI:
                link(dve.scalar_tensor_tensor(out=orw[:, 0, :], in0=orw[:, 1, :], scalar=-part, in1=orw[:, 0, :],
                                              op0=ALU.mult, op1=ALU.add))
            dve.tensor_scalar(orw[:, 0, :], orw[:, 0, :], 3.1415925, -3.1415925, ALU.min, ALU.max).then_inc(ang_d, 1)
            dve.wait_ge(ang_a, 1)
            link(dve.tensor_tensor(csn[:, 0, :], csn[:, 0, :], csn[:, 0, :], ALU.mult))
            link(dve.tensor_scalar(csn[:, 0, :], csn[:, 0, :], -2.0, 1.0, ALU.mult, ALU.add))
            wait_product(dve, "ok")
            dve.wait_ge(odd_in, 32)
            for i in range(4):
                key = ("rt", i)
                wait_done(dve, key)
                dve.tensor_tensor(orw[:, 1, :], bank(job_banks(key)[0]), csn[:, 1, :], ALU.mult).then_inc(job_d, 1)
                link(dve.tensor_tensor(orw[:, 0, :], oqk[:, i, :], csn[:, 0, :], ALU.mult))
                ins = dve.tensor_tensor(oqk[:, i, :], orw[:, 0, :], orw[:, 1, :], ALU.add)
                if i < 2:
                    link(ins)
                    ins = dve.tensor_tensor(oqi[:, i, :], oqk[:, i, :], cret[:, 4 * P + S * i:4 * P + S * i + S],
                                            ALU.mult)
                ins.then_inc(rot_done, 1)
                dve.wait_ge(rot_done, i + 1)
            wait_product(dve, "ogd")
            for g, w in enumerate(POOL_WINDOWS):
                dve.wait_ge(win_p, g + 1)
                src = psh[:, g % 2, PAD:PAD + S]
                dve.scalar_tensor_tensor(out=omix[:, 4 + g, 16:S], in0=src[:, 16:S], scalar=1.0 / w,
                                         in1=opp[:, g, PAD + 16:PAD + S], op0=ALU.mult, op1=ALU.subtract)
                link(dve.tensor_tensor(pool16[:, :], src[:, 0:16], cst[:, C_CNT + 16 * g:C_CNT + 16 * g + 16],
                                       ALU.mult))
                dve.tensor_tensor(omix[:, 4 + g, 0:16], pool16[:, :], opp[:, g, PAD:PAD + 16],
                                  ALU.subtract).then_inc(win_d, 1)
                key = ("pool", g)
                wait_done(dve, key)
                dve.scalar_tensor_tensor(out=omix[:, 4 + g, :], in0=bank(job_banks(key)[0]),
                                         scalar=pcol("l1_pool_scale_2", g), in1=ogd[:, g, :], op0=ALU.mult,
                                         op1=ALU.mult).then_inc(job_d, 1)
            dve.wait_ge(kstep, step_end(PL.first["ogd"] + 1))
            dve.memset(est[0][:, :, :], 0.0).then_inc(r_state, 1)
            for tt in range(-1, TT):
                if tt + 1 < TT:
                    key = ("rkt", tt + 1)
                    wait_done(dve, key)
                    if tt >= 1:
                        wait_done(dve, ("ro", tt - 1))
                    dve.tensor_tensor(kt2[:, (tt + 1) % 2, :].rearrange("p (h c) -> p h c", h=4),
                                      bank(job_banks(key)[0], 256).rearrange("p (h c) -> p h c", h=4),
                                      cst[:, C_WST:C_WST + 4][:, :, None].to_broadcast([P, 4, HN]),
                                      ALU.mult).then_inc(job_d, 1)
                    key = ("rs", tt + 1)
                    wait_done(dve, key)
                    for half in range(2):
                        q = slice(256 * half, 256 * half + 256)
                        ins = dve.tensor_tensor(sT[:, (tt + 1) % 2, q], bank(job_banks(key)[half], 256), cret[:, q],
                                                ALU.mult)
                    ins.then_inc(job_d, 1)
                if tt >= 0:
                    key = ("ru", tt)
                    wait_done(dve, key)
                    dve.wait_ge(r_state, tt + 1)
                    if tt:
                        wait_done(dve, ("ro", tt - 1))
                    old, new = est[tt % 2], est[(tt + 1) % 2]
                    new_state(None, new, key)
                    wait_job(dve, key)
                    for h in range(4):
                        ins = dve.scalar_tensor_tensor(out=new[:, h, :], in0=old[:, h, :], scalar=GAMMA_CHUNK[h],
                                                       in1=new[:, h, :], op0=ALU.mult, op1=ALU.add)
                    ins.then_inc(r_state, 1)
            for h in range(4):
                key = ("rmean", h)
                wait_done(dve, key)
                dve.tensor_tensor(omix[:, h, :], omix[:, h, :], bank(job_banks(key)[0]), ALU.subtract).then_inc(job_d, 1)
            head_inverse(("rvar",), 8, on_hi, on_lo)
            for h in range(4):
                key = ("rrb", h)
                wait_done(dve, key)
                dve.scalar_tensor_tensor(out=omix[:, h, :], in0=omix[:, h, :], scalar=pcol("l1_ret_norm_g_2", h),
                                         in1=bank(job_banks(key)[0]), op0=ALU.mult, op1=ALU.mult).then_inc(job_d, 1)
                wait_job(dve, key)
                dve.tensor_tensor(omix[:, h, :], omix[:, h, :], ogc[:, h, :], ALU.mult).then_inc(omix_a, 1)
            for k in range(KT):
                x_low1(XV["oddmix"], k, omix)
            layer_norm(1)

        @block.tensor
        def _(pe):
            order = [0]

            def begin(key):
                assert JB.order[order[0]] == key, (JB.order[order[0]], key)
                order[0] += 1
                wait_banks(pe, key)
                return job_banks(key)[0]

            def three(ps, w, xx, start, stop):
                (wh, wl), (xh, xl) = w, xx
                pe.matmul(ps, wh, xh, start=start, stop=False, skip_group_check=True)
                pe.matmul(ps, wh, xl, start=False, stop=False, skip_group_check=True)
                return pe.matmul(ps, wl, xh, start=False, stop=stop, skip_group_check=True)

            def two(ps, w, xx):
                pe.matmul(ps, w, xx[0], start=True, stop=False, skip_group_check=True)
                return pe.matmul(ps, w, xx[1], start=False, stop=True, skip_group_check=True)

            def features(s, v=None, xh=None, xl=None, m_count=2, cols=None, dyn=0, check=True,
                         tile_ready=None):
                name, at, n_slots, ks = PL.steps[s]
                if check:
                    wait_banks(pe, ("step", s))
                xh, xl = (X_hi, X_lo) if xh is None else (xh, xl)
                b = step_banks(s)
                for k in range(ks):
                    n = at + k // 8
                    if k % 8 == 0:
                        pe.wait_ge(lo_ready, n + 1 + dyn)
                    if tile_ready is not None:
                        pe.wait_ge(tile_ready[0], tile_ready[1] + k + 1)
                    if v is not None:
                        pe.wait_ge(xlo_ready, xready(v, k))
                    whi, wlo = wv(w_hi[n % 2]), wv(w_lo[n % 2])
                    for m in range(m_count):
                        c = slice(128 * m, 128 * m + 128) if cols is None else cols[m]
                        last = three(bank(b[m]), (whi[:, k % 8, c], wlo[:, k % 8, c]), (xh[:, k, :], xl[:, k, :]),
                                     k == 0, k == ks - 1)
                    last.then_inc(kstep, 1)

            def ffn(layer):
                s0, v = PL.first[f"gu{layer}"], XV[f"ffn{layer}"]
                with pe.Fori(0, FT // 2) as i:
                    for j in range(2):
                        pe.wait_ge(step_d, PL.taken[s0 + j][1] - 2 + 2 * i)
                        features(s0 + j, v if j == 0 else None, dyn=2 * i, check=False)
                s0 = PL.first[f"dn{layer}"]
                with pe.Fori(0, 2) as i:
                    for j in range(2):
                        pe.wait_ge(step_d, PL.taken[s0 + j][1] - 2 + 2 * i)
                        features(s0 + j, None, hb_hi, hb_lo, dyn=6 * i, check=False,
                                 tile_ready=(ff_lo, FT * layer) if j == 0 else None)

            def tokens(s, v=None):
                name, at, n_slots, ks = PL.steps[s]
                wait_banks(pe, ("step", s))
                b = step_banks(s)
                pe.wait_ge(lo_ready, at + 1)
                whi, wlo = wv(w_hi[at % 2]), wv(w_lo[at % 2])
                for k in range(ks):
                    if v is not None:
                        pe.wait_ge(xlo_ready, xready(v, k))
                    for m in range(2):
                        for r in range(2):
                            tk = slice(P * (2 * m + r), P * (2 * m + r) + P)
                            last = three(psum[:, b[m], 256 * r:256 * r + 256], (X_hi[:, k, tk], X_lo[:, k, tk]),
                                         (whi[:, k, :], wlo[:, k, :]), k == 0 and r == 0, k == ks - 1)
                    last.then_inc(kstep, 1)

            def product(name, v, kind=None):
                for i in range(PL.count[name]):
                    (kind or features)(PL.first[name] + i, v if i == 0 else None)

            def norm_sum(i):
                begin(("rms", i))
                for k in range(KT):
                    pe.wait_ge(sq_ready, 8 * i + k + 1)
                    ins = pe.matmul(bank(6), c_("ones"), xf[:, k % 2, :], start=k == 0, stop=k == KT - 1)
                    ins.then_inc(sq_used if k < KT - 1 else job_done, 1)

            def head_sum(key, n, at, sel):
                b = begin(key)
                for k in range(n):
                    pe.wait_ge(hn_a, at + k + 1)
                    pe.matmul(psum[0:16, b, :], c_(sel, 16, 16 * k), xf[:, k % 2, :], start=k == 0,
                              stop=k == n - 1).then_inc(hn_pe if k < n - 1 else job_done, 1)

            pe.wait_ge(cst_in, 16)
            pe.wait_ge(rows_in, 16 * (len(ROWS_A) + len(ROWS_B) + 2))
            b = begin(("pv",))
            pe.transpose(psum[:, b, 0:P], prow[0][:, :], c_("ident"))
            pe.transpose(psum[:, b, P:P + NROWS_B], prow[1][:, :], cst[0:NROWS_B, CST["ident"]:CST["ident"] + NROWS_B]
                         ).then_inc(job_done, 1)
            pe.wait_ge(x_in, 32)
            for k in range(KT):
                b = begin(("xt", k))
                for tt in range(TT):
                    ins = pe.transpose(psum[:, b, P * tt:P * tt + P], xtok[:, tt, P * k:P * k + P], c_("ident"))
                ins.then_inc(job_done, 1)
            norm_sum(0)
            product("k", 0)
            product("v", 1, tokens)
            product("r", 2)
            features(PL.first["g1"], 3, cols=(slice(0, 128), slice(32, 160)))
            features(PL.first["a1"], 4, m_count=1)
            features(PL.first["w1"], 5, m_count=1)
            for name, rows, n in (("a2", slice(64, 128), 1), ("w2", slice(0, 64), 2)):
                for i in range(4):
                    s = PL.first[name] + i
                    wait_banks(pe, ("step", s))
                    at = PL.steps[s][1]
                    if i == 0:
                        pe.wait_ge(lo_ready, at + 1)
                        pe.wait_ge(mid_l, n)
                    for m in range(2):
                        c = slice(P * (2 * i + m), P * (2 * i + m) + P)
                        ins = three(bank(step_banks(s)[m]), (w_hi[at % 2][rows, c], w_lo[at % 2][rows, c]),
                                    (mid_hi[rows, :], mid_lo[rows, :]), True, True)
                    ins.then_inc(kstep, 1)
            wait_banks(pe, ("ksq",))
            wait_banks(pe, ("bonus",))
            for k in range(KT):
                sel = c_("sel64", 16, 16 * k)
                pe.wait_ge(prep_a, 5 * k + 1)
                ins = pe.matmul(psum[0:16, 4, :], sel, tmp[:, k % 2, :], start=k == 0, stop=k == KT - 1)
                ins.then_inc(prep_pe if k < KT - 1 else job_done, 1)
                pe.wait_ge(prep_d, 6 * k + 4)
                ins = pe.matmul(psum[0:16, 5, :], sel, tmp[:, 2 + k % 2, :], start=k == 0, stop=k == KT - 1)
                ins.then_inc(prep_pe if k < KT - 1 else job_done, 1)
            order[0] += 2
            pe.wait_ge(heads_ready, 1)
            pe.wait_ge(kn_l, 1)
            for k in range(KT):
                b = begin(("kinv", k))
                two(bank(b), heads_r[:, P * k:P * k + P], (mid_hi[0:16, :], mid_lo[0:16, :])).then_inc(job_done, 1)
            pe.wait_ge(at_ready, KT)
            pe.wait_ge(prep_p, 2 * KT)
            pe.wait_ge(zero_ready, 1)
            n_t = 0
            n_lv = 0
            for tt in range(TT):
                tk = slice(P * tt, P * tt + P)
                for name, src in (("bt", af), ("kt", kf)):
                    for i in range(2):
                        b = begin((name, tt, i))
                        for j in range(4):
                            ins = pe.transpose(psum[:, b, P * j:P * j + P], src[:, 4 * i + j, tk], c_("ident"))
                        ins.then_inc(job_done, 1)
                for pair in range(2):
                    gs = (2 * pair, 2 * pair + 1)
                    for g in gs:
                        for m, left, right in (("At", af, u0), ("Rb", af, rf), ("Ak", kf, u0), ("Rk", kf, rf)):
                            b = begin((m, tt, g))
                            for j in range(4):
                                hd = group_head(g, j)
                                rows = slice(64 * (hd % 2), 64 * (hd % 2) + 64)
                                ins = pe.matmul(psum[:, b, P * j:P * j + P], left[rows, hd // 2, tk],
                                                right[rows, hd // 2, tk], start=True, stop=True,
                                                skip_group_check=True)
                            ins.then_inc(job_done, 1)
                    for g in gs:
                        n_t += 1
                        pe.wait_ge(t_init, n_t)
                        b = begin(("T1", tt, g))
                        for j in range(4):
                            ins = pe.transpose(psum[:, b, P * j:P * j + P], Tt[:, g, P * j:P * j + P], c_("ident"))
                        ins.then_inc(job_done, 1)
                    for g in gs:
                        b = begin(("AV", tt, g))
                        wait_job(pe, ("Ak", tt, g))
                        for j in range(4):
                            hd = group_head(g, j)
                            ins = pe.matmul(psum[:, b, HN * j:HN * j + HN], Ak[:, g % 2, P * j:P * j + P],
                                            vt[:, tt, HN * hd:HN * hd + HN], start=True, stop=True)
                        ins.then_inc(job_done, 1)
                    for lv in range(1, NL):
                        for g in gs:
                            n_lv += 1
                            pe.wait_ge(level_ready, n_lv)
                            wait_job(pe, ("T1", tt, g) if lv == 1 else ("TG", tt, g, lv - 1))
                            b = begin(("G", tt, g, lv))
                            for j in range(4):
                                c = slice(P * j, P * j + P)
                                ins = pe.matmul(psum[:, b, c], Lm[:, g % 2, c], Tn[:, g % 2, c], start=True, stop=True)
                            ins.then_inc(job_done, 1)
                        for g in gs:
                            wait_job(pe, ("G", tt, g, lv))
                            if lv > 1:
                                wait_job(pe, ("TGt", tt, g, lv - 1))
                            if lv < NL - 1:
                                b = begin(("TG", tt, g, lv))
                                for j in range(4):
                                    c = slice(P * j, P * j + P)
                                    ins = pe.matmul(psum[:, b, c], Tt[:, g, c], Gs[:, g % 2, c], start=True, stop=True)
                                ins.then_inc(job_done, 1)
                            b = begin(("TGt", tt, g, lv))
                            for j in range(4):
                                c = slice(P * j, P * j + P)
                                ins = pe.matmul(psum[:, b, c], Gs[:, g % 2, c], Tt[:, g, c], start=True, stop=True)
                            ins.then_inc(job_done, 1)
                for c in (2 * tt, 2 * tt + 1):
                    r0 = 64 * (c % 2)
                    rb = slice(r0, r0 + 64)
                    ck = slice(CH * c, CH * c + CH)
                    old = state[c % 2]
                    for hh in range(2):
                        if c:
                            pe.wait_ge(s_new, 2 * (c - 1) + hh + 1)
                        b = begin(("X", c, hh))
                        for j in range(4):
                            ins = pe.matmul(psum[rb, b, P * j:P * j + P], u0[:, 4 * hh + j, ck], old[:, 4 * hh + j, :],
                                            start=True, stop=True)
                        ins.then_inc(job_done, 1)
                    for hh in range(2):
                        wait_job(pe, ("X", c, hh))
                        if c % 2 == 0:
                            wait_job(pe, ("TGt", tt, 3, NL - 1))
                        b = begin(("U", c, hh))
                        for j in range(8):
                            hd = 8 * hh + j
                            g, i = head_group(hd)
                            ins = pe.matmul(psum[rb, b, HN * j:HN * j + HN], Tt[rb, g, P * i + r0:P * i + r0 + 64],
                                            xs[rb, HN * hd:HN * hd + HN], start=True, stop=True)
                        ins.then_inc(job_done, 1)
                    for hh in range(2):
                        wait_job(pe, ("U", c, hh))
                        b = begin(("SU", c, hh))
                        for j in range(4):
                            q = slice(P * (4 * hh + j), P * (4 * hh + j) + P)
                            pe.matmul(psum[:, b, P * j:P * j + P], btok[rb, q], us[rb, q], start=True, stop=False,
                                      skip_group_check=True)
                            ins = pe.matmul(psum[:, b, P * j:P * j + P], ktok[rb, q], vt[rb, tt, q], start=False,
                                            stop=True, skip_group_check=True)
                        ins.then_inc(job_done, 1)
                    b = begin(("Y", c))
                    for pr in range(KT):
                        o = slice(CH * pr, CH * pr + CH)
                        pe.matmul(psum[:, b, o], old[:, pr, :], rf[:, pr, ck], start=True, stop=False,
                                  skip_group_check=True)
                        for m, left in ((Rb, us), (Rk, vt[:, tt, :])):
                            for half in range(2):
                                hd = 2 * pr + half
                                g, i = head_group(hd)
                                ins = pe.matmul(psum[64 * half:64 * half + 64, b, o], left[:, HN * hd:HN * hd + HN],
                                                m[:, g, P * i + r0:P * i + r0 + 64],
                                                start=False, stop=m is Rk, skip_group_check=True)
                    ins.then_inc(job_done, 1)
            def gvar(k):
                if k == 0:
                    wait_banks(pe, ("gvar",))
                pe.wait_ge(gn_q, k + 1)
                pe.matmul(psum[0:16, 5, :], c_("sel64", 16, 16 * k), pt8[:, k % 2, :], start=k == 0,
                          stop=k == KT - 1).then_inc(gn_pe if k < KT - 1 else job_done, 1)

            wait_job(pe, ("Y", NCH - 1))
            for k in range(KT):
                b = begin(("gmean", k))
                pe.matmul(bank(b), c_("blkmean"), h_sb[:, k, 1:S + 1], start=True, stop=True).then_inc(job_done, 1)
                if k:
                    gvar(k - 1)
            gvar(KT - 1)
            order[0] += 1
            pe.wait_ge(kn_l, 2)
            pe.wait_ge(sg_l, 1)
            for k in range(KT):
                b = begin(("grstd", k))
                two(bank(b), heads_r[:, P * k:P * k + P], (gn_hi[:, :], gn_lo[:, :])).then_inc(job_done, 1)
                b = begin(("vT", k))
                for tt in range(TT):
                    ins = pe.transpose(psum[:, b, P * tt:P * tt + P], vt[:, tt, P * k:P * k + P], c_("ident"))
                ins.then_inc(job_done, 1)
                b = begin(("bb", k))
                two(bank(b), heads_r[:, P * k:P * k + P], (bon_hi[:, :], bon_lo[:, :])).then_inc(job_done, 1)
                if k % 2 == 0:
                    s = PL.first["g2"] + k // 2
                    wait_banks(pe, ("step", s))
                    at = PL.steps[s][1]
                    pe.wait_ge(lo_ready, at + 1)
                    for m in range(2):
                        c = slice(P * (k + m), P * (k + m) + P)
                        c2 = slice(1024 + P * (k + m), 1024 + P * (k + m) + P)
                        three(bank(step_banks(s)[m]), (w_hi[at % 2][:, c], w_lo[at % 2][:, c]),
                              (sg_hi[:, 0, :], sg_lo[:, 0, :]), True, False)
                        ins = three(bank(step_banks(s)[m]), (w_hi[at % 2][96:128, c2], w_lo[at % 2][96:128, c2]),
                                    (sg_hi[96:128, 1, :], sg_lo[96:128, 1, :]), False, True)
                    ins.then_inc(kstep, 1)
            product("o", XV["y"])
            norm_sum(1)
            ffn(0)
            pe.wait_ge(lam_row, 1)
            b = begin(("lam",))
            pe.matmul(psum[:, b, 0:2], cst[0:1, CST["ones"]:CST["ones"] + P], col[0:1, 14:16], start=True,
                      stop=True).then_inc(job_done, 1)
            norm_sum(2)
            product("kk", XV["kvin"])
            product("kv", None, tokens)
            product("q", XV["qin"])
            for n, (w, src) in enumerate((("k", ak), ("q", aq))):
                if n == 0:
                    wait_product(pe, "q")
                head_sum(("hsq", w), KT, 8 * n, "sel64")
                pe.wait_ge(kn_l, 3 + n)
                for k in range(KT + 1):
                    if k < KT:
                        b = begin(("hinv", w, k))
                        two(bank(b), heads_r[:, P * k:P * k + P], (n_hi[:, :], n_lo[:, :])).then_inc(job_done, 1)
                    if k:
                        wait_job(pe, ("hinv", w, k - 1))
                        b = begin(("rot", w, k - 1))
                        pe.matmul(bank(b), c_("rot1"), src[:, k - 1, :], start=True, stop=True).then_inc(job_done, 1)
            pe.wait_ge(hn_rot, 16)
            n_i = HEADS // 2 * TT

            def scores(i):
                hd, tq = i // TT, i % TT
                b = begin(("sc", i))
                for sub in range(2):
                    rows = slice(64 * sub, 64 * sub + 64)
                    ins = pe.matmul(psum[:, b + sub, 0:P * (tq + 1)], aq[rows, hd, P * tq:P * tq + P],
                                    ak[rows, hd, 0:P * (tq + 1)], start=True, stop=True)
                ins.then_inc(job_done, 1)

            def values(i):
                hd, tq = i // TT, i % TT
                key = ("ot", hd)
                b = job_banks(key)[0]
                if tq == 0:
                    wait_banks(pe, key)
                wait_job(pe, ("pt", i))
                for kt in range(tq + 1):
                    ins = pe.matmul(psum[:, b, P * tq:P * tq + P], av[:, kt, P * hd:P * hd + P],
                                    PTs[:, i % 2, P * kt:P * kt + P], start=kt == 0, stop=kt == tq)
                if tq == TT - 1:
                    assert JB.order[order[0]] == key
                    order[0] += 1
                    ins.then_inc(job_done, 1)

            scores(0)
            for i in range(n_i):
                if i + 1 < n_i:
                    scores(i + 1)
                pe.wait_ge(pc_ready, i + 1)
                if i >= 1:
                    values(i - 1)
                b = begin(("pt", i))
                for kt in range(i % TT + 1):
                    ins = pe.transpose(psum[:, b, P * kt:P * kt + P], Pb[:, 2 * (i % 2), P * kt:P * kt + P],
                                       c_("ident"))
                ins.then_inc(job_done, 1)
            values(n_i - 1)
            head_sum(("osq",), KT, 16, "sel128")
            pe.wait_ge(kn_l, 5)
            for k in range(KT):
                b = begin(("oinv", k))
                two(bank(b), heads_r[:, P * k:P * k + P], (n_hi[:, :], n_lo[:, :])).then_inc(job_done, 1)
            product("ao", XV["attn"])
            norm_sum(3)
            ffn(1)
            product("eq", XV["even"])
            product("ek", None)
            features(PL.first["elr"], None, m_count=1)
            wait_product(pe, "elr")
            pe.wait_ge(small_in, 64)
            for m in range(2):
                b = begin(("za", m))
                pe.matmul(bank(b), wa2[:, P * m:P * m + P], elr[:, :], start=True, stop=True).then_inc(job_done, 1)
            product("ev", None, tokens)
            for name in ("ega", "esv", "eu", "egb"):
                product(name, None)
            b = begin(("wsT",))
            for g in range(4):
                ins = pe.transpose(psum[:, b, P * g:P * g + P], ws[:, g, :], c_("ident"))
            ins.then_inc(job_done, 1)
            pe.wait_ge(gl_d, 4)

            def keys_and_scores(name, tt, qk):
                tk = slice(P * tt, P * tt + P)
                b = begin((name + "kt", tt))
                for m in range(2):
                    ins = pe.transpose(psum[:, b, P * m:P * m + P], qk[:, 2 + m, tk], c_("ident"))
                ins.then_inc(job_done, 1)
                b = begin((name + "s", tt))
                for half in range(2):
                    rows = slice(64 * half, 64 * half + 64)
                    for m in range(2):
                        ins = pe.matmul(psum[:, b + half, P * m:P * m + P], qk[rows, 2 + m, tk], qk[rows, m, tk],
                                        start=True, stop=True)
                ins.then_inc(job_done, 1)

            def state_update(key, tt, rows, v):
                b = begin(key)
                for h in range(4):
                    ins = pe.matmul(psum[:, b, P * h:P * h + P], kt2[rows, tt % 2, P * (h // 2):P * (h // 2) + P],
                                    v[rows, tt, P * h:P * h + P], start=True, stop=True)
                ins.then_inc(job_done, 1)

            def outputs(key, tt, tok, state_, q, v):
                b = begin(key)
                n = tok.stop - tok.start
                for h in range(4):
                    o = psum[:, b, n * h:n * h + n]
                    pe.matmul(o, state_[:, h, :], q[:, h // 2, P * tt + tok.start:P * tt + tok.stop], start=True,
                              stop=False)
                    at = P * HEAD_SLOT[h]
                    ins = pe.matmul(o, v[:, tt, P * h:P * h + P], sT[:, tt % 2, at + tok.start:at + tok.stop],
                                    start=False, stop=True)
                ins.then_inc(job_done, 1)

            for tt in range(-1, TT):
                if tt + 1 < TT:
                    keys_and_scores("g", tt + 1, eqk)
                if tt >= 0:
                    wait_job(pe, ("gkt", tt))
                    for c in (2 * tt, 2 * tt + 1):
                        state_update(("gu", c), tt, slice(64 * (c % 2), 64 * (c % 2) + 64), ev)
                    wait_job(pe, ("gs", tt))
                    for c in (2 * tt, 2 * tt + 1):
                        pe.wait_ge(g_state, c + 1)
                        outputs(("go", c), tt, slice(64 * (c % 2), 64 * (c % 2) + 64), est[c % 2], eqk, ev)
            for g in range(4):
                b = begin(("smean", g))
                pe.matmul(bank(b), c_("allmean"), esv[:, g, :], start=True, stop=True).then_inc(job_done, 1)
            head_sum(("gosq",), 4, 24, "sel128")
            head_sum(("svar",), 4, 28, "sel128")
            pe.wait_ge(kn_l, 6)
            for g in range(4):
                b = begin(("gorb", g))
                two(bank(b), heads_r[:, P * g:P * g + P], (en_hi[:, :], en_lo[:, :])).then_inc(job_done, 1)
            pe.wait_ge(kn_l, 7)
            for g in range(4):
                b = begin(("srb", g))
                two(bank(b), heads_r[:, P * g:P * g + P], (en_hi[:, :], en_lo[:, :])).then_inc(job_done, 1)
            for g in range(4):
                pe.wait_ge(sv_ready, g + 1)
                b = begin(("svT", g))
                for tt in range(TT):
                    ins = pe.transpose(psum[:, b, P * tt:P * tt + P], esv[:, g, P * tt:P * tt + P], c_("ident"))
                ins.then_inc(job_done, 1)
                wait_job(pe, ("svT", g))
                wait_job(pe, ("wsT",))
                b = begin(("sg", g))
                for tt in range(TT):
                    o = psum[:, b, P * tt:P * tt + P]
                    pe.matmul(o, svt[:, g % 2, P * tt:P * tt + P], wsT[:, g, :], start=True, stop=False)
                    ins = pe.matmul(o, cst[0:1, CST["ones"]:CST["ones"] + P], bsr[0:1, P * g:P * g + P],
                                    start=False, stop=True)
                ins.then_inc(job_done, 1)

            def layer_norm(n):
                name = ("eo", "oo")[n]
                for which in ("lm", "lv"):
                    b = begin((which, n))
                    for k in range(KT):
                        if which == "lm":
                            wait_step(pe, PL.first[name] + k // 2)
                        else:
                            pe.wait_ge(sq_ready, 8 * (4 + n) + k + 1)
                        ins = pe.matmul(bank(b), c_("ones"), x[:, k, :] if which == "lm" else xf[:, k % 2, :],
                                        start=k == 0, stop=k == KT - 1)
                        if k == KT - 1:
                            ins.then_inc(job_done, 1)
                        elif which == "lv":
                            ins.then_inc(sq_used, 1)

            product("eo", XV["evenmix"])
            layer_norm(0)
            product("oq", XV["odd"])
            product("ok", None)
            wait_product(pe, "ok")
            for i in range(4):
                b = begin(("rt", i))
                pe.matmul(bank(b), c_("rot2"), oqk[:, i, :], start=True, stop=True).then_inc(job_done, 1)
            product("ov", None, tokens)
            for name in ("ogc", "op", "ogd"):
                product(name, None)
            pe.wait_ge(odd_in, 32)
            for g in range(4):
                pe.wait_ge(win_d, g + 1)
                b = begin(("pool", g))
                pe.matmul(bank(b), wpl[:, g, :], omix[:, 4 + g, :], start=True, stop=True).then_inc(job_done, 1)
            pe.wait_ge(rot_done, 4)
            for tt in range(-1, TT):
                if tt + 1 < TT:
                    keys_and_scores("r", tt + 1, oqk)
                if tt >= 0:
                    wait_job(pe, ("rkt", tt))
                    state_update(("ru", tt), tt, slice(0, P), ov)
                    wait_job(pe, ("rs", tt))
                    pe.wait_ge(r_state, tt + 1)
                    outputs(("ro", tt), tt, slice(0, P), est[tt % 2], oqi, ov)
            wait_job(pe, ("ro", TT - 1))
            for h in range(4):
                b = begin(("rmean", h))
                pe.matmul(bank(b), c_("allmean"), omix[:, h, :], start=True, stop=True).then_inc(job_done, 1)
            head_sum(("rvar",), 4, 32, "sel128")
            pe.wait_ge(kn_l, 8)
            for h in range(4):
                b = begin(("rrb", h))
                two(bank(b), heads_r[:, P * h:P * h + P], (on_hi[:, :], on_lo[:, :])).then_inc(job_done, 1)
            product("oo", XV["oddmix"])
            layer_norm(1)
            for tt in range(TT):
                for i in range(2):
                    if i == 0 and tt == 0:
                        pe.wait_ge(ln_b, 16)
                    b = begin(("out", tt, i))
                    for j in range(4):
                        ins = pe.transpose(psum[:, b, P * j:P * j + P], x[:, 4 * i + j, P * tt:P * tt + P], c_("ident"))
                    ins.then_inc(job_done, 1)


_INS = ["x", "g_mix", "g_ffn", "rw_mu", "rw_w_r", "rw_w_k",
        "rw_w_v", "rw_w_o", "rw_w0", "rw_w1", "rw_w2", "rw_a0",
        "rw_a1", "rw_a2", "rw_g1", "rw_g2", "rw_k_k", "rw_k_a",
        "rw_r_k", "rw_lnx_w", "rw_lnx_b", "kv_g", "kv_w", "k_norm_g",
        "da_w_q", "da_q_norm_g", "da_lam_q1", "da_lam_k1", "da_lam_q2", "da_lam_k2",
        "da_subln_g", "da_w_o", "ffn_w_gu", "ffn_w_down", "positions_2", "l0_w_in_2",
        "l0_w_a2_2", "l0_b_a_2", "l0_gla_norm_g_2", "l0_sgu_ln_g_2", "l0_sgu_ln_b_2", "l0_w_s_2",
        "l0_b_s_2", "l0_w_out_2", "l0_ln_g_2", "l0_ln_b_2", "l1_w_in_2", "l1_ret_norm_g_2",
        "l1_w_pool_2", "l1_pool_scale_2", "l1_w_out_2", "l1_ln_g_2", "l1_ln_b_2"]


def kernel(**inputs):
    import numpy as _np
    import concourse.bacc as _bacc
    from concourse import mybir as _mybir
    from concourse.bass_utils import run_bass_kernel_spmd as _run

    nc = _bacc.Bacc("TRN2", target_bir_lowering=False, num_devices=1)
    arrays, t = {}, {}
    for name in _INS:
        a = _np.ascontiguousarray(inputs[name])
        arrays[f"in_{name}"] = a
        t[name] = nc.dram_tensor(f"in_{name}", a.shape, _mybir.dt.from_np(a.dtype), kind="ExternalInput").ap()
    for name, a in host_constants().items():
        arrays[name] = a
        t[name] = nc.dram_tensor(name, a.shape, _mybir.dt.from_np(a.dtype), kind="ExternalInput").ap()
    out = nc.dram_tensor("out_x", (1, S, D), _mybir.dt.float32, kind="ExternalOutput").ap()
    build(nc, t, out)
    return _run(nc, [arrays], core_ids=[0]).results[0]["out_x"]
```

```python
from contextlib import ExitStack

import numpy as np

import concourse.bass as bass
from concourse import mybir

F32 = mybir.dt.float32
F32R = mybir.dt.float32r
BF16 = mybir.dt.bfloat16
I32 = mybir.dt.int32
ALU = mybir.AluOpType
ACT = mybir.ActivationFunctionType
AX = mybir.AxisListType

P = 128
S = 512
D = 1024
KT = D // P
TT = S // P
F = 2816
FT = F // P
HEADS, HN = 16, 64
CH = 64
NCH = S // CH
LAM_INIT = 0.8 - 0.6 * float(np.exp(-0.3))
ALPHA = 4.0 ** 0.25
EXPW = float(np.exp(-0.5))
POOL_WINDOWS = (2, 4, 8, 16)
HEAD_SLOT = (0, 2, 1, 3)
ROUND = 12582912.0
TWO_PI = (6.28125, 0.0019350051879882812, float(2.0 * np.pi - 6.28125 - 0.0019350051879882812))

LEVELS = (1, 2, 4, 8, 16, 32)
CST_PARTS = ("ident", "ones", "blkmean", "allmean", "sel64", "sel128", "rot1", "rot2", "incl", "causal", "blk")
CST = {n: i * P for i, n in enumerate(CST_PARTS)}
MISC = len(CST_PARTS) * P
C_EPS6, C_EPSL, C_EPS5, C_INVF, C_WST, C_CNT = MISC, MISC + 1, MISC + 2, MISC + 3, MISC + 4, MISC + 8
NCST = C_CNT + 4 * 16
LOG_GAMMA = np.log(1.0 - 2.0 ** (-5.0 - np.arange(4)))
GAMMA_CHUNK = [float(np.exp(P * g)) for g in LOG_GAMMA]


def host_constants():
    p = np.arange(P)
    same = (p[:, None] // 64) == (p[None, :] // 64)
    up = p[:, None] <= p[None, :]
    c = np.zeros((P, NCST), np.float32)

    def put(name, m):
        c[:, CST[name]:CST[name] + P] = m

    put("ident", np.eye(P))
    put("ones", 1.0)
    put("blkmean", same / 64.0)
    put("allmean", 1.0 / P)
    sel64 = np.zeros((P, KT, 16))
    sel128 = np.zeros((P, KT, 16))
    for k in range(KT):
        sel64[:64, k, 2 * k] = 1.0
        sel64[64:, k, 2 * k + 1] = 1.0
        sel128[:, k, 2 * k:2 * k + 2] = 1.0
    put("sel64", sel64.reshape(P, P))
    put("sel128", sel128.reshape(P, P))
    rot1 = np.zeros((P, P))
    rot2 = np.zeros((P, P))
    for b in (0, 64):
        for i in range(8):
            rot1[b + 8 + i, b + i] = -1.0
            rot1[b + i, b + 8 + i] = 1.0
        for i in range(32):
            rot2[b + 32 + i, b + i] = -1.0
            rot2[b + i, b + 32 + i] = 1.0
    put("rot1", rot1)
    put("rot2", rot2)
    put("incl", same & up)
    put("causal", up)
    put("blk", same)
    c[:, C_EPS6] = 1e-6
    c[:, C_EPSL] = 64e-5
    c[:, C_EPS5] = 1e-5
    c[:, C_INVF] = (10000.0 ** (-(p % 32).astype(np.float32) / np.float32(32))).astype(np.float32)
    for h in range(4):
        c[:, C_WST + h] = np.exp((P - 1.0 - p) * LOG_GAMMA[h])
    for g, w in enumerate(POOL_WINDOWS):
        c[:, C_CNT + 16 * g:C_CNT + 16 * g + 16] = 1.0 / np.minimum(np.arange(16) + 1, w)
    heads = np.zeros((16, D), np.float32)
    for h in range(16):
        heads[h, 64 * h:64 * h + 64] = 1.0
    lv = np.zeros((P, 7, P), np.float32)
    lv[:, 0] = same & (p[:, None] < p[None, :])
    for n, s in enumerate(LEVELS):
        one_block = p[:, None] // (2 * s) == p[None, :] // (2 * s)
        lv[:, n + 1] = one_block & (p[:, None] % (2 * s) < s) & (p[None, :] % (2 * s) >= s)
    keep = np.ones((P, S), np.float32)
    keep[:, ::CH] = 0.0
    inv = 500000.0 ** (-np.arange(0, 16, 2, dtype=np.float32) / np.float32(16))
    ang = np.arange(S, dtype=np.float32)[None, :] * inv.astype(np.float32)[:, None]
    rope = np.zeros((P, 2, S), np.float32)
    rope[:, 0] = 1.0
    for b in (0, 64):
        for r in (0, 8):
            rope[b + r:b + r + 8, 0] = np.cos(ang)
            rope[b + r:b + r + 8, 1] = np.sin(ang)
    ret = np.zeros((P, 4 * P + 2 * S), np.float32)
    for h in range(4):
        rel = p[None, :] - p[:, None]
        at = P * HEAD_SLOT[h]
        ret[:, at:at + P] = 0.125 * np.where(rel >= 0, np.exp(np.maximum(rel, 0) * LOG_GAMMA[h]), 0.0)
        t, b = h // 2, 64 * (h % 2)
        ret[b:b + 64, 4 * P + t * S:4 * P + t * S + S] = 0.125 * np.exp((np.arange(S) % P + 1.0) * LOG_GAMMA[h])
    return {"c_main": c, "c_heads": heads, "c_levels": lv.reshape(P, 7 * P), "c_keep": keep,
            "c_rope": rope.reshape(P, 2 * S), "c_ret": ret}


ROWS_A = (("g_mix", 16), ("g_ffn", 16), ("rw_mu", 48), ("rw_w0", 8), ("rw_a0", 8), ("rw_k_k", 8), ("rw_k_a", 8),
          ("rw_r_k", 8), ("rw_lnx_w", 8))
ROWS_B = (("rw_lnx_b", 8), ("kv_g", 8), ("l0_ln_g_2", 8), ("l0_ln_b_2", 8), ("l1_ln_g_2", 8), ("l1_ln_b_2", 8),
          ("l0_b_a_2", 2), ("l0_gla_norm_g_2", 4), ("l0_sgu_ln_g_2", 4), ("l0_sgu_ln_b_2", 4), ("l1_ret_norm_g_2", 4),
          ("l1_pool_scale_2", 4), ("da_subln_g", 1), ("k_norm_g", 1), ("da_q_norm_g", 1))
PV = {}
for _base, _rows in ((0, ROWS_A), (P, ROWS_B)):
    _at = _base
    for _name, _n in _rows:
        PV[_name] = _at
        _at += _n
NROWS_B = sum(n for _, n in ROWS_B)
MU_R, MU_W, MU_K, MU_V, MU_A, MU_G = range(6)


class Plan:
    def __init__(self):
        self.slots = []
        self.steps = []
        self.first = {}
        self.count = {}
        self.first_slot = {}
        self.kstart = [0]
        self.taken = []
        self.last_step_of_slot = {}
        self.n_taken = {"A": 0, "D": 0}

    def product(self, name, slots, steps, slots_per_step, ksteps, taker, reuse=False):
        self.first[name], self.count[name] = len(self.steps), steps
        s0 = len(self.slots) - (slots if reuse else 0)
        self.first_slot[name] = s0
        if not reuse:
            self.slots += [(name, i) for i in range(slots)]
        for i in range(steps):
            at = s0 + (i * slots_per_step if slots_per_step else 0)
            n = slots_per_step or 1
            self.steps.append((name, at, n, ksteps))
            self.kstart.append(self.kstart[-1] + ksteps)
            self.n_taken[taker] += 1
            self.taken.append((taker, self.n_taken[taker]))
            for q in range(at, at + n):
                self.last_step_of_slot[q] = len(self.steps) - 1


def make_plan():
    pl = Plan()
    pl.product("k", 4, 4, 1, 8, "A")
    pl.product("v", 4, 4, 1, 8, "A")
    pl.product("r", 4, 4, 1, 8, "A")
    pl.product("g1", 1, 1, 1, 8, "A")
    pl.product("a1", 1, 1, 1, 8, "A")
    pl.product("w1", 1, 1, 1, 8, "A", reuse=True)
    pl.product("a2", 1, 4, 0, 1, "A")
    pl.product("w2", 1, 4, 0, 1, "A", reuse=True)
    pl.product("g2", 1, 4, 0, 1, "D")
    pl.product("o", 4, 4, 1, 8, "D")
    pl.product("gu0", 22, 22, 1, 8, "D")
    pl.product("dn0", 12, 4, 3, 22, "D")
    pl.product("q", 4, 4, 1, 8, "D")
    pl.product("kk", 4, 4, 1, 8, "D")
    pl.product("kv", 4, 4, 1, 8, "A")
    pl.product("ao", 4, 4, 1, 8, "D")
    pl.product("gu1", 22, 22, 1, 8, "D")
    pl.product("dn1", 12, 4, 3, 22, "D")
    for n, c in (("eq", 1), ("ek", 1), ("elr", 1), ("ev", 2), ("esv", 2), ("eu", 2), ("egb", 2), ("ega", 2)):
        pl.product(n, c, c, 1, 8, "A")
    pl.product("eo", 4, 4, 1, 8, "D")
    for n, c in (("oq", 1), ("ok", 1), ("ov", 2), ("op", 2), ("ogd", 2), ("ogc", 2)):
        pl.product(n, c, c, 1, 8, "A")
    pl.product("oo", 4, 4, 1, 8, "D")
    return pl


PL = make_plan()
X_LAST = ("k", "v", "r", "g1", "a1", "w1", "o", "gu0", "q", "kv", "ao", "gu1", "ega", "eo", "ogc", "oo")
XV = {n: i for i, n in enumerate(("xk", "xv", "xr", "xg", "xa", "xw", "y", "ffn0", "qin", "kvin", "attn", "ffn1",
                                  "even", "evenmix", "odd", "oddmix"))}


NO_XF = ("attn", "even", "evenmix", "odd", "oddmix")
NORM_AT = (0, 8, 16, 24, 28, 32)


def step_end(s):
    return PL.kstart[s + 1]


def slot_end(n):
    s = PL.last_step_of_slot[n]
    name, at, cnt, ks = PL.steps[s]
    return PL.kstart[s] + min(ks, 8 * (n - at + 1))


def xv_last_k(v, k):
    name = X_LAST[v]
    s = PL.first[name] + PL.count[name] - 1
    return PL.kstart[s] + k + 1


class Jobs:
    def __init__(self):
        self.order = []
        self.info = {}
        self.n = {"A": 0, "D": 0}
        self.before = {}
        self.user = {}

    def add(self, key, banks, eng):
        banks = (banks,) if isinstance(banks, int) else tuple(banks)
        self.n[eng] += 1
        self.info[key] = (banks, eng, len(self.order), self.n[eng])
        self.before[key] = [self.user[b] for b in banks if b in self.user]
        for b in banks:
            self.user[b] = ("job", key)
        self.order.append(key)

    def step(self, name):
        for i in range(PL.count[name]):
            s = PL.first[name] + i
            pair = (2 * (s % 2), 2 * (s % 2) + 1)
            self.before[("step", s)] = [self.user[b] for b in pair if b in self.user]
            for b in pair:
                self.user[b] = ("step", s)


ATT_AT = {9: (("root", 0),), 10: (("inv", 0),)}
for _t in range(KT):
    ATT_AT[1 + _t] = (("sq", _t),)
    ATT_AT[16 + _t] = (("hinv", _t), ("rot", _t - 1)) if _t else (("hinv", 0),)
ATT_AT[16 + KT] = (("rot", KT - 1),)
EVEN_BESIDE = ("eu", "egb", "ega")
EVEN_AT = {1: (("ks", 0),), 31: (("root", 0),), 32: (("wsT", 0),), 33: (("inv", 0),),
           35: (("gorb", 0), ("gorb", 1)), 36: (("gorb", 2), ("gorb", 3)), 37: (("inv", 1),),
           40: (("srb", 0), ("srb", 1)), 41: (("srb", 2), ("srb", 3)),
           42: (("svT", 0),), 43: (("sg", 0), ("svT", 1)), 44: (("sg", 1), ("svT", 2)),
           45: (("sg", 2), ("svT", 3)), 46: (("sg", 3),)}
ODD_BESIDE = ("op", "ogd", "ogc")
ODD_AT = {0: (("rt", 0),), 1: (("rt", 1),), 3: (("rt", 2),), 4: (("rt", 3),), 8: (("ks", 0),),
          19: (("win", 0),), 22: (("win", 1),), 24: (("win", 2),), 27: (("win", 3),), 38: (("inv", 0),),
          42: (("rrb", 0), ("rrb", 1)), 43: (("rrb", 2), ("rrb", 3))}
for _t in range(TT):
    for _at, _what in ((3, ("ks", _t + 1)), (4, ("gu", 2 * _t)), (5, ("gu", 2 * _t + 1)), (6, ("go", 2 * _t)),
                       (7, ("go", 2 * _t + 1))):
        if _what != ("ks", TT):
            EVEN_AT[5 * _t + _at] = (_what,)
    for _at, _what in ((10, ("ks", _t + 1)), (11, ("ru", _t)), (13, ("ro", _t))):
        if _what != ("ks", TT):
            ODD_AT[5 * _t + _at] = (_what,)
    EVEN_AT[23 + _t] = (("smean", _t),)
    EVEN_AT[27 + _t] = (("sq", _t),)
    ODD_AT[29 + _t] = (("rmean", _t),)
    ODD_AT[33 + _t] = (("pool", _t), ("sq", _t))


GROUPS = 4
NL = len(LEVELS)


def make_jobs():
    j = Jobs()
    for k in range(KT):
        j.add(("xt", k), 4 + k % 2, "A")
    j.add(("rms", 0), 6, "A")
    j.add(("pv",), 7, "A")
    for n in ("k", "v", "r", "g1", "a1", "w1", "a2", "w2"):
        j.step(n)
    j.add(("ksq",), 4, "A")
    j.add(("bonus",), 5, "A")
    for k in range(KT):
        j.add(("kinv", k), 6 + k % 2, "D")
    ring = [0]

    def core(key, eng):
        j.add(key, ring[0] % 8, eng)
        ring[0] += 1

    for tt in range(TT):
        for i in range(2):
            core(("bt", tt, i), "A")
        for i in range(2):
            core(("kt", tt, i), "D")
        for pair in range(2):
            gs = (2 * pair, 2 * pair + 1)
            for g in gs:
                for m in ("At", "Rb", "Ak", "Rk"):
                    core((m, tt, g), "D")
            for g in gs:
                core(("T1", tt, g), "A")
            for g in gs:
                core(("AV", tt, g), "A")
            for lv in range(1, NL):
                for g in gs:
                    core(("G", tt, g, lv), "A")
                for g in gs:
                    if lv < NL - 1:
                        core(("TG", tt, g, lv), "D")
                    core(("TGt", tt, g, lv), "D")
        for c in (2 * tt, 2 * tt + 1):
            for hh in range(2):
                core(("X", c, hh), "D")
            for hh in range(2):
                core(("U", c, hh), "A")
            for hh in range(2):
                core(("SU", c, hh), "D")
            core(("Y", c), "A")
    for k in range(KT):
        j.add(("gmean", k), 6 + k % 2, "D")
    j.add(("gvar",), 5, "A")
    for k in range(KT):
        j.add(("grstd", k), 4, "D")
        j.add(("vT", k), 5, "D")
        j.add(("bb", k), 6, "A")
        if k % 2:
            s = PL.first["g2"] + k // 2
            pr = (2 * (s % 2), 2 * (s % 2) + 1)
            j.before[("step", s)] = [j.user[b] for b in pr if b in j.user]
            for b in pr:
                j.user[b] = ("step", s)
    j.step("o")
    j.add(("rms", 1), 6, "A")
    j.step("gu0")
    j.step("dn0")
    j.add(("lam",), 7, "A")
    j.add(("rms", 2), 6, "A")
    j.step("q")
    j.add(("rtT",), 7, "D")
    j.step("kk")
    j.step("kv")
    for w in "qk":
        for n in range(32):
            for what, k in ATT_AT.get(n, ()):
                if what == "hinv":
                    j.add((what, w, k), 4 + k % 2, "D")
                elif what == "rot":
                    j.add((what, w, k), 6 + k % 2, "D")
                elif what == "sq" and k == KT - 1:
                    j.add(("hsq", w), 4, "A")

    def sc(i):
        j.add(("sc", i), (2 * (i % 3), 2 * (i % 3) + 1), "A")

    sc(0)
    sc(1)
    for i in range(HEADS // 2 * TT):
        if i + 2 < HEADS // 2 * TT:
            sc(i + 2)
        if i and i % TT == 0:
            j.add(("ot", i // TT - 1), 7, "A")
        j.add(("pt", i), 6, "A")
    j.add(("ot", HEADS // 2 - 1), 7, "A")
    j.add(("osq",), 4, "A")
    for k in range(KT):
        j.add(("oinv", k), 5 + k % 2, "D")
    j.step("ao")
    j.add(("rms", 3), 6, "A")
    j.step("gu1")
    j.step("dn1")
    for n in ("eq", "ek", "elr"):
        j.step(n)
    j.add(("za", 0), 4, "D")
    j.add(("za", 1), 5, "D")
    for n in ("ev", "esv", "eu", "egb", "ega"):
        j.step(n)
    for n in range(48):
        for what, i in EVEN_AT.get(n, ()):
            if what == "ks":
                j.add(("gkt", i), 4, "A")
                j.add(("gs", i), (6, 7), "D")
            elif what == "gu":
                j.add((what, i), 5, "D")
            elif what in ("go", "svT"):
                j.add((what, i), 4 if what == "go" else 6 + i % 2, "A")
            elif what in ("smean", "gorb"):
                j.add((what, i), 6 + i % 2, "D")
            elif what in ("srb", "sg"):
                j.add((what, i), 4 + i % 2, "D")
            elif what == "sq" and i == 3:
                j.add(("gosq",), 4, "A")
                j.add(("svar",), 5, "A")
            elif what == "wsT":
                j.add(("wsT",), 6, "D")
    j.step("eo")
    j.add(("lm", 0), 6, "D")
    j.add(("lv", 0), 7, "A")
    for n in ("oq", "ok", "ov", "op", "ogd", "ogc"):
        j.step(n)
    for n in range(48):
        for what, i in ODD_AT.get(n, ()):
            if what == "ks":
                j.add(("rkt", i), 4, "D")
                j.add(("rs", i), (6, 7), "D")
            elif what == "rt":
                j.add((what, i), 4 + i % 2, "D")
            elif what in ("ru", "pool"):
                j.add((what, i), 5, "D")
            elif what == "ro":
                j.add((what, i), 4, "A")
            elif what in ("rmean", "rrb"):
                j.add((what, i), 6 + i % 2, "D")
            elif what == "sq" and i == 3:
                j.add(("rvar",), 4, "A")
    j.step("oo")
    j.add(("lm", 1), 6, "D")
    j.add(("lv", 1), 7, "A")
    for i in range(2):
        for t in range(TT):
            j.add(("out", t, i), 2 + t, "AD"[t % 2])
    return j


NDMA = {"g1": 1, "elr": 1}


def raw_count(n):
    return sum(NDMA.get(PL.slots[q][0], 2) for q in range(n % 2, n + 1, 2))


def regions(n, t):
    name = PL.slots[n][0]
    v = t[:, :].rearrange("p (k c) -> p k c", k=8)
    if name in ("a1", "elr"):
        return [v[:, :, 0:128]]
    if name == "g1":
        return [v[:, :, 0:160]]
    if name == "a2":
        return [t[:, 0:1024]]
    if name == "g2":
        return [t[:, 0:1024], t[96:128, 1024:2048]]
    if name in ("dn0", "dn1") and PL.slots[n][1] % 3 == 2:
        return [v[:, 0:6, :]]
    return [t[:, :]]


def build(nc, t, out):
    JB = make_jobs()
    ctx = ExitStack()
    with ctx:
        base = (nc.sbuf_base + 31) // 32 * 32
        end = nc.sbuf_usable_end
        top = [base]

        def size(shape, dt):
            n = 2 if dt == BF16 else 4
            for s in shape[1:]:
                n *= s
            return (n + 31) // 32 * 32

        def at(name, shape, dt, offset):
            assert offset + size(shape, dt) <= end, (name, offset + size(shape, dt) - end)
            return nc.alloc_sbuf_tensor_at(name, shape, dt, offset=offset)

        def sb(name, shape, dt=F32):
            r = at(name, shape, dt, top[0])
            top[0] += size(shape, dt)
            return r

        def sem(name):
            return ctx.enter_context(nc.semaphore(name))

        x = sb("x", [P, KT, S])
        xf = sb("xf", [P, 2, S])
        rt = sb("rt", [P, S])
        cst = sb("cst", [P, NCST])
        heads_r = sb("heads_r", [16, D], F32R)
        pv = sb("pv", [P, P + NROWS_B])
        omu = sb("omu", [P, 48])
        col = sb("col", [P, 28])
        raw_at = top[0]
        weight_raw = [sb(f"weight_raw{i}", [P, 2048]) for i in range(2)]
        w_at = top[0]
        w_hi = [sb(f"w_hi{i}", [P, 2048], F32R) for i in range(2)]
        w_lo = [sb(f"w_lo{i}", [P, 2048], F32R) for i in range(2)]
        x_at = top[0]
        X_hi = sb("X_hi", [P, KT, S], F32R)
        X_lo = sb("X_lo", [P, KT, S], F32R)
        arena = top[0]

        def here(offset):
            spot = [offset]

            def alloc(name, shape, dt=F32):
                r = at(name, shape, dt, spot[0])
                spot[0] += size(shape, dt)
                return r
            alloc.spot = spot
            return alloc

        a_ = here(arena)
        xtok = a_("xtok", [P, TT, D])
        prow = [a_("prow0", [P, P]), a_("prow1", [NROWS_B, P])]
        heads_f = a_("heads_f", [16, D])
        lamr = a_("lamr", [1, 256])
        lamp = a_("lamp", [1, 128])
        a_ = here(arena)
        h_sb = a_("h_sb", [P, KT, S + 1])
        kf = a_("kf", [P, KT, S])
        rf = a_("rf", [P, KT, S])
        af = a_("af", [P, KT, S])
        vt = a_("vt", [P, TT, D])
        sgf = a_("sgf", [P, 2, S])
        keep = a_("keep", [P, S])
        pchunk = a_("pchunk", [P, KT, NCH])
        mid_hi = a_("mid_hi", [P, S], F32R)
        mid_lo = a_("mid_lo", [P, S], F32R)
        midf_at = a_.spot[0]
        midf = a_("midf", [P, S])
        lvl = here(midf_at)("lvl", [P, 7, P])
        xs = here(midf_at - 2 * size([P, S], F32))("xs", [P, D])
        b_ = here(x_at)
        u0 = b_("u0", [P, KT, S])
        u1 = b_("u1", [P, KT, S])
        b_ = here(x_at + size([P, KT, S], F32))
        btok = b_("btok", [P, D])
        ktok = b_("ktok", [P, D])
        state = [b_(f"state{i}", [P, KT, P]) for i in range(2)]
        b_ = here(w_at)
        Tt = b_("Tt", [P, 4, GROUPS * P])
        Rb = b_("Rb", [P, 4, GROUPS * P])
        Rk = b_("Rk", [P, 4, GROUPS * P])
        AV = b_("AV", [P, D])
        us = b_("us", [P, D])
        b_ = here(raw_at)
        tmp = b_("tmp", [P, 8, S])
        b_ = here(raw_at)
        At = b_("At", [P, 2, S])
        Tn = b_("Tn", [P, 2, S])
        Gs = b_("Gs", [P, 2, S])
        Lm = b_("Lm", [P, 2, S])
        Ak = xf
        b_ = here(arena + size([P, KT, S + 1], F32))
        sg_hi = b_("sg_hi", [P, 2, S], F32R)
        sg_lo = b_("sg_lo", [P, 2, S], F32R)
        gn_hi = b_("gn_hi", [16, S], F32R)
        gn_lo = b_("gn_lo", [16, S], F32R)
        bon_hi = b_("bon_hi", [16, S], F32R)
        bon_lo = b_("bon_lo", [16, S], F32R)
        b_ = here(arena + size([P, KT, S + 1], F32) + 2 * size([P, KT, S], F32))
        pt8 = b_("pt8", [P, 8, S])
        a_ = here(arena)
        hb_hi = a_("hb_hi", [P, FT, S], F32R)
        hb_lo = a_("hb_lo", [P, FT, S], F32R)
        sgate = a_("sgate", [P, 2, S])
        a_ = here(arena)
        ak = a_("ak", [P, KT, S])
        aq = a_("aq", [P, KT, S])
        av = a_("av", [P, TT, D])
        oT = a_("oT", [P, KT, S])
        rope = a_("rope", [P, 2, S])
        Pb = a_("Pb", [P, 6, S])
        PTs = a_("PTs", [P, 2, S])
        tq2 = a_("tq2", [P, 2, S])
        rth = a_("rth", [16, S])
        n_hi = a_("n_hi", [16, S], F32R)
        n_lo = a_("n_lo", [16, S], F32R)
        a_ = here(arena)
        mix = a_("mix", [P, KT, S])
        eqk = a_("eqk", [P, 4, S])
        ev = a_("ev", [P, TT, S])
        ega = a_("ega", [P, 4, S])
        esv = a_("esv", [P, 4, S])
        egb = a_("egb", [P, 4, S])
        elr = a_("elr", [16, S])
        gw = a_("gw", [P, 4, S])
        svt = here(a_.spot[0])("svt", [P, 2, S])
        gcum = a_("gcum", [P, 2, S])
        gend = a_("gend", [P, 2, NCH])
        keep_e = a_("keep_e", [P, S])
        en_hi = a_("en_hi", [16, S], F32R)
        en_lo = a_("en_lo", [16, S], F32R)
        wa2 = a_("wa2", [16, 256])
        ws = a_("ws", [P, 4, P])
        wsT = a_("wsT", [P, 4, P])
        bsr = a_("bsr", [1, S])
        even_end = a_.spot[0]
        b_ = here((end - 5 * size([P, S], F32)) // 32 * 32)
        kt2 = b_("kt2", [P, 2, 256])
        posi = here(b_.spot[0])("posi", [P, S], I32)
        sT = b_("sT", [P, 2, S])
        est = [b_(f"est{i}", [P, 4, P]) for i in range(2)]
        assert even_end <= (end - 5 * size([P, S], F32)) // 32 * 32, (even_end - end) / 2048
        a_ = here(arena)
        omix = a_("omix", [P, KT, S])
        oqk = a_("oqk", [P, 4, S])
        ov = a_("ov", [P, TT, S])
        ogc = a_("ogc", [P, 4, S])
        ogd = a_("ogd", [P, 4, S])
        PAD = max(POOL_WINDOWS)
        opp = a_("opp", [P, 4, PAD + S])
        csn = here(a_.spot[0])("csn", [P, 2, S])
        psh = a_("psh", [P, 2, PAD + S])
        cret = a_("cret", [P, 4 * P + 2 * S])
        oqi = a_("oqi", [P, 2, S])
        orw = a_("orw", [P, 2, S])
        pool16 = a_("pool16", [P, 16])
        wpl = a_("wpl", [P, 4, P])
        on_hi = a_("on_hi", [16, S], F32R)
        on_lo = a_("on_lo", [16, S], F32R)
        assert a_.spot[0] <= (end - 5 * size([P, S], F32)) // 32 * 32, (a_.spot[0] - end) / 2048
        a_ = here(arena)
        ost = a_("ost", [P, TT, D])
        psum = ctx.enter_context(nc.psum_tensor("psum", [P, 8, S], F32))

        cst_in = sem("cst_in")
        rows_in = sem("rows_in")
        x_in = [sem(f"x_in{i}") for i in range(4)]
        heads_in = sem("heads_in")
        keep_in = sem("keep_in")
        lvl_in = sem("lvl_in")
        raw_full = [sem("raw_full0"), sem("raw_full1")]
        hi_ready = sem("hi_ready")
        lo_ready = sem("lo_ready")
        kstep = sem("kstep")
        step_a, step_d = sem("step_a"), sem("step_d")
        job_done = sem("job_done")
        job_a, job_d = sem("job_a"), sem("job_d")
        xf_ready = sem("xf_ready")
        xhi_ready, xlo_ready = sem("xhi_ready"), sem("xlo_ready")
        sq_ready, sq_used = sem("sq_ready"), sem("sq_used")
        heads_ready = sem("heads_ready")
        dve_seq = sem("dve_seq")
        act_seq = sem("act_seq")
        pool_seq = sem("pool_seq")
        mid_f, mid_h, mid_l = sem("mid_f"), sem("mid_h"), sem("mid_l")
        prep_a, prep_d, prep_p, prep_pe = sem("prep_a"), sem("prep_d"), sem("prep_p"), sem("prep_pe")
        rt_ready = sem("rt_ready")
        ff_raw, ff_prod = sem("ff_raw"), sem("ff_prod")
        kn_f, kn_h, kn_l = sem("kn_f"), sem("kn_h"), sem("kn_l")
        at_ready = sem("at_ready")
        zero_ready = sem("zero_ready")
        level_ready = sem("level_ready")
        t_init = sem("t_init")
        s_new = sem("s_new")
        sg_h, sg_l = sem("sg_h"), sem("sg_l")
        gn_q, gn_pe, gn_aff = sem("gn_q"), sem("gn_pe"), sem("gn_aff")
        ff_gate, ff_hi, ff_lo = sem("ff_gate"), sem("ff_hi"), sem("ff_lo")
        out_sem = sem("out_sem")
        hn_a, hn_pe = sem("hn_a"), sem("hn_pe")
        rope_in, lam_in = sem("rope_in"), sem("lam_in")
        lam_row, lam_ready = sem("lam_row"), sem("lam_ready")
        sc_max = sem("sc_max")
        pc_ready = sem("pc_ready")
        hn_rot = sem("hn_rot")
        small_in = sem("small_in")
        gl_a, gl_d = sem("gl_a"), sem("gl_d")
        g_state = sem("g_state")
        pad_p = sem("pad_p")
        sv_ready = sem("sv_ready")
        gate_p = sem("gate_p")
        mix_a = sem("mix_a")
        ln_x, ln_c, ln_g, ln_b = sem("ln_x"), sem("ln_c"), sem("ln_g"), sem("ln_b")
        odd_in, pos_in = sem("odd_in"), sem("pos_in")
        ang_d, ang_a = sem("ang_d"), sem("ang_a")
        rot_done = sem("rot_done")
        r_state = sem("r_state")
        win_p, win_d = sem("win_p"), sem("win_d")
        omix_a = sem("omix_a")

        def bank(i, n=S):
            return psum[:, i, 0:n]

        def job_banks(key):
            return JB.info[key][0]

        def wait_done(eng, key):
            eng.wait_ge(job_done, JB.info[key][2] + 1)

        def wait_job(eng, key):
            _, who, _, n = JB.info[key]
            eng.wait_ge(job_a if who == "A" else job_d, n)

        def wait_step(eng, s):
            who, n = PL.taken[s]
            eng.wait_ge(step_a if who == "A" else step_d, n)

        def wait_product(eng, name):
            wait_step(eng, PL.first[name] + PL.count[name] - 1)

        def wait_banks(eng, key):
            for kind, what in JB.before[key]:
                if kind == "job":
                    wait_job(eng, what)
                else:
                    wait_step(eng, what)

        def step_banks(s):
            return 2 * (s % 2), 2 * (s % 2) + 1

        def pcol(name, i=0, rows=slice(0, P)):
            return pv[rows, PV[name] + i:PV[name] + i + 1]

        def c_(name, n=P, o=0):
            return cst[:, CST[name] + o:CST[name] + o + n]

        def wv(tile):
            return tile[:, :].rearrange("p (k c) -> p k c", k=8)

        def xready(v, k):
            return 8 * v + k + 1

        def xf_count(v, k):
            return 8 * (v - sum(1 for n in NO_XF if XV[n] < v)) + k + 1

        def group_head(g, j):
            return 8 * (g // 2) + 2 * j + g % 2

        def head_group(hd):
            return 2 * (hd // 8) + hd % 2, hd % 8 // 2

        def square_buffer(i):
            return (xf[:, :, :], pt8[:, 6:8, :], sgate[:, :, :], tq2[:, :, :])[i]

        def hn_pe_count(at, k):
            return at - NORM_AT.index(at) + k + 1

        block = ctx.enter_context(nc.Block())

        @block.sync
        def _(sp):
            def weight_src(n):
                name, i = PL.slots[n]
                square = {"k": t["rw_w_k"][0], "v": t["rw_w_v"][0], "r": t["rw_w_r"][0], "o": t["rw_w_o"][0],
                          "kk": t["kv_w"][:, 0:D], "kv": t["kv_w"][:, D:2 * D], "q": t["da_w_q"][0],
                          "ao": t["da_w_o"][0], "eo": t["l0_w_out_2"], "oo": t["l1_w_out_2"]}
                inner = {"eq": ("l0_w_in_2", 0), "ek": ("l0_w_in_2", 256), "ev": ("l0_w_in_2", 512),
                         "ega": ("l0_w_in_2", 1024), "eu": ("l0_w_in_2", 1552), "esv": ("l0_w_in_2", 2064),
                         "egb": ("l0_w_in_2", 2576), "oq": ("l1_w_in_2", 0), "ok": ("l1_w_in_2", 256),
                         "ov": ("l1_w_in_2", 512), "ogc": ("l1_w_in_2", 1024), "op": ("l1_w_in_2", 1536),
                         "ogd": ("l1_w_in_2", 2048)}
                r = weight_raw[n % 2]
                w3 = wv(r)
                if name in square:
                    src = square[name][:, 256 * i:256 * i + 256].rearrange("(k p) c -> p k c", p=P)
                    return [(w3[:, 0:4, :], src[:, 0:4, :]), (w3[:, 4:8, :], src[:, 4:8, :])]
                if name in inner:
                    w, c0 = inner[name]
                    src = t[w][:, c0 + 256 * i:c0 + 256 * i + 256].rearrange("(k p) c -> p k c", p=P)
                    return [(w3[:, 0:4, :], src[:, 0:4, :]), (w3[:, 4:8, :], src[:, 4:8, :])]
                if name == "elr":
                    return [(w3[:, :, 0:128], t["l0_w_in_2"][:, 1536:1664].rearrange("(k p) c -> p k c", p=P))]
                if name == "g1":
                    return [(w3[:, :, 0:160], t["rw_g1"][0].rearrange("(k p) c -> p k c", p=P))]
                if name == "a1":
                    return [(w3[:, :, 0:64], t["rw_w1"][0].rearrange("(k p) c -> p k c", p=P)),
                            (w3[:, :, 64:128], t["rw_a1"][0].rearrange("(k p) c -> p k c", p=P))]
                if name == "a2":
                    return [(r[0:64, 0:1024], t["rw_w2"][0]), (r[64:128, 0:1024], t["rw_a2"][0])]
                if name == "g2":
                    return [(r[:, 0:1024], t["rw_g2"][0, 0:128, :]), (r[96:128, 1024:2048], t["rw_g2"][0, 128:160, :])]
                raise AssertionError(name)

            def fill(n):
                if n >= 2:
                    sp.wait_ge(lo_ready, n - 1)
                for dst, src in weight_src(n):
                    sp.dma_start(dst, src).then_inc(raw_full[n % 2], 16)

            def fill_product(name):
                for i in range(sum(1 for q in PL.slots if q[0] == name)):
                    fill(PL.first_slot[name] + i)

            def fill_ffn(layer):
                n0 = PL.first_slot[f"gu{layer}"]
                src = t["ffn_w_gu"][layer].rearrange("(k p) (g c) -> p k g c", p=P, g=2)
                with sp.Fori(0, FT // 2) as i:
                    for j in range(2):
                        sp.wait_ge(lo_ready, n0 + j - 1 + 2 * i)
                        d3 = wv(weight_raw[(n0 + j) % 2])
                        for g in range(2):
                            sp.dma_start(d3[:, :, P * g:P * g + P],
                                         src[:, :, g, bass.ds(256 * i + 128 * j, 128)]).then_inc(
                                             raw_full[(n0 + j) % 2], 16)
                n0 = PL.first_slot[f"dn{layer}"]
                wd = t["ffn_w_down"][layer].rearrange("(k p) c -> p k c", p=P)
                with sp.Fori(0, 2) as i:
                    for j in range(6):
                        sp.wait_ge(lo_ready, n0 + j - 1 + 6 * i)
                        ks = 8 if j % 3 < 2 else 6
                        for k0, k1 in ((0, 4), (4, ks)):
                            sp.dma_start(wv(weight_raw[(n0 + j) % 2])[:, k0:k1, :],
                                         wd[:, 8 * (j % 3) + k0:8 * (j % 3) + k1,
                                            bass.ds(512 * i + 256 * (j // 3), 256)]
                                         ).then_inc(raw_full[(n0 + j) % 2], 16)

            sp.dma_start(cst[:, :], t["c_main"]).then_inc(cst_in, 16)
            for i in range(4):
                sp.dma_start(xtok[:, :, 256 * i:256 * i + 256],
                             t["x"][0].rearrange("(t p) d -> p t d", p=P)[:, :, 256 * i:256 * i + 256]
                             ).then_inc(x_in[i], 16)
            fill(0)
            fill(1)
            for i, rows in enumerate((ROWS_A, ROWS_B)):
                r = 0
                for name, n in rows:
                    src = t[name]
                    if name in ("k_norm_g", "da_q_norm_g"):
                        src = src if len(src.shape) == 1 else src[0]
                        for half in range(2):
                            sp.dma_start(prow[i][r:r + 1, 64 * half:64 * half + 64],
                                         src.rearrange("(a b) -> a b", a=1)).then_inc(rows_in, 16)
                    else:
                        dims = " ".join("abc"[:len(src.shape)])
                        flat = src.rearrange(f"{dims} -> ({dims})") if len(src.shape) > 1 else src
                        sp.dma_start(prow[i][r:r + n, :], flat.rearrange("(r c) -> r c", c=P)).then_inc(rows_in, 16)
                    r += n
            for i, name in enumerate(("da_lam_q1", "da_lam_k1", "da_lam_q2", "da_lam_k2")):
                sp.dma_start(lamr[0:1, 64 * i:64 * i + 64], t[name]).then_inc(lam_in, 16)
            sp.dma_start(heads_f[:, :], t["c_heads"]).then_inc(heads_in, 16)
            for name in ("k", "v", "r", "g1", "a1", "a2"):
                if name == "k":
                    fill(2)
                    fill(3)
                else:
                    fill_product(name)
                if name == "k":
                    sp.dma_start(keep[:, :], t["c_keep"]).then_inc(keep_in, 16)
            wait_product(sp, "w2")
            sp.wait_ge(mid_l, 2)
            sp.dma_start(lvl[:, :, :], t["c_levels"].rearrange("p (n c) -> p n c", c=P)).then_inc(lvl_in, 16)
            wait_job(sp, ("Y", NCH - 1))
            fill_product("g2")
            fill_product("o")
            fill_ffn(0)
            fill_product("q")
            wait_product(sp, "dn0")
            sp.dma_start(rope[:, :, :], t["c_rope"].rearrange("p (a s) -> p a s", a=2)).then_inc(rope_in, 16)
            for name in ("kk", "kv", "ao"):
                fill_product(name)
            fill_ffn(1)
            fill_product("eq")
            wait_product(sp, "dn1")
            sp.dma_start(keep_e[:, :], t["c_keep"]).then_inc(small_in, 16)
            sp.dma_start(wa2[:, :], t["l0_w_a2_2"]).then_inc(small_in, 16)
            sp.dma_start(ws[:, :, :], t["l0_w_s_2"].rearrange("g t s -> t g s")).then_inc(small_in, 16)
            sp.dma_start(bsr[0:1, :], t["l0_b_s_2"].rearrange("(a g) t -> a (g t)", a=1)).then_inc(small_in, 16)
            for name in ("ek", "elr", "ev", "esv", "eu", "egb", "ega", "eo"):
                fill_product(name)
            fill_product("oq")
            wait_product(sp, "eo")
            sp.dma_start(posi[:, :], t["positions_2"].to_broadcast([P, S])).then_inc(pos_in, 16)
            sp.dma_start(cret[:, :], t["c_ret"]).then_inc(odd_in, 16)
            sp.dma_start(wpl[:, :, :], t["l1_w_pool_2"].rearrange("g c d -> c g d")).then_inc(odd_in, 16)
            for name in ("ok", "ov", "op", "ogd", "ogc", "oo"):
                fill_product(name)
            for i in range(2):
                for tt in range(TT):
                    c = slice(S * i, S * i + S)
                    wait_job(sp, ("out", tt, i))
                    sp.dma_start(out.rearrange("a (t p) d -> p (a t) d", p=P)[:, tt, c], ost[:, tt, c]
                                 ).then_inc(out_sem, 16)
            sp.wait_ge(out_sem, 16 * 2 * TT)

        @block.gpsimd
        def _(pool):
            seq = [0]

            def link(ins):
                seq[0] += 1
                ins.then_inc(pool_seq, 1)
                pool.wait_ge(pool_seq, seq[0])

            def low(n, dyn=0):
                pool.wait_ge(hi_ready, n + 1 + dyn)
                parts = list(zip(regions(n, weight_raw[n % 2]), regions(n, w_hi[n % 2]), regions(n, w_lo[n % 2])))
                for i, (r, h, l) in enumerate(parts):
                    ins = pool.tensor_tensor(l, r, h.bitcast(F32), ALU.subtract)
                    if i < len(parts) - 1:
                        link(ins)
                ins.then_inc(lo_ready, 1)
                if len(parts) > 1:
                    pool.wait_ge(lo_ready, n + 1)

            def low_product(name):
                for i in range(sum(1 for q in PL.slots if q[0] == name)):
                    low(PL.first_slot[name] + i)

            def low_ffn(layer):
                n0 = PL.first_slot[f"gu{layer}"]
                with pool.Fori(0, FT // 2) as i:
                    for j in range(2):
                        low(n0 + j, 2 * i)
                n0 = PL.first_slot[f"dn{layer}"]
                with pool.Fori(0, 2) as i:
                    for j in range(6):
                        low(n0 + j, 6 * i)

            for name in ("k", "v", "r", "g1", "a1", "a2"):
                low_product(name)
            for k in range(KT):
                pool.wait_ge(prep_d, 6 * k + 1)
                pool.tensor_tensor(h_sb[:, k, 0:S], u1[:, k, :], h_sb[:, k, 0:S], ALU.subtract).then_inc(prep_p, 1)
                pool.wait_ge(prep_a, 5 * k + 3)
                pool.wait_ge(prep_d, 6 * k + 4)
                pool.tensor_tensor(rf[:, k, :], rf[:, k, :], tmp[:, 4 + k % 2, :], ALU.mult).then_inc(prep_p, 1)
            pool.wait_ge(prep_a, 5 * KT)
            wait_product(pool, "w2")
            pool.memset(us[:, :], 0.0)
            for i in range(2):
                ins = pool.memset(state[i][:, :, :], 0.0)
            ins.then_inc(zero_ready, 1)
            pool.wait_ge(lvl_in, 16)
            for tt in range(TT):
                for pair in range(2):
                    for g in (2 * pair, 2 * pair + 1):
                        wait_job(pool, ("At", tt, g))
                        if tt:
                            wait_done(pool, ("Y", 2 * tt - 1))
                        gb = g % 2
                        a3 = At[:, gb, :].rearrange("p (h c) -> p h c", h=GROUPS)
                        t3 = Tt[:, g, :].rearrange("p (h c) -> p h c", h=GROUPS)
                        link(pool.tensor_tensor(t3, a3, lvl[:, 1:2, :].to_broadcast([P, GROUPS, P]), ALU.mult))
                        pool.tensor_tensor(t3, t3, c_("ident")[:, None, :].to_broadcast([P, GROUPS, P]),
                                           ALU.add).then_inc(t_init, 1)
                    for lv in range(1, NL):
                        for g in (2 * pair, 2 * pair + 1):
                            gb = g % 2
                            if lv > 1:
                                wait_done(pool, ("G", tt, g, lv - 1))
                            elif tt or pair:
                                wait_done(pool, ("G", tt if pair else tt - 1, (g + 2) % 4, NL - 1))
                            pool.tensor_tensor(Lm[:, gb, :].rearrange("p (h c) -> p h c", h=GROUPS),
                                               At[:, gb, :].rearrange("p (h c) -> p h c", h=GROUPS),
                                               lvl[:, lv + 1:lv + 2, :].to_broadcast([P, GROUPS, P]),
                                               ALU.mult).then_inc(level_ready, 1)
            low_product("g2")
            low_product("o")
            low_ffn(0)
            for name in ("q", "kk", "kv", "ao"):
                low_product(name)
            low_ffn(1)
            for name in ("eq", "ek", "elr", "ev", "esv", "eu", "egb", "ega"):
                low_product(name)
            wait_product(pool, "egb")
            for g in range(4):
                pool.tensor_tensor(mix[:, 4 + g, :], mix[:, 4 + g, :], egb[:, g, :], ALU.mult).then_inc(gate_p, 1)
            low_product("eo")
            wait_product(pool, "eo")
            pool.memset(opp[:, :, 0:PAD], 0.0).then_inc(pad_p, 1)
            for name in ("oq", "ok", "ov", "op", "ogd"):
                low_product(name)
            pool.wait_ge(pad_p, 1)
            pool.wait_ge(rot_done, 4)
            link(pool.memset(psh[:, :, 0:PAD], 0.0))
            wait_product(pool, "op")
            for g in range(4):
                if g >= 1:
                    pool.wait_ge(win_d, g)
                src = opp[:, g, :]
                for i in range(g + 1):
                    dst = psh[:, i % 2, :]
                    sh = 1 << i
                    ins = pool.tensor_tensor(dst[:, PAD:PAD + S], src[:, PAD:PAD + S],
                                             src[:, PAD - sh:PAD - sh + S], ALU.add)
                    if i < g:
                        link(ins)
                    src = dst
                ins.then_inc(win_p, 1)
                if g in (1, 3):
                    low(PL.first_slot["ogc"] + g // 2)
            low_product("oo")

        @block.scalar
        def _(act):
            seq = [0]

            def link(ins):
                seq[0] += 1
                ins.then_inc(act_seq, 1)
                act.wait_ge(act_seq, seq[0])

            def ffn(layer):
                s0, n0 = PL.first[f"gu{layer}"], PL.first_slot[f"gu{layer}"]
                with act.Fori(0, FT // 2) as i:
                    for j in range(2):
                        high(n0 + j + 1, 32 * i, 16 * i)
                        act.wait_ge(ff_raw, FT * layer + j + 1 + 2 * i)
                        act.activation(sgate[:, j, :], sgate[:, j, :], ACT.Silu).then_inc(ff_gate, 1)
                        act.wait_ge(ff_prod, FT * layer + j + 1 + 2 * i)
                        act.activation(hb_hi[:, bass.ds(2 * i + j, 1), :], xf[:, j:j + 1, :],
                                       ACT.Copy).then_inc(ff_hi, 1)
                n0 = PL.first_slot[f"dn{layer}"]
                with act.Fori(0, 2) as i:
                    for j in range(6):
                        high(n0 + j + 1, 96 * i, 44 * i)

            def high(n, raw_dyn=0, k_dyn=0):
                act.wait_ge(raw_full[n % 2], 16 * raw_count(n) + raw_dyn)
                if n >= 2:
                    act.wait_ge(kstep, slot_end(n - 2) + k_dyn)
                for r, h in zip(regions(n, weight_raw[n % 2]), regions(n, w_hi[n % 2])):
                    last = act.activation(h, r, ACT.Copy)
                last.then_inc(hi_ready, 1)

            def next_slot(s):
                n = PL.steps[s][1]
                if n + 1 < len(PL.slots) and (s == 0 or PL.steps[s - 1][1] != n):
                    high(n + 1)

            def empty(key, out_, func=ACT.Copy, **kw):
                wait_done(act, key)
                act.activation(out_, bank(job_banks(key)[0]), func, **kw).then_inc(job_a, 1)

            def x_high1(v, k, src=None):
                if src is None:
                    act.wait_ge(xf_ready, xf_count(v, k))
                if v:
                    act.wait_ge(kstep, xv_last_k(v - 1, k))
                act.activation(X_hi[:, k, :], src[:, k, :] if src is not None else xf[:, (8 * v + k) % 2, :],
                               ACT.Copy).then_inc(xhi_ready, 1)

            def x_high(v, src=None):
                for k in range(KT):
                    x_high1(v, k, src)

            def norm_squares(i, v=None):
                for k in range(0 if v is None else 6):
                    x_high1(v, k)
                for k in range(KT):
                    if k >= 6 and v is not None:
                        x_high1(v, k)
                    if i == 0:
                        wait_job(act, ("xt", k))
                    elif k % 2 == 0:
                        wait_step(act, PL.first[("", "o", "dn0", "ao")[i]] + k // 2)
                    if k >= 2:
                        act.wait_ge(sq_used, 7 * i + k - 1)
                    act.activation(square_buffer(i)[:, k % 2, :], x[:, k, :], ACT.Square).then_inc(sq_ready, 1)
                wait_done(act, ("rms", i))
                act.activation(rt[:, :], bank(6), ACT.Sqrt, bias=cst[:, C_EPS6:C_EPS6 + 1],
                               scale=1.0 / D).then_inc(job_a, 1)

            def plain_last(name, dst, then=None, func=ACT.Copy, tokens=False, parts=None):
                for i in range(PL.count[name]):
                    s = PL.first[name] + i
                    next_slot(s)
                    if i == PL.count[name] - 1 and then is not None:
                        x_high(then)
                    for k in range(KT if parts is not None else 0):
                        parts(8 * i + k)
                    act.wait_ge(kstep, step_end(s))
                    b = step_banks(s)
                    if tokens:
                        for m in range(2):
                            last = act.activation(dst[:, 2 * m:2 * m + 2, 256 * i:256 * i + 256],
                                                  psum[:, b[m], :].rearrange("p (t c) -> p t c", t=2), func)
                    else:
                        for m in range(2):
                            last = act.activation(dst[:, 2 * i + m, 0:S], bank(b[m]), func)
                    last.then_inc(step_a, 1)

            def head_scale(src, n, at, key, scale, eps, ready, count, hi):
                for k in range(n):
                    if k >= 2:
                        act.wait_ge(hn_pe, hn_pe_count(at, k - 2))
                    act.activation(xf[:, k % 2, :], src[:, k, 0:S], ACT.Square).then_inc(hn_a, 1)
                wait_done(act, key)
                act.activation(rt[0:16, :], psum[0:16, job_banks(key)[0], :], ACT.Sqrt, bias=cst[0:16, eps:eps + 1],
                               scale=scale).then_inc(job_a, 1)
                act.wait_ge(ready, count)
                act.activation(hi[:, :], rt[0:16, :], ACT.Copy).then_inc(kn_h, 1)

            def layer_norm(n):
                name = ("eo", "oo")[n]
                for i in range(PL.count[name]):
                    next_slot(PL.first[name] + i)
                for k in range(KT):
                    act.wait_ge(ln_c, 8 * n + k + 1)
                    if k >= 2:
                        act.wait_ge(sq_used, 7 * (4 + n) + k - 1)
                    act.activation(xf[:, k % 2, :], x[:, k, :], ACT.Square).then_inc(sq_ready, 1)
                wait_done(act, ("lv", n))
                act.activation(rt[:, :], bank(7), ACT.Sqrt, bias=cst[:, C_EPS5:C_EPS5 + 1],
                               scale=1.0 / D).then_inc(job_a, 1)
                for k in range(KT):
                    act.wait_ge(ln_g, 8 * n + k + 1)
                    act.activation(x[:, k, :], x[:, k, :], ACT.Identity,
                                   bias=pcol(f"l{n}_ln_b_2", k)).then_inc(ln_b, 1)
                    if n == 0:
                        act.wait_ge(ln_b, k + 1)
                        x_high1(XV["odd"], k, x)

            def odd_angles():
                act.wait_ge(ang_d, 1)
                act.activation(csn[:, 1, :], orw[:, 0, :], ACT.Sin)
                act.activation(csn[:, 0, :], orw[:, 0, :], ACT.Sin, scale=0.5).then_inc(ang_a, 1)

            for k in range(KT):
                empty(("xt", k), x[:, k, :])
            norm_squares(0)
            wait_done(act, ("pv",))
            act.activation(pv[:, :], psum[:, 7, 0:P + NROWS_B], ACT.Copy).then_inc(job_a, 1)
            high(0)
            act.wait_ge(heads_in, 16)
            act.activation(heads_r[:, :], heads_f[:, :], ACT.Copy).then_inc(heads_ready, 1)
            x_high(0)
            plain_last("k", kf, 1)
            plain_last("v", vt, 2, tokens=True)
            plain_last("r", rf, 3)
            s = PL.first["g1"]
            next_slot(s)
            x_high(4)
            act.wait_ge(kstep, step_end(s))
            b = step_banks(s)
            act.activation(sgf[:, 0, :], bank(b[0]), ACT.Sigmoid)
            act.activation(sgf[96:128, 1, :], psum[96:128, b[1], :], ACT.Sigmoid).then_inc(step_a, 1)
            s = PL.first["a1"]
            next_slot(s)
            x_high(5)
            act.wait_ge(kstep, step_end(s))
            act.activation(midf[64:128, :], psum[64:128, step_banks(s)[0], :], ACT.Copy).then_inc(step_a, 1)
            wait_step(act, s)
            act.activation(mid_hi[64:128, :], midf[64:128, :], ACT.Copy).then_inc(mid_h, 1)
            s = PL.first["w1"]
            act.wait_ge(kstep, step_end(s))
            act.activation(midf[0:64, :], psum[0:64, step_banks(s)[0], :], ACT.Tanh).then_inc(step_a, 1)
            wait_step(act, s)
            act.activation(mid_hi[0:64, :], midf[0:64, :], ACT.Copy).then_inc(mid_h, 1)
            act.wait_ge(xlo_ready, xready(5, 7))
            for name, dst, vec in (("a2", af, "rw_a0"), ("w2", h_sb, "rw_w0")):
                for i in range(4):
                    s = PL.first[name] + i
                    act.wait_ge(kstep, step_end(s))
                    for m in range(2):
                        last = act.activation(dst[:, 2 * i + m, 0:S], bank(step_banks(s)[m]), ACT.Sigmoid,
                                              bias=pcol(vec, 2 * i + m))
                    last.then_inc(step_a, 1)
            wait_product(act, "w2")
            for k in range(KT):
                if k >= 2:
                    act.wait_ge(prep_pe, 2 * (k - 2) + 1)
                act.activation(tmp[:, k % 2, :], kf[:, k, :], ACT.Square, scale=pcol("rw_k_k", k)).then_inc(prep_a, 1)
                act.activation(u0[:, k, :], kf[:, k, :], ACT.Copy, scale=pcol("rw_k_k", k)).then_inc(prep_a, 1)
                act.wait_ge(prep_d, 6 * k + 1)
                if k >= 2:
                    act.wait_ge(prep_p, 2 * (k - 2) + 2)
                act.activation(pchunk[:, k, :], u1[:, k, CH - 1:S:CH], ACT.Exp, scale=-EXPW)
                act.activation(tmp[:, 4 + k % 2, :], u1[:, k, :], ACT.Exp, scale=-EXPW).then_inc(prep_a, 1)
                if k >= 2:
                    act.wait_ge(prep_d, 6 * (k - 2) + 6)
                act.activation(tmp[:, 6 + k % 2, :], u1[:, k, :], ACT.Exp, scale=EXPW).then_inc(prep_a, 1)
                act.wait_ge(prep_p, 2 * k + 1)
                act.activation(h_sb[:, k, 0:S], h_sb[:, k, 0:S], ACT.Exp, scale=-EXPW).then_inc(prep_a, 1)
            wait_done(act, ("ksq",))
            rn = xf[0:16, 1, :]
            act.activation(rn, psum[0:16, 4, :], ACT.Sqrt).then_inc(job_a, 1)
            act.wait_ge(kn_f, 1)
            act.activation(mid_hi[0:16, :], rn, ACT.Copy).then_inc(kn_h, 1)
            wait_done(act, ("bonus",))
            act.activation(rt[0:16, :], psum[0:16, 5, :], ACT.Copy).then_inc(job_a, 1)
            for tt in range(TT):
                for i in range(2):
                    if tt:
                        wait_done(act, ("SU", 2 * tt - 1, 1))
                    empty(("bt", tt, i), btok[:, S * i:S * i + S])
                for pair in range(2):
                    gs = (2 * pair, 2 * pair + 1)
                    for g in gs:
                        empty(("T1", tt, g), Tn[:, g % 2, :])
                    for g in gs:
                        key = ("AV", tt, g)
                        wait_done(act, key)
                        if tt:
                            wait_job(act, ("X", 2 * tt - 1, 1))
                        h0 = group_head(g, 0)
                        act.activation(AV[:, :].rearrange("p (h c) -> p h c", h=HEADS)[:, h0:h0 + 7:2, :],
                                       bank(job_banks(key)[0], 256).rearrange("p (h c) -> p h c", h=GROUPS),
                                       ACT.Copy).then_inc(job_a, 1)
                    for lv in range(1, NL):
                        for g in gs:
                            empty(("G", tt, g, lv), Gs[:, g % 2, :])
                for c in (2 * tt, 2 * tt + 1):
                    rb = slice(64 * (c % 2), 64 * (c % 2) + 64)
                    for hh in range(2):
                        key = ("U", c, hh)
                        wait_done(act, key)
                        act.activation(us[rb, S * hh:S * hh + S], psum[rb, job_banks(key)[0], :],
                                       ACT.Copy).then_inc(job_a, 1)
                    key = ("Y", c)
                    wait_done(act, key)
                    act.activation(h_sb[:, :, 1 + CH * c:1 + CH * c + CH],
                                   bank(job_banks(key)[0]).rearrange("p (k c) -> p k c", k=KT),
                                   ACT.Copy).then_inc(job_a, 1)
            act.activation(sg_hi[:, 0, :], sgf[:, 0, :], ACT.Copy)
            act.activation(sg_hi[96:128, 1, :], sgf[96:128, 1, :], ACT.Copy)
            act.activation(bon_hi[:, :], rt[0:16, :], ACT.Copy).then_inc(sg_h, 1)
            high(PL.first_slot["g2"])
            high(PL.first_slot["g2"] + 1)
            for k in range(KT):
                wait_job(act, ("gmean", k))
                if k >= 2:
                    act.wait_ge(gn_pe, k - 1)
                act.activation(pt8[:, k % 2, :], h_sb[:, k, 1:S + 1], ACT.Square).then_inc(gn_q, 1)
            wait_done(act, ("gvar",))
            act.activation(rn, psum[0:16, 5, :], ACT.Sqrt, bias=cst[0:16, C_EPSL:C_EPSL + 1],
                           scale=1.0 / HN).then_inc(job_a, 1)
            act.wait_ge(kn_f, 2)
            act.activation(gn_hi[:, :], rn, ACT.Copy).then_inc(kn_h, 1)
            for k in range(KT):
                wait_job(act, ("grstd", k))
                if k >= 2:
                    act.wait_ge(xf_ready, xf_count(XV["y"], k - 2))
                act.activation(pt8[:, 2 + k % 2, :], h_sb[:, k, 1:S + 1], ACT.Identity, bias=pcol("rw_lnx_b", k),
                               scale=pcol("rw_lnx_w", k)).then_inc(gn_aff, 1)
                empty(("bb", k), pt8[:, 4 + k % 2, :])
                if k >= 1:
                    x_high1(XV["y"], k - 1)
            x_high1(XV["y"], KT - 1)
            for i in range(4):
                if PL.first_slot["o"] + 1 + i < len(PL.slots):
                    high(PL.first_slot["o"] + 1 + i)
            norm_squares(1, XV["ffn0"])
            ffn(0)
            act.wait_ge(lam_row, 1)
            wait_done(act, ("lam",))
            act.activation(col[:, 0:2], psum[:, 7, 0:2], ACT.Exp).then_inc(job_a, 1)
            norm_squares(2, XV["qin"])
            for i in range(PL.count["q"]):
                next_slot(PL.first["q"] + i)
            x_high(XV["kvin"])
            act.wait_ge(xlo_ready, xready(XV["kvin"], KT - 1))

            def att_part(w, n):
                for what, k in ATT_AT.get(n, ()):
                    at = 8 * "qk".index(w)
                    if what == "sq":
                        if k == 0:
                            wait_product(act, "q" if w == "q" else "kk")
                        if k >= 2:
                            act.wait_ge(hn_pe, hn_pe_count(at, k - 2))
                        act.activation(xf[:, k % 2, :], (aq if w == "q" else ak)[:, k, 0:S],
                                       ACT.Square).then_inc(hn_a, 1)
                    elif what == "root":
                        key = ("hsq", w)
                        wait_done(act, key)
                        act.activation(rth[:, :], psum[0:16, job_banks(key)[0], :], ACT.Sqrt,
                                       bias=cst[0:16, C_EPS6:C_EPS6 + 1], scale=1.0 / HN).then_inc(job_a, 1)
                    elif what == "inv":
                        act.wait_ge(kn_f, 3 + at // 8)
                        act.activation(n_hi[:, :], rth[:, :], ACT.Copy).then_inc(kn_h, 1)

            for i in range(PL.count["kk"]):
                next_slot(PL.first["kk"] + i)
                for k in range(KT):
                    att_part("q", 8 * i + k)
            wait_job(act, ("rtT",))
            for i in range(PL.count["kv"]):
                s = PL.first["kv"] + i
                next_slot(s)
                for k in range(KT):
                    att_part("k", 8 * i + k)
                act.wait_ge(kstep, step_end(s))
                for tt in range(TT):
                    last = act.activation(av[:, tt, 256 * i:256 * i + 256],
                                          psum[:, step_banks(s)[tt // 2], 256 * (tt % 2):256 * (tt % 2) + 256],
                                          ACT.Copy, scale=col[:, 24 + tt:25 + tt])
                last.then_inc(step_a, 1)
            for i in range(-2, HEADS // 2 * TT):
                if i + 2 < HEADS // 2 * TT:
                    tq = (i + 2) % TT
                    b = job_banks(("sc", i + 2))
                    act.wait_ge(sc_max, i + 3)
                    if i >= 1:
                        wait_done(act, ("pt", i - 1))
                    for sub in range(2):
                        q = 2 * ((i + 2) % 3) + sub
                        ins = act.activation(Pb[:, q, 0:P * (tq + 1)], psum[:, b[sub], 0:P * (tq + 1)], ACT.Exp,
                                             bias=col[:, 4 + q:5 + q], scale=HN ** -0.5,
                                             accum_out=col[:, 16 + q:17 + q])
                    ins.then_inc(job_a, 1)
                if i >= 0:
                    if i >= 1 and (i - 1) % TT == TT - 1:
                        empty(("ot", (i - 1) // TT), oT[:, (i - 1) // TT, :])
                    tq = i % TT
                    key = ("pt", i)
                    wait_done(act, key)
                    act.activation(PTs[:, i % 2, 0:P * (tq + 1)], bank(job_banks(key)[0], P * (tq + 1)),
                                   ACT.Copy).then_inc(job_a, 1)
            empty(("ot", HEADS // 2 - 1), oT[:, HEADS // 2 - 1, :])
            wait_job(act, ("ot", HEADS // 2 - 1))
            head_scale(oT, KT, 16, ("osq",), 1.0 / P, C_EPS5, kn_f, 5, n_hi)
            for k in range(KT):
                wait_job(act, ("oinv", k))
                x_high1(XV["attn"], k, oT)
            for i in range(PL.count["ao"]):
                next_slot(PL.first["ao"] + i)
            norm_squares(3, XV["ffn1"])
            ffn(1)
            for k in range(KT):
                wait_step(act, PL.first["dn1"] + k // 2)
                x_high1(XV["even"], k, x)
            plain_last("eq", eqk)
            plain_last("ek", eqk[:, 2:4, :])
            s = PL.first["elr"]
            next_slot(s)
            act.wait_ge(kstep, step_end(s))
            act.activation(elr[:, :], psum[0:16, step_banks(s)[0], :], ACT.Copy).then_inc(step_a, 1)
            for m in range(2):
                wait_done(act, ("za", m))
                ins = act.activation(gw[:, m, :], bank(job_banks(("za", m))[0]), ACT.Abs, bias=pcol("l0_b_a_2", m))
            link(ins)
            link(act.activation(gw[:, 0:2, :], gw[:, 0:2, :], ACT.Exp, scale=-1.0))
            act.activation(gw[:, 0:2, :], gw[:, 0:2, :], ACT.Ln, bias=cst[:, CST["ones"]:CST["ones"] + 1]
                           ).then_inc(gl_a, 1)
            plain_last("ev", ev, tokens=True)
            act.wait_ge(gl_d, 2)
            act.activation(gend[:, :, :], gcum[:, :, CH - 1:S:CH], ACT.Exp, scale=1.0 / 16)
            act.activation(gw[:, 0:2, :], gcum[:, :, :], ACT.Exp, scale=1.0 / 16)
            act.activation(gw[:, 2:4, :], gcum[:, :, :], ACT.Exp, scale=-1.0 / 16).then_inc(gl_a, 1)
            plain_last("esv", esv, func=ACT.Gelu_apprx_tanh)

            def even_part(n):
                for what, i in EVEN_AT.get(n, ()):
                    if what == "ks":
                        key = ("gkt", i)
                        wait_done(act, key)
                        if i >= 2:
                            wait_done(act, ("gu", 2 * (i - 2) + 1))
                        act.activation(kt2[:, i % 2, :], bank(job_banks(key)[0], 256), ACT.Copy).then_inc(job_a, 1)
                    elif what == "go":
                        wait_done(act, ("go", i))
                        act.activation(mix[:, 0:4, CH * i:CH * i + CH],
                                       bank(job_banks(("go", i))[0], 256).rearrange("p (h c) -> p h c", h=4),
                                       ACT.Copy).then_inc(job_a, 1)
                    elif what == "sq":
                        if i == 0:
                            wait_job(act, ("go", NCH - 1))
                        else:
                            act.wait_ge(hn_pe, 21 + 2 * i - 1)
                        act.activation(xf[:, 0, :], mix[:, i, :], ACT.Square).then_inc(hn_a, 1)
                        wait_job(act, ("smean", i))
                        if i:
                            act.wait_ge(hn_pe, 21 + 2 * i)
                        act.activation(xf[:, 1, :], esv[:, i, :], ACT.Square).then_inc(hn_a, 1)
                    elif what == "root":
                        for key, dst in (("gosq", rt[0:16, :]), ("svar", elr[:, :])):
                            wait_done(act, (key,))
                            act.activation(dst, psum[0:16, job_banks((key,))[0], :], ACT.Sqrt,
                                           bias=cst[0:16, C_EPS5:C_EPS5 + 1], scale=1.0 / P).then_inc(job_a, 1)
                    elif what == "inv":
                        act.wait_ge(kn_f, 6 + i)
                        if i:
                            wait_done(act, ("gorb", 3))
                        act.activation(en_hi[:, :], (rt[0:16, :], elr[:, :])[i], ACT.Copy).then_inc(kn_h, 1)
                    elif what == "svT":
                        if i >= 2:
                            wait_done(act, ("sg", i - 2))
                        empty(("svT", i), svt[:, i % 2, :])

            for p_, (name, dst, func) in enumerate((("eu", mix[:, 4:8, :], ACT.Gelu_apprx_tanh),
                                                    ("egb", egb, ACT.Silu), ("ega", ega, ACT.Silu))):
                plain_last(name, dst, func=func, parts=lambda n: even_part(16 * p_ + n))
            for k in range(KT):
                if k < 4:
                    act.wait_ge(mix_a, k + 1)
                else:
                    wait_job(act, ("sg", k - 4))
                x_high1(XV["evenmix"], k, mix)
            layer_norm(0)
            odd_angles()
            plain_last("oq", oqk)
            plain_last("ok", oqk[:, 2:4, :])
            plain_last("ov", ov, tokens=True)

            def odd_part(n):
                for what, i in ODD_AT.get(n, ()):
                    if what == "ro":
                        wait_done(act, ("ro", i))
                        act.activation(omix[:, 0:4, P * i:P * i + P],
                                       bank(job_banks(("ro", i))[0]).rearrange("p (h c) -> p h c", h=4),
                                       ACT.Copy).then_inc(job_a, 1)
                    elif what == "sq":
                        wait_job(act, ("rmean", i))
                        if i >= 2:
                            act.wait_ge(hn_pe, 27 + i - 1)
                        act.activation(xf[:, i % 2, :], omix[:, i, :], ACT.Square).then_inc(hn_a, 1)
                    elif what == "inv":
                        wait_done(act, ("rvar",))
                        act.activation(rt[0:16, :], psum[0:16, job_banks(("rvar",))[0], :], ACT.Sqrt,
                                       bias=cst[0:16, C_EPS5:C_EPS5 + 1], scale=1.0 / P).then_inc(job_a, 1)
                        act.wait_ge(kn_f, 8)
                        act.activation(on_hi[:, :], rt[0:16, :], ACT.Copy).then_inc(kn_h, 1)

            for p_, (name, dst, func) in enumerate((("op", opp[:, :, PAD:PAD + S], ACT.Copy),
                                                    ("ogd", ogd, ACT.Silu), ("ogc", ogc, ACT.Silu))):
                plain_last(name, dst, func=func, parts=lambda n: odd_part(16 * p_ + n))
            for k in range(KT):
                if k < 4:
                    act.wait_ge(omix_a, k + 1)
                else:
                    wait_job(act, ("pool", k - 4))
                x_high1(XV["oddmix"], k, omix)
            layer_norm(1)
            for i in range(2):
                for tt in range(0, TT, 2):
                    empty(("out", tt, i), ost[:, tt, S * i:S * i + S])

        @block.vector
        def _(dve):
            seq = [0]

            def link(ins):
                seq[0] += 1
                ins.then_inc(dve_seq, 1)
                dve.wait_ge(dve_seq, seq[0])

            def x_low1(v, k, src=None):
                dve.wait_ge(xhi_ready, xready(v, k))
                f = src[:, k, :] if src is not None else xf[:, (8 * v + k) % 2, :]
                dve.tensor_tensor(X_lo[:, k, :], f, X_hi[:, k, :].bitcast(F32), ALU.subtract).then_inc(xlo_ready, 1)

            def split(v, produce):
                for k in range(KT):
                    if 8 * v + k >= 2:
                        dve.wait_ge(xlo_ready, 8 * v + k - 1)
                    produce(k, xf[:, (8 * v + k) % 2, :]).then_inc(xf_ready, 1)
                    if k:
                        x_low1(v, k - 1)
                x_low1(v, KT - 1)

            def norm_scale(i):
                wait_job(dve, ("rms", i))
                dve.reciprocal(rt[:, :], rt[:, :]).then_inc(rt_ready, 1)
                dve.wait_ge(rt_ready, i + 1)

            def residual_and_split(name, v, gain, i0, i):
                residual(name, range(3))
                wait_step(dve, PL.first[name] + 2)
                for k in range(KT):
                    if k == 6:
                        residual(name, (3,))
                        wait_product(dve, name)
                    dve.wait_ge(xlo_ready, 8 * v + k - 1)
                    dve.tensor_scalar(xf[:, (8 * v + k) % 2, :], x[:, k, :], pcol(gain, i0 + k), None,
                                      ALU.mult).then_inc(xf_ready, 1)
                    if k:
                        x_low1(v, k - 1)
                x_low1(v, KT - 1)
                norm_scale(i)

            def residual(name, steps=range(4)):
                for i in steps:
                    s = PL.first[name] + i
                    dve.wait_ge(kstep, step_end(s))
                    for m in range(2):
                        last = dve.tensor_tensor(x[:, 2 * i + m, :], x[:, 2 * i + m, :], bank(step_banks(s)[m]),
                                                 ALU.add)
                    last.then_inc(step_d, 1)

            def ffn(layer):
                s0 = PL.first[f"gu{layer}"]
                with dve.Fori(0, FT // 2) as i:
                    for j in range(2):
                        b = step_banks(s0 + j)
                        dve.wait_ge(kstep, step_end(s0 + j) + 16 * i)
                        dve.tensor_tensor(sgate[:, j, :], rt[:, :], bank(b[0]), ALU.mult).then_inc(ff_raw, 1)
                        dve.tensor_tensor(xf[:, j, :], rt[:, :], bank(b[1]), ALU.mult).then_inc(step_d, 1)
                        dve.wait_ge(step_d, PL.taken[s0 + j][1] + 2 * i)
                        dve.wait_ge(ff_gate, FT * layer + j + 1 + 2 * i)
                        dve.tensor_tensor(xf[:, j, :], sgate[:, j, :], xf[:, j, :], ALU.mult).then_inc(ff_prod, 1)
                        dve.wait_ge(ff_hi, FT * layer + j + 1 + 2 * i)
                        h1 = bass.ds(2 * i + j, 1)
                        dve.tensor_tensor(hb_lo[:, h1, :], xf[:, j:j + 1, :], hb_hi[:, h1, :].bitcast(F32),
                                          ALU.subtract).then_inc(ff_lo, 1)
                        dve.wait_ge(ff_lo, FT * layer + j + 1 + 2 * i)

            def new_state(old, new, key):
                b = bank(job_banks(key)[0]).rearrange("p (h c) -> p h c", h=4)
                for half in range(2):
                    own = c_("blk")[:, 64 * half:64 * half + 1]
                    if old is not None:
                        ins = dve.scalar_tensor_tensor(out=new[:, half:4:2, :], in0=b[:, half:4:2, :], scalar=own,
                                                       in1=old[:, half:4:2, :], op0=ALU.mult, op1=ALU.add)
                    else:
                        ins = dve.tensor_scalar(new[:, half:4:2, :], b[:, half:4:2, :], own, None, ALU.mult)
                ins.then_inc(job_d, 1)

            def layer_norm(n):
                name = ("eo", "oo")[n]
                for i in range(4):
                    s = PL.first[name] + i
                    dve.wait_ge(kstep, step_end(s))
                    for m in range(2):
                        ins = dve.scalar_tensor_tensor(out=x[:, 2 * i + m, :], in0=x[:, 2 * i + m, :], scalar=ALPHA,
                                                       in1=bank(step_banks(s)[m]), op0=ALU.mult, op1=ALU.add)
                    ins.then_inc(step_d, 1)
                wait_done(dve, ("lm", n))
                dve.tensor_scalar(rt[:, :], bank(job_banks(("lm", n))[0]), 1.0 / D, None, ALU.mult).then_inc(job_d, 1)
                wait_job(dve, ("lm", n))
                for k in range(KT):
                    dve.tensor_tensor(x[:, k, :], x[:, k, :], rt[:, :], ALU.subtract).then_inc(ln_c, 1)
                wait_job(dve, ("lv", n))
                link(dve.reciprocal(rt[:, :], rt[:, :]))
                for k in range(KT):
                    dve.scalar_tensor_tensor(out=x[:, k, :], in0=x[:, k, :], scalar=pcol(f"l{n}_ln_g_2", k),
                                             in1=rt[:, :], op0=ALU.mult, op1=ALU.mult).then_inc(ln_g, 1)
                    if n == 0 and k:
                        x_low1(XV["odd"], k - 1, x)
                if n == 0:
                    x_low1(XV["odd"], KT - 1, x)

            def head_inverse(key, count, hi, lo):
                wait_job(dve, key)
                dve.reciprocal(rt[0:16, :], rt[0:16, :]).then_inc(kn_f, 1)
                dve.wait_ge(kn_h, count)
                dve.tensor_tensor(lo[:, :], rt[0:16, :], hi[:, :].bitcast(F32), ALU.subtract).then_inc(kn_l, 1)

            wait_done(dve, ("xt", KT - 1))
            dve.memset(h_sb[:, :, 0:1], 0.0)
            norm_scale(0)
            wait_job(dve, ("pv",))
            link(dve.tensor_scalar(omu[:, :], pv[:, PV["rw_mu"]:PV["rw_mu"] + 48], -1.0, 1.0, ALU.mult, ALU.add))
            dve.wait_ge(lam_in, 64)
            l4 = lamr[0:1, :].rearrange("p (a b c) -> p a b c", a=2, b=2)
            link(dve.tensor_tensor(lamp[0:1, :].rearrange("p (a c) -> p a c", a=2), l4[:, :, 0, :], l4[:, :, 1, :],
                                   ALU.mult))
            dve.tensor_reduce(col[0:1, 14:16], lamp[0:1, :].rearrange("p (a c) -> p a c", a=2), AX.X,
                              ALU.add).then_inc(lam_row, 1)
            dve.wait_ge(lam_row, 1)
            for k in range(KT):
                ins = dve.scalar_tensor_tensor(out=h_sb[:, k, 1:S + 1], in0=x[:, k, :], scalar=pcol("g_mix", k),
                                               in1=rt[:, :], op0=ALU.mult, op1=ALU.mult)
            link(ins)

            def mixed(mu):
                def produce(k, f):
                    link(dve.tensor_scalar(f, h_sb[:, k, 1:S + 1], omu[:, 8 * mu + k:8 * mu + k + 1], None, ALU.mult))
                    return dve.scalar_tensor_tensor(out=f, in0=h_sb[:, k, 0:S], scalar=pcol("rw_mu", 8 * mu + k),
                                                    in1=f, op0=ALU.mult, op1=ALU.add)
                return produce

            for v, mu in enumerate((MU_K, MU_V, MU_R, MU_G, MU_A, MU_W)):
                split(v, mixed(mu))
            for n, rows in ((1, slice(64, 128)), (2, slice(0, 64))):
                dve.wait_ge(mid_h, n)
                dve.tensor_tensor(mid_lo[rows, :], midf[rows, :], mid_hi[rows, :].bitcast(F32),
                                  ALU.subtract).then_inc(mid_l, 1)
            wait_product(dve, "w2")
            dve.wait_ge(keep_in, 16)
            for k in range(KT):
                dve.tensor_tensor_scan(u1[:, k, :], keep[:, :], h_sb[:, k, 0:S], 0.0, ALU.mult,
                                       ALU.add).then_inc(prep_d, 1)
                dve.tensor_scalar(xf[:, 0, :], af[:, k, :], -1.0, pcol("rw_k_a", k), ALU.add,
                                  ALU.mult).then_inc(prep_d, 1)
                dve.wait_ge(prep_d, 6 * k + 2)
                dve.wait_ge(prep_a, 5 * k + 2)
                dve.scalar_tensor_tensor(out=kf[:, k, :], in0=xf[:, 0, :], scalar=1.0, in1=kf[:, k, :], op0=ALU.add,
                                         op1=ALU.mult).then_inc(prep_d, 1)
                dve.wait_ge(prep_d, 6 * k + 3)
                if k >= 2:
                    dve.wait_ge(prep_pe, 2 * (k - 2) + 2)
                dve.scalar_tensor_tensor(out=tmp[:, 2 + k % 2, :], in0=rf[:, k, :], scalar=pcol("rw_r_k", k),
                                         in1=kf[:, k, :], op0=ALU.mult, op1=ALU.mult).then_inc(prep_d, 1)
                dve.wait_ge(prep_a, 5 * k + 4)
                dve.wait_ge(prep_d, 6 * k + 4)
                dve.tensor_tensor(kf[:, k, :], kf[:, k, :], tmp[:, 6 + k % 2, :], ALU.mult).then_inc(prep_d, 1)
                dve.tensor_tensor(af[:, k, :], af[:, k, :], tmp[:, 6 + k % 2, :], ALU.mult).then_inc(prep_d, 1)
            wait_job(dve, ("ksq",))
            rn = xf[0:16, 1, :]
            link(dve.tensor_scalar(rn, rn, 1e-12, None, ALU.max))
            dve.reciprocal(rn, rn).then_inc(kn_f, 1)
            dve.wait_ge(kn_h, 1)
            dve.tensor_tensor(mid_lo[0:16, :], rn, mid_hi[0:16, :].bitcast(F32), ALU.subtract).then_inc(kn_l, 1)
            dve.wait_ge(prep_a, 5 * KT)
            for k in range(KT):
                wait_done(dve, ("kinv", k))
                dve.tensor_tensor(u0[:, k, :], u0[:, k, :], bank(job_banks(("kinv", k))[0]),
                                  ALU.mult).then_inc(job_d, 1)
                wait_job(dve, ("kinv", k))
                link(dve.tensor_tensor(af[:, k, :], af[:, k, :], u0[:, k, :], ALU.mult))
                ins = dve.scalar_tensor_tensor(out=u0[:, k, :], in0=u0[:, k, :], scalar=-1.0, in1=h_sb[:, k, 0:S],
                                               op0=ALU.mult, op1=ALU.mult)
                ins.then_inc(at_ready, 1)
            dve.wait_ge(lvl_in, 16)
            incl = c_("incl")[:, None, :].to_broadcast([P, GROUPS, P])
            strict = lvl[:, 0:1, :].to_broadcast([P, GROUPS, P])
            blk4 = c_("blk")[:, None, :].to_broadcast([P, 4, P])

            def four(ap):
                return ap.rearrange("p (h c) -> p h c", h=4)

            for tt in range(TT):
                for i in range(2):
                    key = ("kt", tt, i)
                    wait_done(dve, key)
                    if tt:
                        wait_done(dve, ("SU", 2 * tt - 1, 1))
                    dve.tensor_copy(ktok[:, S * i:S * i + S], bank(job_banks(key)[0])).then_inc(job_d, 1)
                for pair in range(2):
                    gs = (2 * pair, 2 * pair + 1)
                    for g in gs:
                        for m, dst, mask in (("At", At[:, g % 2, :], strict), ("Rb", Rb[:, g, :], incl),
                                             ("Ak", Ak[:, g % 2, :], strict), ("Rk", Rk[:, g, :], incl)):
                            key = (m, tt, g)
                            wait_done(dve, key)
                            if m == "At" and (tt or pair):
                                dve.wait_ge(level_ready, (NL - 1) * 2 * (2 * tt + pair))
                            if m in ("Rb", "Rk") and tt:
                                wait_done(dve, ("Y", 2 * tt - 1))
                            if m == "Ak" and (tt or pair):
                                wait_done(dve, ("AV", tt if pair else tt - 1, (g + 2) % 4))
                            dve.tensor_tensor(four(dst), four(bank(job_banks(key)[0])), mask,
                                              ALU.mult).then_inc(job_d, 1)
                    for lv in range(1, NL):
                        for g in gs:
                            if lv < NL - 1:
                                key = ("TG", tt, g, lv)
                                wait_done(dve, key)
                                dve.tensor_tensor(Tn[:, g % 2, :], Tn[:, g % 2, :], bank(job_banks(key)[0]),
                                                  ALU.add).then_inc(job_d, 1)
                            key = ("TGt", tt, g, lv)
                            wait_done(dve, key)
                            dve.tensor_tensor(Tt[:, g, :], Tt[:, g, :], bank(job_banks(key)[0]),
                                              ALU.add).then_inc(job_d, 1)
                for c in (2 * tt, 2 * tt + 1):
                    rb = slice(64 * (c % 2), 64 * (c % 2) + 64)
                    old, new = state[c % 2], state[(c + 1) % 2]
                    for hh in range(2):
                        key = ("X", c, hh)
                        wait_done(dve, key)
                        wait_job(dve, ("AV", tt, 3))
                        if c:
                            wait_done(dve, ("U", c - 1, hh))
                        dve.tensor_tensor(xs[rb, S * hh:S * hh + S], psum[rb, job_banks(key)[0], :],
                                          AV[rb, S * hh:S * hh + S], ALU.add).then_inc(job_d, 1)
                    for hh in range(2):
                        key = ("SU", c, hh)
                        wait_done(dve, key)
                        o4, n4 = old[:, 4 * hh:4 * hh + 4, :], new[:, 4 * hh:4 * hh + 4, :]
                        if c:
                            wait_done(dve, ("Y", c - 1))
                        dve.tensor_tensor(n4, four(bank(job_banks(key)[0])), blk4, ALU.mult).then_inc(job_d, 1)
                        wait_job(dve, key)
                        link(dve.tensor_tensor(n4, n4, o4, ALU.add))
                        dve.tensor_tensor(n4, n4, pchunk[:, 4 * hh:4 * hh + 4, c:c + 1].to_broadcast([P, 4, P]),
                                          ALU.mult).then_inc(s_new, 1)
            dve.wait_ge(sg_h, 1)
            dve.tensor_tensor(sg_lo[:, 0, :], sgf[:, 0, :], sg_hi[:, 0, :].bitcast(F32), ALU.subtract)
            dve.tensor_tensor(sg_lo[96:128, 1, :], sgf[96:128, 1, :], sg_hi[96:128, 1, :].bitcast(F32), ALU.subtract)
            dve.tensor_tensor(bon_lo[:, :], rt[0:16, :], bon_hi[:, :].bitcast(F32), ALU.subtract).then_inc(sg_l, 1)
            for k in range(KT):
                key = ("gmean", k)
                wait_done(dve, key)
                dve.tensor_tensor(h_sb[:, k, 1:S + 1], h_sb[:, k, 1:S + 1], bank(job_banks(key)[0]),
                                  ALU.subtract).then_inc(job_d, 1)
            wait_job(dve, ("gvar",))
            dve.reciprocal(rn, rn).then_inc(kn_f, 1)
            dve.wait_ge(kn_h, 2)
            dve.tensor_tensor(gn_lo[:, :], rn, gn_hi[:, :].bitcast(F32), ALU.subtract).then_inc(kn_l, 1)
            v = XV["y"]
            for k in range(KT):
                key = ("grstd", k)
                wait_done(dve, key)
                dve.tensor_tensor(h_sb[:, k, 1:S + 1], h_sb[:, k, 1:S + 1], bank(job_banks(key)[0]),
                                  ALU.mult).then_inc(job_d, 1)
                key = ("vT", k)
                wait_done(dve, key)
                wait_job(dve, ("bb", k))
                dve.tensor_tensor(pt8[:, 4 + k % 2, :], pt8[:, 4 + k % 2, :], bank(job_banks(key)[0]),
                                  ALU.mult).then_inc(job_d, 1)
                wait_job(dve, key)
                dve.wait_ge(gn_aff, k + 1)
                link(dve.tensor_tensor(pt8[:, 2 + k % 2, :], pt8[:, 2 + k % 2, :], pt8[:, 4 + k % 2, :], ALU.add))
                s = PL.first["g2"] + k // 2
                dve.wait_ge(kstep, step_end(s))
                if k >= 2:
                    dve.wait_ge(xlo_ready, xready(v, k - 2))
                ins = dve.tensor_tensor(xf[:, (8 * v + k) % 2, :], pt8[:, 2 + k % 2, :], bank(step_banks(s)[k % 2]),
                                        ALU.mult)
                ins.then_inc(xf_ready, 1)
                dve.wait_ge(xf_ready, xf_count(v, k))
                if k % 2:
                    dve.sem_inc(step_d, 1)
                if k:
                    x_low1(v, k - 1)
            x_low1(v, KT - 1)
            residual_and_split("o", XV["ffn0"], "g_ffn", 0, 1)
            ffn(0)
            residual_and_split("dn0", XV["qin"], "g_mix", 8, 2)
            wait_job(dve, ("lam",))
            link(dve.tensor_tensor(col[:, 2:3], col[:, 1:2], col[:, 0:1], ALU.subtract))
            dve.tensor_scalar(col[:, 3:4], col[:, 2:3], -LAM_INIT, None, ALU.add)
            link(dve.tensor_scalar(col[:, 12:13], pcol("da_subln_g"), 1.0 - LAM_INIT, None, ALU.mult))

            def scaled(name, dst, steps):
                for i in steps:
                    s = PL.first[name] + i
                    dve.wait_ge(kstep, step_end(s))
                    for m in range(2):
                        ins = dve.tensor_tensor(dst[:, 2 * i + m, :], rt[:, :], bank(step_banks(s)[m]), ALU.mult)
                    ins.then_inc(step_d, 1)

            scaled("q", aq, range(3))
            split(XV["kvin"], lambda k, f: dve.tensor_scalar(f, x[:, k, :], pcol("kv_g", k), None, ALU.mult))
            scaled("q", aq, (3,))
            wait_done(dve, ("rtT",))
            dve.tensor_copy(col[:, 24:28], bank(job_banks(("rtT",))[0], TT)).then_inc(job_d, 1)
            wait_job(dve, ("rtT",))
            dve.wait_ge(rope_in, 16)

            def att_part(n_, w, src, g, n):
                for what, k in ATT_AT.get(n, ()):
                    key = (what, w, k)
                    if what == "inv":
                        wait_job(dve, ("hsq", w))
                        dve.reciprocal(rth[:, :], rth[:, :]).then_inc(kn_f, 1)
                        dve.wait_ge(kn_h, 3 + n_)
                        dve.tensor_tensor(n_lo[:, :], rth[:, :], n_hi[:, :].bitcast(F32),
                                          ALU.subtract).then_inc(kn_l, 1)
                    elif what == "hinv":
                        wait_done(dve, key)
                        dve.scalar_tensor_tensor(out=src[:, k, :], in0=src[:, k, :], scalar=pcol(g),
                                                 in1=bank(job_banks(key)[0]), op0=ALU.mult,
                                                 op1=ALU.mult).then_inc(job_d, 1)
                    elif what == "rot":
                        wait_job(dve, ("hinv", w, k))
                        rotate(n_, src, key, k)

            def rotate(n_, src, key, k):
                link(dve.tensor_tensor(tq2[:, 0, :], src[:, k, :], rope[:, 0, :], ALU.mult))
                wait_done(dve, key)
                dve.tensor_tensor(tq2[:, 1, :], bank(job_banks(key)[0]), rope[:, 1, :], ALU.mult).then_inc(job_d, 1)
                wait_job(dve, key)
                dve.tensor_tensor(src[:, k, :], tq2[:, 0, :], tq2[:, 1, :], ALU.add).then_inc(hn_rot, 1)
                dve.wait_ge(hn_rot, 8 * n_ + k + 1)

            for n in range(32):
                att_part(0, "q", aq, "da_q_norm_g", n)
                if n % 8 == 7:
                    scaled("kk", ak, (n // 8,))
            wait_product(dve, "kk")
            for n in range(32):
                att_part(1, "k", ak, "k_norm_g", n)
            n_i = HEADS // 2 * TT
            for i in range(-2, n_i):
                if i >= 0:
                    N = P * (i % TT + 1)
                    q = 2 * (i % 3)
                    wait_job(dve, ("sc", i))
                    link(dve.reciprocal(col[:, 16 + q:18 + q], col[:, 16 + q:18 + q]))
                    dve.tensor_scalar(Pb[:, q, 0:N], Pb[:, q, 0:N], col[:, 16 + q:17 + q], None, ALU.mult)
                    link(dve.tensor_tensor(col[:, 17 + q:18 + q], col[:, 17 + q:18 + q], col[:, 3:4], ALU.mult))
                    dve.scalar_tensor_tensor(out=Pb[:, q, 0:N], in0=Pb[:, q + 1, 0:N],
                                             scalar=col[:, 17 + q:18 + q], in1=Pb[:, q, 0:N], op0=ALU.mult,
                                             op1=ALU.add).then_inc(pc_ready, 1)
                if i + 2 < n_i:
                    b = job_banks(("sc", i + 2))[0]
                    N = P * ((i + 2) % TT + 1)
                    q = 4 + 2 * ((i + 2) % 3)
                    wait_done(dve, ("sc", i + 2))
                    link(dve.memset(psum[0:64, b:b + 2, N - CH:N], -1e30))
                    link(dve.tensor_reduce(col[:, 14:16], psum[:, b:b + 2, 0:N], AX.X, ALU.max))
                    dve.tensor_scalar(col[:, q:q + 2], col[:, 14:16], -(HN ** -0.5), None,
                                      ALU.mult).then_inc(sc_max, 1)
                    dve.wait_ge(sc_max, i + 3)
            head_inverse(("osq",), 5, n_hi, n_lo)
            for k in range(KT):
                key = ("oinv", k)
                wait_done(dve, key)
                dve.scalar_tensor_tensor(out=oT[:, k, :], in0=oT[:, k, :], scalar=col[:, 12:13],
                                         in1=bank(job_banks(key)[0]), op0=ALU.mult, op1=ALU.mult).then_inc(job_d, 1)
                if k:
                    x_low1(XV["attn"], k - 1, oT)
            x_low1(XV["attn"], KT - 1, oT)
            residual_and_split("ao", XV["ffn1"], "g_ffn", 8, 3)
            ffn(1)
            residual("dn1", range(3))
            for k in range(KT):
                if k == 6:
                    residual("dn1", (3,))
                x_low1(XV["even"], k, x)
            dve.wait_ge(small_in, 64)
            for m in range(2):
                key = ("za", m)
                wait_done(dve, key)
                dve.wait_ge(gl_a, 1)
                dve.tensor_scalar(gw[:, 2 + m, :], bank(job_banks(key)[0]), pcol("l0_b_a_2", m), 0.0, ALU.add,
                                  ALU.min).then_inc(job_d, 1)
                wait_job(dve, key)
                link(dve.tensor_tensor(gw[:, 2 + m, :], gw[:, 2 + m, :], gw[:, m, :], ALU.subtract))
                dve.tensor_tensor_scan(gcum[:, m, :], keep_e[:, :], gw[:, 2 + m, :], 0.0, ALU.mult,
                                       ALU.add).then_inc(gl_d, 1)
            wait_product(dve, "ek")
            dve.wait_ge(gl_a, 2)
            for m in range(2):
                dve.scalar_tensor_tensor(out=eqk[:, m, :], in0=eqk[:, m, :], scalar=HN ** -0.5,
                                         in1=gw[:, m, :], op0=ALU.mult, op1=ALU.mult)
                dve.tensor_tensor(eqk[:, 2 + m, :], eqk[:, 2 + m, :], gw[:, 2 + m, :], ALU.mult).then_inc(gl_d, 1)
            dve.memset(est[0][:, :, :], 0.0).then_inc(g_state, 1)

            def even_part(n):
                for what, i in EVEN_AT.get(n, ()):
                    key = (what, i)
                    if what not in ("ks", "sq", "root", "inv", "wsT", "svT", "go"):
                        wait_done(dve, key)
                        ps = bank(job_banks(key)[0])
                    if what == "ks":
                        key = ("gs", i)
                        wait_done(dve, key)
                        if i >= 2:
                            wait_done(dve, ("go", 2 * (i - 2) + 1))
                        for half in range(2):
                            ins = dve.tensor_tensor(
                                sT[:, i % 2, 256 * half:256 * half + 256].rearrange("p (h c) -> p h c", h=2),
                                bank(job_banks(key)[half], 256).rearrange("p (h c) -> p h c", h=2),
                                c_("incl")[:, None, :].to_broadcast([P, 2, P]), ALU.mult)
                        ins.then_inc(job_d, 1)
                    elif what == "gu":
                        if i:
                            wait_done(dve, ("go", i - 1))
                        dve.wait_ge(g_state, i + 1)
                        old, new = est[i % 2], est[(i + 1) % 2]
                        new_state(old, new, key)
                        wait_job(dve, key)
                        for half in range(2):
                            ins = dve.tensor_tensor(new[:, half:4:2, :], new[:, half:4:2, :],
                                                    gend[:, :, i:i + 1].to_broadcast([P, 2, P]), ALU.mult)
                        ins.then_inc(g_state, 1)
                    elif what == "smean":
                        dve.tensor_tensor(esv[:, i, :], esv[:, i, :], ps, ALU.subtract).then_inc(job_d, 1)
                    elif what == "inv":
                        wait_job(dve, (("gosq",), ("svar",))[i])
                        root = (rt[0:16, :], elr[:, :])[i]
                        dve.reciprocal(root, root).then_inc(kn_f, 1)
                        dve.wait_ge(kn_h, 6 + i)
                        dve.tensor_tensor(en_lo[:, :], root, en_hi[:, :].bitcast(F32), ALU.subtract).then_inc(kn_l, 1)
                    elif what == "wsT":
                        key = ("wsT",)
                        wait_done(dve, key)
                        dve.tensor_tensor(wsT[:, :, :], bank(job_banks(key)[0]).rearrange("p (g c) -> p g c", g=4),
                                          c_("causal")[:, None, :].to_broadcast([P, 4, P]), ALU.mult
                                          ).then_inc(job_d, 1)
                    elif what == "gorb":
                        dve.scalar_tensor_tensor(out=mix[:, i, :], in0=mix[:, i, :],
                                                 scalar=pcol("l0_gla_norm_g_2", i), in1=ps, op0=ALU.mult,
                                                 op1=ALU.mult).then_inc(job_d, 1)
                    elif what == "srb":
                        dve.scalar_tensor_tensor(out=esv[:, i, :], in0=esv[:, i, :],
                                                 scalar=pcol("l0_sgu_ln_g_2", i), in1=ps, op0=ALU.mult,
                                                 op1=ALU.mult).then_inc(job_d, 1)
                        wait_job(dve, key)
                        dve.tensor_scalar(esv[:, i, :], esv[:, i, :], pcol("l0_sgu_ln_b_2", i), None,
                                          ALU.add).then_inc(sv_ready, 1)
                    elif what == "sg":
                        dve.wait_ge(gate_p, i + 1)
                        dve.tensor_tensor(mix[:, 4 + i, :], mix[:, 4 + i, :], ps, ALU.mult).then_inc(job_d, 1)

            for n in range(48):
                even_part(n)
            wait_product(dve, "ega")
            wait_job(dve, ("gorb", 3))
            for g in range(4):
                dve.tensor_tensor(mix[:, g, :], mix[:, g, :], ega[:, g, :], ALU.mult).then_inc(mix_a, 1)
            for k in range(KT):
                x_low1(XV["evenmix"], k, mix)
            layer_norm(0)
            dve.wait_ge(pos_in, 16)
            link(dve.tensor_copy(orw[:, 0, :], posi[:, :]))
            link(dve.tensor_scalar(orw[:, 0, :], orw[:, 0, :], cst[:, C_INVF:C_INVF + 1], None, ALU.mult))
            link(dve.tensor_scalar(orw[:, 1, :], orw[:, 0, :], 1.0 / (2.0 * np.pi), None, ALU.mult))
            link(dve.tensor_scalar(orw[:, 1, :], orw[:, 1, :], ROUND, None, ALU.add))
            link(dve.tensor_scalar(orw[:, 1, :], orw[:, 1, :], -ROUND, None, ALU.add))
            for part in TWO_PI:
                link(dve.scalar_tensor_tensor(out=orw[:, 0, :], in0=orw[:, 1, :], scalar=-part, in1=orw[:, 0, :],
                                              op0=ALU.mult, op1=ALU.add))
            dve.tensor_scalar(orw[:, 0, :], orw[:, 0, :], 3.1415925, -3.1415925, ALU.min, ALU.max).then_inc(ang_d, 1)
            dve.wait_ge(ang_a, 1)
            link(dve.tensor_tensor(csn[:, 0, :], csn[:, 0, :], csn[:, 0, :], ALU.mult))
            link(dve.tensor_scalar(csn[:, 0, :], csn[:, 0, :], -2.0, 1.0, ALU.mult, ALU.add))
            wait_product(dve, "ok")
            dve.wait_ge(odd_in, 32)
            dve.memset(est[0][:, :, :], 0.0).then_inc(r_state, 1)

            def odd_part(n):
                for what, i in ODD_AT.get(n, ()):
                    key = (what, i)
                    if what in ("rt", "ru", "pool", "rmean", "rrb"):
                        wait_done(dve, key)
                        ps = bank(job_banks(key)[0])
                    if what == "rt":
                        dve.tensor_tensor(orw[:, 1, :], ps, csn[:, 1, :], ALU.mult).then_inc(job_d, 1)
                        link(dve.tensor_tensor(orw[:, 0, :], oqk[:, i, :], csn[:, 0, :], ALU.mult))
                        ins = dve.tensor_tensor(oqk[:, i, :], orw[:, 0, :], orw[:, 1, :], ALU.add)
                        if i < 2:
                            link(ins)
                            ins = dve.tensor_tensor(oqi[:, i, :], oqk[:, i, :],
                                                    cret[:, 4 * P + S * i:4 * P + S * i + S], ALU.mult)
                        ins.then_inc(rot_done, 1)
                        dve.wait_ge(rot_done, i + 1)
                    elif what == "ks":
                        key = ("rkt", i)
                        wait_done(dve, key)
                        if i >= 2:
                            wait_done(dve, ("ro", i - 2))
                        dve.tensor_tensor(kt2[:, i % 2, :].rearrange("p (h c) -> p h c", h=4),
                                          bank(job_banks(key)[0], 256).rearrange("p (h c) -> p h c", h=4),
                                          cst[:, C_WST:C_WST + 4][:, :, None].to_broadcast([P, 4, HN]),
                                          ALU.mult).then_inc(job_d, 1)
                        key = ("rs", i)
                        wait_done(dve, key)
                        for half in range(2):
                            q = slice(256 * half, 256 * half + 256)
                            ins = dve.tensor_tensor(sT[:, i % 2, q], bank(job_banks(key)[half], 256), cret[:, q],
                                                    ALU.mult)
                        ins.then_inc(job_d, 1)
                    elif what == "ru":
                        dve.wait_ge(r_state, i + 1)
                        if i:
                            wait_done(dve, ("ro", i - 1))
                        old, new = est[i % 2], est[(i + 1) % 2]
                        new_state(None, new, key)
                        wait_job(dve, key)
                        for h in range(4):
                            ins = dve.scalar_tensor_tensor(out=new[:, h, :], in0=old[:, h, :],
                                                           scalar=GAMMA_CHUNK[h], in1=new[:, h, :],
                                                           op0=ALU.mult, op1=ALU.add)
                        ins.then_inc(r_state, 1)
                    elif what == "win":
                        w = POOL_WINDOWS[i]
                        dve.wait_ge(win_p, i + 1)
                        src = psh[:, i % 2, PAD:PAD + S]
                        dve.scalar_tensor_tensor(out=omix[:, 4 + i, 16:S], in0=src[:, 16:S], scalar=1.0 / w,
                                                 in1=opp[:, i, PAD + 16:PAD + S], op0=ALU.mult, op1=ALU.subtract)
                        if i:
                            dve.wait_ge(win_d, i)
                        link(dve.tensor_tensor(pool16[:, :], src[:, 0:16],
                                               cst[:, C_CNT + 16 * i:C_CNT + 16 * i + 16], ALU.mult))
                        dve.tensor_tensor(omix[:, 4 + i, 0:16], pool16[:, :], opp[:, i, PAD:PAD + 16],
                                          ALU.subtract).then_inc(win_d, 1)
                    elif what == "pool":
                        wait_product(dve, "ogd")
                        dve.scalar_tensor_tensor(out=omix[:, 4 + i, :], in0=ps, scalar=pcol("l1_pool_scale_2", i),
                                                 in1=ogd[:, i, :], op0=ALU.mult, op1=ALU.mult).then_inc(job_d, 1)
                    elif what == "rmean":
                        dve.tensor_tensor(omix[:, i, :], omix[:, i, :], ps, ALU.subtract).then_inc(job_d, 1)
                    elif what == "inv":
                        head_inverse(("rvar",), 8, on_hi, on_lo)
                    elif what == "rrb":
                        dve.scalar_tensor_tensor(out=omix[:, i, :], in0=omix[:, i, :],
                                                 scalar=pcol("l1_ret_norm_g_2", i), in1=ps, op0=ALU.mult,
                                                 op1=ALU.mult).then_inc(job_d, 1)

            for n in range(48):
                odd_part(n)
            wait_product(dve, "ogc")
            wait_job(dve, ("rrb", 3))
            for h in range(4):
                dve.tensor_tensor(omix[:, h, :], omix[:, h, :], ogc[:, h, :], ALU.mult).then_inc(omix_a, 1)
            for k in range(KT):
                x_low1(XV["oddmix"], k, omix)
            layer_norm(1)
            for i in range(2):
                for tt in range(1, TT, 2):
                    key = ("out", tt, i)
                    wait_done(dve, key)
                    dve.tensor_copy(ost[:, tt, S * i:S * i + S], bank(job_banks(key)[0])).then_inc(job_d, 1)

        @block.tensor
        def _(pe):
            order = [0]

            def begin(key):
                assert JB.order[order[0]] == key, (JB.order[order[0]], key)
                order[0] += 1
                wait_banks(pe, key)
                return job_banks(key)[0]

            def three(ps, w, xx, start, stop):
                (wh, wl), (xh, xl) = w, xx
                pe.matmul(ps, wh, xh, start=start, stop=False, skip_group_check=True)
                pe.matmul(ps, wh, xl, start=False, stop=False, skip_group_check=True)
                return pe.matmul(ps, wl, xh, start=False, stop=stop, skip_group_check=True)

            def two(ps, w, xx):
                pe.matmul(ps, w, xx[0], start=True, stop=False, skip_group_check=True)
                return pe.matmul(ps, w, xx[1], start=False, stop=True, skip_group_check=True)

            def features(s, v=None, xh=None, xl=None, m_count=2, cols=None, dyn=0, check=True,
                         tile_ready=None, parts=None):
                name, at, n_slots, ks = PL.steps[s]
                if check:
                    wait_banks(pe, ("step", s))
                xh, xl = (X_hi, X_lo) if xh is None else (xh, xl)
                b = step_banks(s)
                for k in range(ks):
                    if parts is not None:
                        parts(k)
                    n = at + k // 8
                    if k % 8 == 0:
                        pe.wait_ge(lo_ready, n + 1 + dyn)
                    if tile_ready is not None:
                        pe.wait_ge(tile_ready[0], tile_ready[1] + k + 1)
                    if v is not None:
                        pe.wait_ge(xlo_ready, xready(v, k))
                    whi, wlo = wv(w_hi[n % 2]), wv(w_lo[n % 2])
                    for m in range(m_count):
                        c = slice(128 * m, 128 * m + 128) if cols is None else cols[m]
                        last = three(bank(b[m]), (whi[:, k % 8, c], wlo[:, k % 8, c]), (xh[:, k, :], xl[:, k, :]),
                                     k == 0, k == ks - 1)
                    last.then_inc(kstep, 1)

            def ffn(layer):
                s0, v = PL.first[f"gu{layer}"], XV[f"ffn{layer}"]
                with pe.Fori(0, FT // 2) as i:
                    for j in range(2):
                        pe.wait_ge(step_d, PL.taken[s0 + j][1] - 2 + 2 * i)
                        features(s0 + j, v if j == 0 else None, dyn=2 * i, check=False)
                s0 = PL.first[f"dn{layer}"]
                with pe.Fori(0, 2) as i:
                    for j in range(2):
                        pe.wait_ge(step_d, PL.taken[s0 + j][1] - 2 + 2 * i)
                        features(s0 + j, None, hb_hi, hb_lo, dyn=6 * i, check=False,
                                 tile_ready=(ff_lo, FT * layer) if j == 0 else None)

            def tokens(s, v=None, parts=None):
                name, at, n_slots, ks = PL.steps[s]
                wait_banks(pe, ("step", s))
                b = step_banks(s)
                pe.wait_ge(lo_ready, at + 1)
                whi, wlo = wv(w_hi[at % 2]), wv(w_lo[at % 2])
                for k in range(ks):
                    if parts is not None:
                        parts(k)
                    if v is not None:
                        pe.wait_ge(xlo_ready, xready(v, k))
                    for m in range(2):
                        for r in range(2):
                            tk = slice(P * (2 * m + r), P * (2 * m + r) + P)
                            last = three(psum[:, b[m], 256 * r:256 * r + 256], (X_hi[:, k, tk], X_lo[:, k, tk]),
                                         (whi[:, k, :], wlo[:, k, :]), k == 0 and r == 0, k == ks - 1)
                    last.then_inc(kstep, 1)

            def product(name, v, kind=None):
                for i in range(PL.count[name]):
                    (kind or features)(PL.first[name] + i, v if i == 0 else None)

            def norm_sum(i):
                begin(("rms", i))
                for k in range(KT):
                    pe.wait_ge(sq_ready, 8 * i + k + 1)
                    ins = pe.matmul(bank(6), c_("ones"), square_buffer(i)[:, k % 2, :], start=k == 0, stop=k == KT - 1)
                    ins.then_inc(sq_used if k < KT - 1 else job_done, 1)

            def head_sum(key, n, at, sel):
                b = begin(key)
                for k in range(n):
                    pe.wait_ge(hn_a, at + k + 1)
                    pe.matmul(psum[0:16, b, :], c_(sel, 16, 16 * k), xf[:, k % 2, :], start=k == 0,
                              stop=k == n - 1).then_inc(hn_pe if k < n - 1 else job_done, 1)

            pe.wait_ge(cst_in, 16)
            for k in range(KT):
                pe.wait_ge(x_in[k // 2], 16)
                b = begin(("xt", k))
                for tt in range(TT):
                    ins = pe.transpose(psum[:, b, P * tt:P * tt + P], xtok[:, tt, P * k:P * k + P], c_("ident"))
                ins.then_inc(job_done, 1)
            norm_sum(0)
            pe.wait_ge(rows_in, 16 * (len(ROWS_A) + len(ROWS_B) + 2))
            b = begin(("pv",))
            pe.transpose(psum[:, b, 0:P], prow[0][:, :], c_("ident"))
            pe.transpose(psum[:, b, P:P + NROWS_B], prow[1][:, :], cst[0:NROWS_B, CST["ident"]:CST["ident"] + NROWS_B]
                         ).then_inc(job_done, 1)
            product("k", 0)
            product("v", 1, tokens)
            product("r", 2)
            features(PL.first["g1"], 3, cols=(slice(0, 128), slice(32, 160)))
            features(PL.first["a1"], 4, m_count=1)
            features(PL.first["w1"], 5, m_count=1)
            for name, rows, n in (("a2", slice(64, 128), 1), ("w2", slice(0, 64), 2)):
                for i in range(4):
                    s = PL.first[name] + i
                    wait_banks(pe, ("step", s))
                    at = PL.steps[s][1]
                    if i == 0:
                        pe.wait_ge(lo_ready, at + 1)
                        pe.wait_ge(mid_l, n)
                    for m in range(2):
                        c = slice(P * (2 * i + m), P * (2 * i + m) + P)
                        ins = three(bank(step_banks(s)[m]), (w_hi[at % 2][rows, c], w_lo[at % 2][rows, c]),
                                    (mid_hi[rows, :], mid_lo[rows, :]), True, True)
                    ins.then_inc(kstep, 1)
            wait_banks(pe, ("ksq",))
            wait_banks(pe, ("bonus",))
            for k in range(KT):
                sel = c_("sel64", 16, 16 * k)
                pe.wait_ge(prep_a, 5 * k + 1)
                ins = pe.matmul(psum[0:16, 4, :], sel, tmp[:, k % 2, :], start=k == 0, stop=k == KT - 1)
                ins.then_inc(prep_pe if k < KT - 1 else job_done, 1)
                pe.wait_ge(prep_d, 6 * k + 4)
                ins = pe.matmul(psum[0:16, 5, :], sel, tmp[:, 2 + k % 2, :], start=k == 0, stop=k == KT - 1)
                ins.then_inc(prep_pe if k < KT - 1 else job_done, 1)
            order[0] += 2
            pe.wait_ge(heads_ready, 1)
            pe.wait_ge(kn_l, 1)
            for k in range(KT):
                b = begin(("kinv", k))
                two(bank(b), heads_r[:, P * k:P * k + P], (mid_hi[0:16, :], mid_lo[0:16, :])).then_inc(job_done, 1)
            pe.wait_ge(at_ready, KT)
            pe.wait_ge(prep_p, 2 * KT)
            pe.wait_ge(zero_ready, 1)
            n_t = 0
            n_lv = 0
            for tt in range(TT):
                tk = slice(P * tt, P * tt + P)
                for name, src in (("bt", af), ("kt", kf)):
                    for i in range(2):
                        b = begin((name, tt, i))
                        for j in range(4):
                            ins = pe.transpose(psum[:, b, P * j:P * j + P], src[:, 4 * i + j, tk], c_("ident"))
                        ins.then_inc(job_done, 1)
                for pair in range(2):
                    gs = (2 * pair, 2 * pair + 1)
                    for g in gs:
                        for m, left, right in (("At", af, u0), ("Rb", af, rf), ("Ak", kf, u0), ("Rk", kf, rf)):
                            b = begin((m, tt, g))
                            for j in range(4):
                                hd = group_head(g, j)
                                rows = slice(64 * (hd % 2), 64 * (hd % 2) + 64)
                                ins = pe.matmul(psum[:, b, P * j:P * j + P], left[rows, hd // 2, tk],
                                                right[rows, hd // 2, tk], start=True, stop=True,
                                                skip_group_check=True)
                            ins.then_inc(job_done, 1)
                    for g in gs:
                        n_t += 1
                        pe.wait_ge(t_init, n_t)
                        b = begin(("T1", tt, g))
                        for j in range(4):
                            ins = pe.transpose(psum[:, b, P * j:P * j + P], Tt[:, g, P * j:P * j + P], c_("ident"))
                        ins.then_inc(job_done, 1)
                    for g in gs:
                        b = begin(("AV", tt, g))
                        wait_job(pe, ("Ak", tt, g))
                        for j in range(4):
                            hd = group_head(g, j)
                            ins = pe.matmul(psum[:, b, HN * j:HN * j + HN], Ak[:, g % 2, P * j:P * j + P],
                                            vt[:, tt, HN * hd:HN * hd + HN], start=True, stop=True)
                        ins.then_inc(job_done, 1)
                    for lv in range(1, NL):
                        for g in gs:
                            n_lv += 1
                            pe.wait_ge(level_ready, n_lv)
                            wait_job(pe, ("T1", tt, g) if lv == 1 else ("TG", tt, g, lv - 1))
                            b = begin(("G", tt, g, lv))
                            for j in range(4):
                                c = slice(P * j, P * j + P)
                                ins = pe.matmul(psum[:, b, c], Lm[:, g % 2, c], Tn[:, g % 2, c], start=True, stop=True)
                            ins.then_inc(job_done, 1)
                        for g in gs:
                            wait_job(pe, ("G", tt, g, lv))
                            if lv > 1:
                                wait_job(pe, ("TGt", tt, g, lv - 1))
                            if lv < NL - 1:
                                b = begin(("TG", tt, g, lv))
                                for j in range(4):
                                    c = slice(P * j, P * j + P)
                                    ins = pe.matmul(psum[:, b, c], Tt[:, g, c], Gs[:, g % 2, c], start=True, stop=True)
                                ins.then_inc(job_done, 1)
                            b = begin(("TGt", tt, g, lv))
                            for j in range(4):
                                c = slice(P * j, P * j + P)
                                ins = pe.matmul(psum[:, b, c], Gs[:, g % 2, c], Tt[:, g, c], start=True, stop=True)
                            ins.then_inc(job_done, 1)
                for c in (2 * tt, 2 * tt + 1):
                    r0 = 64 * (c % 2)
                    rb = slice(r0, r0 + 64)
                    ck = slice(CH * c, CH * c + CH)
                    old = state[c % 2]
                    for hh in range(2):
                        if c:
                            pe.wait_ge(s_new, 2 * (c - 1) + hh + 1)
                        b = begin(("X", c, hh))
                        for j in range(4):
                            ins = pe.matmul(psum[rb, b, P * j:P * j + P], u0[:, 4 * hh + j, ck], old[:, 4 * hh + j, :],
                                            start=True, stop=True)
                        ins.then_inc(job_done, 1)
                    for hh in range(2):
                        wait_job(pe, ("X", c, hh))
                        if c % 2 == 0:
                            wait_job(pe, ("TGt", tt, 3, NL - 1))
                        b = begin(("U", c, hh))
                        for j in range(8):
                            hd = 8 * hh + j
                            g, i = head_group(hd)
                            ins = pe.matmul(psum[rb, b, HN * j:HN * j + HN], Tt[rb, g, P * i + r0:P * i + r0 + 64],
                                            xs[rb, HN * hd:HN * hd + HN], start=True, stop=True)
                        ins.then_inc(job_done, 1)
                    for hh in range(2):
                        wait_job(pe, ("U", c, hh))
                        b = begin(("SU", c, hh))
                        for j in range(4):
                            q = slice(P * (4 * hh + j), P * (4 * hh + j) + P)
                            pe.matmul(psum[:, b, P * j:P * j + P], btok[rb, q], us[rb, q], start=True, stop=False,
                                      skip_group_check=True)
                            ins = pe.matmul(psum[:, b, P * j:P * j + P], ktok[rb, q], vt[rb, tt, q], start=False,
                                            stop=True, skip_group_check=True)
                        ins.then_inc(job_done, 1)
                    b = begin(("Y", c))
                    for pr in range(KT):
                        o = slice(CH * pr, CH * pr + CH)
                        pe.matmul(psum[:, b, o], old[:, pr, :], rf[:, pr, ck], start=True, stop=False,
                                  skip_group_check=True)
                        for m, left in ((Rb, us), (Rk, vt[:, tt, :])):
                            for half in range(2):
                                hd = 2 * pr + half
                                g, i = head_group(hd)
                                ins = pe.matmul(psum[64 * half:64 * half + 64, b, o], left[:, HN * hd:HN * hd + HN],
                                                m[:, g, P * i + r0:P * i + r0 + 64],
                                                start=False, stop=m is Rk, skip_group_check=True)
                    ins.then_inc(job_done, 1)
            def gvar(k):
                if k == 0:
                    wait_banks(pe, ("gvar",))
                pe.wait_ge(gn_q, k + 1)
                pe.matmul(psum[0:16, 5, :], c_("sel64", 16, 16 * k), pt8[:, k % 2, :], start=k == 0,
                          stop=k == KT - 1).then_inc(gn_pe if k < KT - 1 else job_done, 1)

            wait_job(pe, ("Y", NCH - 1))
            for k in range(KT):
                b = begin(("gmean", k))
                pe.matmul(bank(b), c_("blkmean"), h_sb[:, k, 1:S + 1], start=True, stop=True).then_inc(job_done, 1)
                if k:
                    gvar(k - 1)
            gvar(KT - 1)
            order[0] += 1
            pe.wait_ge(kn_l, 2)
            pe.wait_ge(sg_l, 1)
            for k in range(KT):
                b = begin(("grstd", k))
                two(bank(b), heads_r[:, P * k:P * k + P], (gn_hi[:, :], gn_lo[:, :])).then_inc(job_done, 1)
                b = begin(("vT", k))
                for tt in range(TT):
                    ins = pe.transpose(psum[:, b, P * tt:P * tt + P], vt[:, tt, P * k:P * k + P], c_("ident"))
                ins.then_inc(job_done, 1)
                b = begin(("bb", k))
                two(bank(b), heads_r[:, P * k:P * k + P], (bon_hi[:, :], bon_lo[:, :])).then_inc(job_done, 1)
                if k % 2 == 0:
                    s = PL.first["g2"] + k // 2
                    wait_banks(pe, ("step", s))
                    at = PL.steps[s][1]
                    pe.wait_ge(lo_ready, at + 1)
                    for m in range(2):
                        c = slice(P * (k + m), P * (k + m) + P)
                        c2 = slice(1024 + P * (k + m), 1024 + P * (k + m) + P)
                        three(bank(step_banks(s)[m]), (w_hi[at % 2][:, c], w_lo[at % 2][:, c]),
                              (sg_hi[:, 0, :], sg_lo[:, 0, :]), True, False)
                        ins = three(bank(step_banks(s)[m]), (w_hi[at % 2][96:128, c2], w_lo[at % 2][96:128, c2]),
                                    (sg_hi[96:128, 1, :], sg_lo[96:128, 1, :]), False, True)
                    ins.then_inc(kstep, 1)
            product("o", XV["y"])
            norm_sum(1)
            ffn(0)
            pe.wait_ge(lam_row, 1)
            b = begin(("lam",))
            pe.matmul(psum[:, b, 0:2], cst[0:1, CST["ones"]:CST["ones"] + P], col[0:1, 14:16], start=True,
                      stop=True).then_inc(job_done, 1)
            norm_sum(2)
            product("q", XV["qin"])
            pe.wait_ge(rt_ready, 3)
            b = begin(("rtT",))
            for tt in range(TT):
                ins = pe.matmul(psum[:, b, tt:tt + 1], rt[0:1, P * tt:P * tt + P],
                                cst[0:1, CST["ones"]:CST["ones"] + 1], start=True, stop=True)
            ins.then_inc(job_done, 1)

            def att_part(w, src, n):
                for what, k in ATT_AT.get(n, ()):
                    at = 8 * "qk".index(w)
                    if what == "sq":
                        if k == 0:
                            wait_banks(pe, ("hsq", w))
                        elif k == KT - 1:
                            order[0] += 1
                        pe.wait_ge(hn_a, at + k + 1)
                        pe.matmul(psum[0:16, job_banks(("hsq", w))[0], :], c_("sel64", 16, 16 * k),
                                  xf[:, k % 2, :], start=k == 0, stop=k == KT - 1
                                  ).then_inc(hn_pe if k < KT - 1 else job_done, 1)
                    elif what == "hinv":
                        pe.wait_ge(kn_l, 3 + at // 8)
                        b = begin(("hinv", w, k))
                        two(bank(b), heads_r[:, P * k:P * k + P], (n_hi[:, :], n_lo[:, :])).then_inc(job_done, 1)
                    elif what == "rot":
                        wait_job(pe, ("hinv", w, k))
                        b = begin(("rot", w, k))
                        pe.matmul(bank(b), c_("rot1"), src[:, k, :], start=True, stop=True).then_inc(job_done, 1)

            for i in range(4):
                features(PL.first["kk"] + i, XV["kvin"] if i == 0 else None,
                         parts=lambda k: att_part("q", aq, 8 * i + k))
            for i in range(4):
                tokens(PL.first["kv"] + i, parts=lambda k: att_part("k", ak, 8 * i + k))
            pe.wait_ge(hn_rot, 16)
            n_i = HEADS // 2 * TT

            def scores(i):
                hd, tq = i // TT, i % TT
                b = begin(("sc", i))
                for sub in range(2):
                    rows = slice(64 * sub, 64 * sub + 64)
                    ins = pe.matmul(psum[:, b + sub, 0:P * (tq + 1)], aq[rows, hd, P * tq:P * tq + P],
                                    ak[rows, hd, 0:P * (tq + 1)], start=True, stop=True)
                ins.then_inc(job_done, 1)

            def values(i):
                hd, tq = i // TT, i % TT
                key = ("ot", hd)
                b = job_banks(key)[0]
                if tq == 0:
                    wait_banks(pe, key)
                wait_job(pe, ("pt", i))
                for kt in range(tq + 1):
                    ins = pe.matmul(psum[:, b, P * tq:P * tq + P], av[:, kt, P * hd:P * hd + P],
                                    PTs[:, i % 2, P * kt:P * kt + P], start=kt == 0, stop=kt == tq)
                if tq == TT - 1:
                    assert JB.order[order[0]] == key
                    order[0] += 1
                    ins.then_inc(job_done, 1)

            scores(0)
            scores(1)
            for i in range(n_i):
                if i + 2 < n_i:
                    scores(i + 2)
                pe.wait_ge(pc_ready, i + 1)
                if i >= 1:
                    values(i - 1)
                b = begin(("pt", i))
                for kt in range(i % TT + 1):
                    ins = pe.transpose(psum[:, b, P * kt:P * kt + P], Pb[:, 2 * (i % 3), P * kt:P * kt + P],
                                       c_("ident"))
                ins.then_inc(job_done, 1)
            values(n_i - 1)
            head_sum(("osq",), KT, 16, "sel128")
            pe.wait_ge(kn_l, 5)
            for k in range(KT):
                b = begin(("oinv", k))
                two(bank(b), heads_r[:, P * k:P * k + P], (n_hi[:, :], n_lo[:, :])).then_inc(job_done, 1)
            product("ao", XV["attn"])
            norm_sum(3)
            ffn(1)
            product("eq", XV["even"])
            product("ek", None)
            features(PL.first["elr"], None, m_count=1)
            wait_product(pe, "elr")
            pe.wait_ge(small_in, 64)
            for m in range(2):
                b = begin(("za", m))
                pe.matmul(bank(b), wa2[:, P * m:P * m + P], elr[:, :], start=True, stop=True).then_inc(job_done, 1)
            product("ev", None, tokens)
            product("esv", None)

            def keys_and_scores(name, tt, qk):
                tk = slice(P * tt, P * tt + P)
                b = begin((name + "kt", tt))
                for m in range(2):
                    ins = pe.transpose(psum[:, b, P * m:P * m + P], qk[:, 2 + m, tk], c_("ident"))
                ins.then_inc(job_done, 1)
                b = begin((name + "s", tt))
                for half in range(2):
                    rows = slice(64 * half, 64 * half + 64)
                    for m in range(2):
                        ins = pe.matmul(psum[:, b + half, P * m:P * m + P], qk[rows, 2 + m, tk], qk[rows, m, tk],
                                        start=True, stop=True)
                ins.then_inc(job_done, 1)

            def state_update(key, tt, rows, v):
                b = begin(key)
                for h in range(4):
                    ins = pe.matmul(psum[:, b, P * h:P * h + P], kt2[rows, tt % 2, P * (h // 2):P * (h // 2) + P],
                                    v[rows, tt, P * h:P * h + P], start=True, stop=True)
                ins.then_inc(job_done, 1)

            def outputs(key, tt, tok, state_, q, v):
                b = begin(key)
                n = tok.stop - tok.start
                for h in range(4):
                    o = psum[:, b, n * h:n * h + n]
                    pe.matmul(o, state_[:, h, :], q[:, h // 2, P * tt + tok.start:P * tt + tok.stop], start=True,
                              stop=False)
                    at = P * HEAD_SLOT[h]
                    ins = pe.matmul(o, v[:, tt, P * h:P * h + P], sT[:, tt % 2, at + tok.start:at + tok.stop],
                                    start=False, stop=True)
                ins.then_inc(job_done, 1)

            def even_part(n):
                for what, i in EVEN_AT.get(n, ()):
                    if what == "ks":
                        pe.wait_ge(gl_d, 4)
                        keys_and_scores("g", i, eqk)
                    elif what == "gu":
                        wait_job(pe, ("gkt", i // 2))
                        state_update(("gu", i), i // 2, slice(64 * (i % 2), 64 * (i % 2) + 64), ev)
                    elif what == "go":
                        wait_job(pe, ("gs", i // 2))
                        pe.wait_ge(g_state, i + 1)
                        outputs(("go", i), i // 2, slice(64 * (i % 2), 64 * (i % 2) + 64), est[i % 2], eqk, ev)
                    elif what == "smean":
                        b = begin(("smean", i))
                        pe.matmul(bank(b), c_("allmean"), esv[:, i, :], start=True, stop=True).then_inc(job_done, 1)
                    elif what == "sq":
                        if i == 0:
                            wait_banks(pe, ("gosq",))
                            wait_banks(pe, ("svar",))
                        for q, key in enumerate((("gosq",), ("svar",))):
                            pe.wait_ge(hn_a, 24 + 2 * i + q + 1)
                            pe.matmul(psum[0:16, job_banks(key)[0], :], c_("sel128", 16, 16 * i), xf[:, q, :],
                                      start=i == 0, stop=i == 3).then_inc(hn_pe if i < 3 else job_done, 1)
                        if i == 3:
                            order[0] += 2
                    elif what == "wsT":
                        b = begin(("wsT",))
                        for g in range(4):
                            ins = pe.transpose(psum[:, b, P * g:P * g + P], ws[:, g, :], c_("ident"))
                        ins.then_inc(job_done, 1)
                    elif what in ("gorb", "srb"):
                        pe.wait_ge(kn_l, 6 if what == "gorb" else 7)
                        b = begin((what, i))
                        two(bank(b), heads_r[:, P * i:P * i + P], (en_hi[:, :], en_lo[:, :])).then_inc(job_done, 1)
                    elif what == "svT":
                        pe.wait_ge(sv_ready, i + 1)
                        b = begin(("svT", i))
                        for tt in range(TT):
                            ins = pe.transpose(psum[:, b, P * tt:P * tt + P], esv[:, i, P * tt:P * tt + P],
                                               c_("ident"))
                        ins.then_inc(job_done, 1)
                    elif what == "sg":
                        wait_job(pe, ("svT", i))
                        wait_job(pe, ("wsT",))
                        b = begin(("sg", i))
                        for tt in range(TT):
                            o = psum[:, b, P * tt:P * tt + P]
                            pe.matmul(o, svt[:, i % 2, P * tt:P * tt + P], wsT[:, i, :], start=True, stop=False)
                            ins = pe.matmul(o, cst[0:1, CST["ones"]:CST["ones"] + P], bsr[0:1, P * i:P * i + P],
                                            start=False, stop=True)
                        ins.then_inc(job_done, 1)

            for i in range(6):
                name = EVEN_BESIDE[i // 2]
                features(PL.first[name] + i % 2, parts=lambda k: even_part(8 * i + k))

            def layer_norm(n):
                name = ("eo", "oo")[n]

                def sum_pair(i):
                    wait_step(pe, PL.first[name] + i)
                    for k in (2 * i, 2 * i + 1):
                        ins = pe.matmul(bank(job_banks(("lm", n))[0]), c_("ones"), x[:, k, :], start=k == 0,
                                        stop=k == KT - 1)
                    if i == 3:
                        ins.then_inc(job_done, 1)

                for i in range(4):
                    if i == 2:
                        wait_banks(pe, ("lm", n))
                    if i >= 2:
                        sum_pair(i - 2)
                    features(PL.first[name] + i, XV[("evenmix", "oddmix")[n]] if i == 0 else None)
                sum_pair(2)
                sum_pair(3)
                order[0] += 1
                b = begin(("lv", n))
                for k in range(KT):
                    pe.wait_ge(sq_ready, 8 * (4 + n) + k + 1)
                    pe.matmul(bank(b), c_("ones"), xf[:, k % 2, :], start=k == 0, stop=k == KT - 1
                              ).then_inc(sq_used if k < KT - 1 else job_done, 1)

            layer_norm(0)
            product("oq", XV["odd"])
            product("ok", None)
            product("ov", None, tokens)
            pe.wait_ge(odd_in, 32)

            def odd_part(n):
                for what, i in ODD_AT.get(n, ()):
                    if what == "rt":
                        wait_product(pe, "ok")
                        b = begin(("rt", i))
                        pe.matmul(bank(b), c_("rot2"), oqk[:, i, :], start=True, stop=True).then_inc(job_done, 1)
                    elif what == "ks":
                        pe.wait_ge(rot_done, 4)
                        keys_and_scores("r", i, oqk)
                    elif what == "ru":
                        wait_job(pe, ("rkt", i))
                        state_update(("ru", i), i, slice(0, P), ov)
                    elif what == "ro":
                        wait_job(pe, ("rs", i))
                        pe.wait_ge(r_state, i + 1)
                        outputs(("ro", i), i, slice(0, P), est[i % 2], oqi, ov)
                    elif what == "pool":
                        pe.wait_ge(win_d, i + 1)
                        b = begin(("pool", i))
                        pe.matmul(bank(b), wpl[:, i, :], omix[:, 4 + i, :], start=True, stop=True
                                  ).then_inc(job_done, 1)
                    elif what == "rmean":
                        wait_job(pe, ("ro", TT - 1))
                        b = begin(("rmean", i))
                        pe.matmul(bank(b), c_("allmean"), omix[:, i, :], start=True, stop=True
                                  ).then_inc(job_done, 1)
                    elif what == "sq":
                        if i == 0:
                            wait_banks(pe, ("rvar",))
                        elif i == 3:
                            order[0] += 1
                        pe.wait_ge(hn_a, 32 + i + 1)
                        pe.matmul(psum[0:16, job_banks(("rvar",))[0], :], c_("sel128", 16, 16 * i),
                                  xf[:, i % 2, :], start=i == 0, stop=i == 3
                                  ).then_inc(hn_pe if i < 3 else job_done, 1)
                    elif what == "rrb":
                        pe.wait_ge(kn_l, 8)
                        b = begin(("rrb", i))
                        two(bank(b), heads_r[:, P * i:P * i + P], (on_hi[:, :], on_lo[:, :])).then_inc(job_done, 1)

            for i in range(6):
                name = ODD_BESIDE[i // 2]
                features(PL.first[name] + i % 2, parts=lambda k: odd_part(8 * i + k))
            layer_norm(1)
            for i in range(2):
                for tt in range(TT):
                    if tt == 0:
                        pe.wait_ge(ln_b, 8 + 4 * i + 4)
                    b = begin(("out", tt, i))
                    for j in range(4):
                        ins = pe.transpose(psum[:, b, P * j:P * j + P], x[:, 4 * i + j, P * tt:P * tt + P], c_("ident"))
                    ins.then_inc(job_done, 1)


_INS = ["x", "g_mix", "g_ffn", "rw_mu", "rw_w_r", "rw_w_k",
        "rw_w_v", "rw_w_o", "rw_w0", "rw_w1", "rw_w2", "rw_a0",
        "rw_a1", "rw_a2", "rw_g1", "rw_g2", "rw_k_k", "rw_k_a",
        "rw_r_k", "rw_lnx_w", "rw_lnx_b", "kv_g", "kv_w", "k_norm_g",
        "da_w_q", "da_q_norm_g", "da_lam_q1", "da_lam_k1", "da_lam_q2", "da_lam_k2",
        "da_subln_g", "da_w_o", "ffn_w_gu", "ffn_w_down", "positions_2", "l0_w_in_2",
        "l0_w_a2_2", "l0_b_a_2", "l0_gla_norm_g_2", "l0_sgu_ln_g_2", "l0_sgu_ln_b_2", "l0_w_s_2",
        "l0_b_s_2", "l0_w_out_2", "l0_ln_g_2", "l0_ln_b_2", "l1_w_in_2", "l1_ret_norm_g_2",
        "l1_w_pool_2", "l1_pool_scale_2", "l1_w_out_2", "l1_ln_g_2", "l1_ln_b_2"]


def kernel(**inputs):
    import numpy as _np
    import concourse.bacc as _bacc
    from concourse import mybir as _mybir
    from concourse.bass_utils import run_bass_kernel_spmd as _run

    nc = _bacc.Bacc("TRN2", target_bir_lowering=False, num_devices=1)
    arrays, t = {}, {}
    for name in _INS:
        a = _np.ascontiguousarray(inputs[name])
        arrays[f"in_{name}"] = a
        t[name] = nc.dram_tensor(f"in_{name}", a.shape, _mybir.dt.from_np(a.dtype), kind="ExternalInput").ap()
    for name, a in host_constants().items():
        arrays[name] = a
        t[name] = nc.dram_tensor(name, a.shape, _mybir.dt.from_np(a.dtype), kind="ExternalInput").ap()
    out = nc.dram_tensor("out_x", (1, S, D), _mybir.dt.float32, kind="ExternalOutput").ap()
    build(nc, t, out)
    return _run(nc, [arrays], core_ids=[0]).results[0]["out_x"]
```
